# Optimizing a Trainium2 kernel written in Bass

```python
import math
import jax, jax.numpy as jnp
from jax import lax
import numpy as np
import jax
import jax.numpy as jnp

D_MODEL = 1024
BATCH = 1
SEQ = 256
DEPTH = 1

PLE_DIM = 256
HEAD_DIM = 64
A_Q_HEADS = 8
A_KV_HEADS = 2
A_GROUP = A_Q_HEADS // A_KV_HEADS
A_WINDOW = 128
B_HEADS = 8
B_PATTERNS = ((128, 1), (512, 4), (2048, 16))
N_HEADS_TOTAL = A_Q_HEADS + B_HEADS
A_Q = A_Q_HEADS * HEAD_DIM
A_KV = A_KV_HEADS * HEAD_DIM
B_W = B_HEADS * HEAD_DIM
D_IN = A_Q + 2 * A_KV + 3 * B_W
D_MIX = A_Q + B_W
D_FF = 2816
NUM_BUCKETS = 32
MAX_DISTANCE = 2048
BLOCK = 128
EPS = 1e-6
NEG_INF = -1e30


def rms_norm(x, g):
    xf = x.astype(jnp.float32)
    y = xf * lax.rsqrt(jnp.mean(xf * xf, axis=-1, keepdims=True) + EPS)
    return (y * g.astype(jnp.float32)).astype(x.dtype)

def swiglu(x, w_gu, w_down):
    g, u = jnp.split(x @ w_gu, 2, axis=-1)
    return (jax.nn.silu(g) * u) @ w_down

def t5_bucket(dist):
    max_exact = NUM_BUCKETS // 2
    n = jnp.maximum(dist, 0)
    nf = jnp.maximum(n, 1).astype(jnp.float32)
    large = max_exact + (jnp.log(nf / max_exact) / math.log(MAX_DISTANCE / max_exact)
                         * (NUM_BUCKETS - max_exact)).astype(jnp.int32)
    large = jnp.minimum(large, NUM_BUCKETS - 1)
    return jnp.where(n < max_exact, n, large)

def banded_attention(q, k, v, rel_bias, max_dist, stride):
    n, L, hkv, grp, dh = q.shape
    bq = math.gcd(L, BLOCK)
    nb = L // bq
    nk = bq + max_dist
    pad = ((0, 0), (max_dist, 0), (0, 0), (0, 0))
    k_pad = jnp.pad(k, pad)
    v_pad = jnp.pad(v, pad)
    key_idx = jnp.arange(nb)[:, None] * bq + jnp.arange(nk)[None, :]
    kb = k_pad[:, key_idx]
    vb = v_pad[:, key_idx]
    qb = q.reshape(n, nb, bq, hkv, grp, dh)
    logits = jnp.einsum('nbqhgd,nbkhd->nbhgqk', qb, kb,
                        preferred_element_type=jnp.float32) * (dh ** -0.5)
    rel = jnp.arange(bq)[:, None] + max_dist - jnp.arange(nk)[None, :]
    bias = rel_bias[t5_bucket(rel * stride)].astype(jnp.float32)
    bias = bias.reshape(bq, nk, hkv, grp).transpose(2, 3, 0, 1)
    in_band = (rel >= 0) & (rel <= max_dist)
    key_pos = key_idx - max_dist
    valid = in_band[None] & (key_pos >= 0)[:, None, :]
    logits = jnp.where(valid[None, :, None, None], logits + bias, NEG_INF)
    m = jnp.max(logits, axis=-1)
    pr = jnp.exp(logits - m[..., None])
    s = jnp.sum(pr, axis=-1)
    o = jnp.einsum('nbhgqk,nbkhd->nbqhgd', pr, vb.astype(jnp.float32))
    o = o.reshape(n, L, hkv, grp, dh)
    m = m.transpose(0, 1, 4, 2, 3).reshape(n, L, hkv, grp)
    s = s.transpose(0, 1, 4, 2, 3).reshape(n, L, hkv, grp)
    return o, m, s

def to_classes(t, r):
    b, s = t.shape[:2]
    rest = t.shape[2:]
    t = jnp.moveaxis(t.reshape((b, s // r, r) + rest), 2, 1)
    return t.reshape((b * r, s // r) + rest)

def from_classes(t, b, r):
    n, L = t.shape[:2]
    rest = t.shape[2:]
    t = jnp.moveaxis(t.reshape((b, r, L) + rest), 1, 2)
    return t.reshape((b, L * r) + rest)

def sink_swa_gqa(q_a, k_a, v_a, sinks, rel_bias_a):
    b, s, _ = q_a.shape
    q = q_a.reshape(b, s, A_KV_HEADS, A_GROUP, HEAD_DIM)
    k = k_a.reshape(b, s, A_KV_HEADS, HEAD_DIM)
    v = v_a.reshape(b, s, A_KV_HEADS, HEAD_DIM)
    o, m, den = banded_attention(q, k, v, rel_bias_a, A_WINDOW - 1, 1)
    sink = sinks.reshape(A_KV_HEADS, A_GROUP).astype(jnp.float32)
    m_all = jnp.maximum(m, sink)
    scale = jnp.exp(m - m_all)
    total = den * scale + jnp.exp(sink - m_all)
    o = o * (scale / total)[..., None]
    return o.reshape(b, s, A_Q)

def dilated_mixture(q_b, k_b, v_b, rel_bias_b):
    b, s, _ = q_b.shape
    q = q_b.reshape(b, s, B_HEADS, 1, HEAD_DIM)
    k = k_b.reshape(b, s, B_HEADS, HEAD_DIM)
    v = v_b.reshape(b, s, B_HEADS, HEAD_DIM)
    outs, maxes, dens = [], [], []
    for window, dil in B_PATTERNS:
        o, m, den = banded_attention(to_classes(q, dil), to_classes(k, dil), to_classes(v, dil),
                                     rel_bias_b, window // dil, dil)
        outs.append(from_classes(o, b, dil))
        maxes.append(from_classes(m, b, dil))
        dens.append(from_classes(den, b, dil))
    m_stack = jnp.stack(maxes)
    m_all = jnp.max(m_stack, axis=0)
    w = jnp.exp(m_stack - m_all)
    num = jnp.sum(w[..., None] * jnp.stack(outs), axis=0)
    den_all = jnp.sum(w * jnp.stack(dens), axis=0)
    return (num / den_all[..., None]).reshape(b, s, B_W)

def first_inputs(seed: int = 0) -> dict:
    key = jax.random.key(seed)
    ks = jax.random.split(key, 24)
    f32 = jnp.float32

    def w(k, shape, fan_in):
        return jax.random.normal(k, shape, f32) * (fan_in ** -0.5)

    def gain(k, shape):
        return 1.0 + 0.05 * jax.random.normal(k, shape, f32)

    def small(k, shape, scale=0.02):
        return scale * jax.random.normal(k, shape, f32)

    D = D_MODEL
    return {
        "x": jax.random.normal(ks[0], (BATCH, SEQ, D), f32),
        "p": jax.random.normal(ks[1], (DEPTH, BATCH, SEQ, PLE_DIM), f32),
        "rel_bias": small(ks[2], (NUM_BUCKETS, N_HEADS_TOTAL), 0.5),
        "ffn1_pre_g": gain(ks[3], (DEPTH, D)),
        "ffn1_w_gu": w(ks[4], (DEPTH, D, 2 * D_FF), D),
        "ffn1_w_down": w(ks[5], (DEPTH, D_FF, D), D_FF),
        "ffn1_post_g": gain(ks[6], (DEPTH, D)),
        "attn_pre_g": gain(ks[7], (DEPTH, D)),
        "w_in": w(ks[8], (DEPTH, D, D_IN), D),
        "b_in": small(ks[9], (DEPTH, D_IN)),
        "sinks": small(ks[10], (DEPTH, A_Q_HEADS), 0.5),
        "w_out": w(ks[11], (DEPTH, D_MIX, D), D_MIX),
        "b_out": small(ks[12], (DEPTH, D)),
        "attn_post_g": gain(ks[13], (DEPTH, D)),
        "ffn2_pre_g": gain(ks[14], (DEPTH, D)),
        "ffn2_w_gu": w(ks[15], (DEPTH, D, 2 * D_FF), D),
        "ffn2_w_down": w(ks[16], (DEPTH, D_FF, D), D_FF),
        "ffn2_post_g": gain(ks[17], (DEPTH, D)),
        "ple_pre_g": gain(ks[18], (DEPTH, D)),
        "w_ple_gate": w(ks[19], (DEPTH, D, D), D),
        "w_ple_proj": w(ks[20], (DEPTH, PLE_DIM, D), PLE_DIM),
        "ple_post_g": gain(ks[21], (DEPTH, D)),
    }

def first_block(x, p, rel_bias, ffn1_pre_g, ffn1_w_gu, ffn1_w_down, ffn1_post_g,
              attn_pre_g, w_in, b_in, sinks, w_out, b_out, attn_post_g,
              ffn2_pre_g, ffn2_w_gu, ffn2_w_down, ffn2_post_g,
              ple_pre_g, w_ple_gate, w_ple_proj, ple_post_g):
    h = x
    splits = [A_Q, A_Q + A_KV, A_Q + 2 * A_KV, A_Q + 2 * A_KV + B_W, A_Q + 2 * A_KV + 2 * B_W]
    for i in range(DEPTH):
        f = swiglu(rms_norm(h, ffn1_pre_g[i]), ffn1_w_gu[i], ffn1_w_down[i])
        h = h + 0.5 * rms_norm(f, ffn1_post_g[i])

        z = rms_norm(h, attn_pre_g[i]) @ w_in[i] + b_in[i]
        q_a, k_a, v_a, q_b, k_b, v_b = jnp.split(z, splits, axis=-1)
        out_a = sink_swa_gqa(q_a, k_a, v_a, sinks[i], rel_bias[:, :A_Q_HEADS])
        out_b = dilated_mixture(q_b, k_b, v_b, rel_bias[:, A_Q_HEADS:])
        mix = jnp.concatenate([out_a, out_b], axis=-1).astype(x.dtype)
        att = mix @ w_out[i] + b_out[i]
        h = h + rms_norm(att, attn_post_g[i])

        f = swiglu(rms_norm(h, ffn2_pre_g[i]), ffn2_w_gu[i], ffn2_w_down[i])
        h = h + 0.5 * rms_norm(f, ffn2_post_g[i])

        gate = jax.nn.sigmoid(rms_norm(h, ple_pre_g[i]) @ w_ple_gate[i])
        e = p[i] @ w_ple_proj[i]
        h = h + rms_norm(gate * e, ple_post_g[i])
    return h


DEPTH_2 = 2

CTX_LEN = 256
GRID_W = 64
N_HEADS = 8
N_KV_HEADS = 2
KV_GROUP = N_HEADS // N_KV_HEADS
HEAD_DIM_2 = 128
ATTN_WIDTH = N_HEADS * HEAD_DIM_2
KV_WIDTH = N_KV_HEADS * HEAD_DIM_2
ROPE_AXIS_DIM = HEAD_DIM_2 // 2
ROPE_THETA = 10000.0
Q_BLOCK = 128
HYENA_WIDTH = D_MODEL // 2
HYENA_PROJ = 3 * HYENA_WIDTH
SHORT_CONV = 3
FILTER_EMB = 33
FILTER_BANDS = (FILTER_EMB - 1) // 2
FILTER_HIDDEN = 64
FILTER_OUT_GAIN = 0.05
DECAY_TARGET = 1e-2
FAST_DECAY_PCT = 0.3
SLOW_DECAY_PCT = 1.5
N_BRANCHES = 2
GATE_WIDTH = N_BRANCHES * D_MODEL
PROJ_WIDTH = ATTN_WIDTH + 2 * KV_WIDTH + HYENA_PROJ + GATE_WIDTH
PROJ_SPLITS = (ATTN_WIDTH, ATTN_WIDTH + KV_WIDTH, ATTN_WIDTH + 2 * KV_WIDTH,
               ATTN_WIDTH + 2 * KV_WIDTH + HYENA_PROJ)
D_FF_2 = (8 * D_MODEL + 3 * 256 - 1) // (3 * 256) * 256
N_MOD = 6


def rms_norm_2(x, gain):
    xf = x.astype(jnp.float32)
    y = xf * lax.rsqrt(jnp.mean(xf * xf, axis=-1, keepdims=True) + EPS)
    return (y * gain.astype(jnp.float32)).astype(x.dtype)

def modulate(h, shift, scale):
    return h * (1 + scale) + shift

def split_heads_norm(t, gain, n_heads):
    t = t.reshape(t.shape[0], t.shape[1], n_heads, HEAD_DIM_2)
    return rms_norm_2(t, gain)

def axial_rope_tables(rows):
    row = jnp.repeat(jnp.arange(rows, dtype=jnp.float32), GRID_W)
    col = jnp.tile(jnp.arange(GRID_W, dtype=jnp.float32), rows)
    inv_freq = ROPE_THETA ** (-jnp.arange(0, ROPE_AXIS_DIM, 2, dtype=jnp.float32) / ROPE_AXIS_DIM)
    ang = jnp.concatenate([row[:, None] * inv_freq, col[:, None] * inv_freq], axis=-1)
    return jnp.cos(ang), jnp.sin(ang)

def apply_rope(t, cos, sin):
    tf = t.astype(jnp.float32).reshape(*t.shape[:-1], HEAD_DIM_2 // 2, 2)
    c = cos[None, :, None, :]
    s = sin[None, :, None, :]
    t0, t1 = tf[..., 0], tf[..., 1]
    out = jnp.stack([t0 * c - t1 * s, t0 * s + t1 * c], axis=-1)
    return out.reshape(t.shape).astype(t.dtype)

def latent_attention(q, k, v, k_ctx, v_ctx):
    b, length = q.shape[0], q.shape[1]
    n_blocks = length // Q_BLOCK
    keys = jnp.concatenate([k_ctx, k], axis=1)
    vals = jnp.concatenate([v_ctx, v], axis=1)
    qb = q.reshape(b, n_blocks, Q_BLOCK, N_KV_HEADS, KV_GROUP, HEAD_DIM_2)
    qb = jnp.moveaxis(qb, 1, 0)
    scale = HEAD_DIM_2 ** -0.5

    def one_block(q_blk):
        s = jnp.einsum('bqhgd,bkhd->bhgqk', q_blk, keys, preferred_element_type=jnp.float32) * scale
        p = jax.nn.softmax(s, axis=-1).astype(vals.dtype)
        return jnp.einsum('bhgqk,bkhd->bqhgd', p, vals)

    out = lax.map(one_block, qb)
    return jnp.moveaxis(out, 0, 1).reshape(b, length, ATTN_WIDTH)

def context_attention(q, k, v):
    b, length = q.shape[0], q.shape[1]
    qg = q.reshape(b, length, N_KV_HEADS, KV_GROUP, HEAD_DIM_2)
    s = jnp.einsum('bqhgd,bkhd->bhgqk', qg, k, preferred_element_type=jnp.float32) * HEAD_DIM_2 ** -0.5
    p = jax.nn.softmax(s, axis=-1).astype(v.dtype)
    return jnp.einsum('bhgqk,bkhd->bqhgd', p, v).reshape(b, length, ATTN_WIDTH)

def short_conv(u, w, bias):
    up = jnp.pad(u, ((0, 0), (1, 1), (0, 0)))
    return up[:, :-2] * w[0] + up[:, 1:-1] * w[1] + up[:, 2:] * w[2] + bias

def hyena_filter(length, fw1, fb1, fw2, fb2, fw3, fb3, fw4, freq):
    t = jnp.linspace(0.0, 1.0, length, dtype=jnp.float32)[:, None]
    w = (2.0 * math.pi / length) * jnp.arange(length, dtype=jnp.float32)[:, None]
    f = jnp.linspace(1e-4, FILTER_BANDS - 1, FILTER_BANDS, dtype=jnp.float32)[None, :]
    z = jnp.concatenate([t, jnp.cos(f * w), -jnp.sin(f * w)], axis=-1)
    h = jnp.sin(freq[0] * (z @ fw1 + fb1))
    h = jnp.sin(freq[1] * (h @ fw2 + fb2))
    h = jnp.sin(freq[2] * (h @ fw3 + fb3))
    h = (h @ fw4).reshape(length, 2, HYENA_WIDTH)
    max_decay = math.log(DECAY_TARGET) / FAST_DECAY_PCT
    min_decay = math.log(DECAY_TARGET) / SLOW_DECAY_PCT
    deltas = jnp.abs(jnp.linspace(min_decay, max_decay, HYENA_WIDTH, dtype=jnp.float32))
    decay = jnp.exp(-t * deltas)
    h = h * decay[:, None, :]
    return h[:, 0], h[:, 1]

def bidirectional_long_conv(v, h_fwd, h_bwd):
    length = v.shape[1]
    n_fft = 2 * length
    k = jnp.concatenate([h_fwd, jnp.zeros((1, HYENA_WIDTH), h_fwd.dtype), h_bwd[:0:-1]], axis=0)
    v_f = jnp.fft.rfft(v.astype(jnp.float32), n=n_fft, axis=1)
    k_f = jnp.fft.rfft(k, n=n_fft, axis=0)
    return jnp.fft.irfft(v_f * k_f[None], n=n_fft, axis=1)[:, :length]

def hyena_mix(u, conv_w, conv_b, fw1, fb1, fw2, fb2, fw3, fb3, fw4, freq, bias):
    length = u.shape[1]
    x0, x1, v = jnp.split(short_conv(u, conv_w, conv_b), 3, axis=-1)
    v = v * x1
    h_fwd, h_bwd = hyena_filter(length, fw1, fb1, fw2, fb2, fw3, fb3, fw4, freq)
    y = bidirectional_long_conv(v, h_fwd, h_bwd) + v.astype(jnp.float32) * bias
    return (y * x0).astype(u.dtype)

def merge_branches(attn_out, hyena_out, gate_logits, w_o_attn, w_o_hyena, w_out):
    g_attn, g_hyena = jnp.split(jax.nn.sigmoid(gate_logits), N_BRANCHES, axis=-1)
    merged = g_attn * (attn_out @ w_o_attn) + g_hyena * (hyena_out @ w_o_hyena)
    return merged @ w_out

def swiglu_2(h, w_gate_up, w_down):
    g, u = jnp.split(h @ w_gate_up, 2, axis=-1)
    return (jax.nn.silu(g) * u) @ w_down

def second_inputs(seed: int = 0) -> dict:
    key = jax.random.key(seed)
    ks = jax.random.split(key, 28)
    D = D_MODEL

    def nrm(k, shape, scale=1.0):
        return jax.random.normal(k, shape, jnp.float32) * scale

    return {
        'x': nrm(ks[0], (BATCH, SEQ, D)),
        'c': nrm(ks[1], (BATCH, D)),
        'ctx': nrm(ks[2], (BATCH, CTX_LEN, D)),
        'c_ctx': nrm(ks[3], (D,)),
        'w_mod': nrm(ks[4], (DEPTH_2, D, N_MOD * D), D ** -0.5),
        'b_mod': nrm(ks[5], (DEPTH_2, N_MOD * D), 0.01),
        'norm_mix': 1.0 + nrm(ks[6], (DEPTH_2, D), 0.05),
        'w_in': nrm(ks[7], (DEPTH_2, D, PROJ_WIDTH), D ** -0.5),
        'q_norm': 1.0 + nrm(ks[8], (DEPTH_2, HEAD_DIM_2), 0.05),
        'k_norm': 1.0 + nrm(ks[9], (DEPTH_2, HEAD_DIM_2), 0.05),
        'conv_w': nrm(ks[10], (DEPTH_2, SHORT_CONV, HYENA_PROJ), SHORT_CONV ** -0.5),
        'conv_b': nrm(ks[11], (DEPTH_2, HYENA_PROJ), 0.01),
        'filt_w1': nrm(ks[12], (DEPTH_2, FILTER_EMB, FILTER_HIDDEN), FILTER_EMB ** -0.5),
        'filt_b1': nrm(ks[13], (DEPTH_2, FILTER_HIDDEN), 0.1),
        'filt_w2': nrm(ks[14], (DEPTH_2, FILTER_HIDDEN, FILTER_HIDDEN), FILTER_HIDDEN ** -0.5),
        'filt_b2': nrm(ks[15], (DEPTH_2, FILTER_HIDDEN), 0.1),
        'filt_w3': nrm(ks[16], (DEPTH_2, FILTER_HIDDEN, FILTER_HIDDEN), FILTER_HIDDEN ** -0.5),
        'filt_b3': nrm(ks[17], (DEPTH_2, FILTER_HIDDEN), 0.1),
        'filt_w4': nrm(ks[18], (DEPTH_2, FILTER_HIDDEN, 2 * HYENA_WIDTH), FILTER_HIDDEN ** -0.5 * FILTER_OUT_GAIN),
        'filt_freq': 1.0 + nrm(ks[19], (DEPTH_2, 3, FILTER_HIDDEN), 0.1),
        'hyena_bias': nrm(ks[20], (DEPTH_2, HYENA_WIDTH), 0.5),
        'w_o_attn': nrm(ks[21], (DEPTH_2, ATTN_WIDTH, D), ATTN_WIDTH ** -0.5),
        'w_o_hyena': nrm(ks[22], (DEPTH_2, HYENA_WIDTH, D), HYENA_WIDTH ** -0.5),
        'w_out': nrm(ks[23], (DEPTH_2, D, D), D ** -0.5),
        'norm_ffn': 1.0 + nrm(ks[24], (DEPTH_2, D), 0.05),
        'w_gate_up': nrm(ks[25], (DEPTH_2, D, 2 * D_FF_2), D ** -0.5),
        'w_down': nrm(ks[26], (DEPTH_2, D_FF_2, D), D_FF_2 ** -0.5),
        'norm_final': 1.0 + nrm(ks[27], (D,), 0.05),
    }

def second_block(x, c, ctx, c_ctx, w_mod, b_mod, norm_mix, w_in, q_norm, k_norm, conv_w, conv_b,
              filt_w1, filt_b1, filt_w2, filt_b2, filt_w3, filt_b3, filt_w4, filt_freq, hyena_bias,
              w_o_attn, w_o_hyena, w_out, norm_ffn, w_gate_up, w_down, norm_final):
    b, length = x.shape[0], x.shape[1]
    rows = length // GRID_W
    cos, sin = axial_rope_tables(rows)
    silu_c = jax.nn.silu(c)
    silu_cc = jax.nn.silu(c_ctx)
    for layer in range(DEPTH_2):
        last = layer == DEPTH_2 - 1
        mod = (silu_c @ w_mod[layer] + b_mod[layer])[:, None, :]
        mod_c = silu_cc @ w_mod[layer] + b_mod[layer]
        shift1, scale1, gate1, shift2, scale2, gate2 = jnp.split(mod, N_MOD, axis=-1)
        c_shift1, c_scale1, c_gate1, c_shift2, c_scale2, c_gate2 = jnp.split(mod_c, N_MOD, axis=-1)
        filt = (filt_w1[layer], filt_b1[layer], filt_w2[layer], filt_b2[layer],
                filt_w3[layer], filt_b3[layer], filt_w4[layer], filt_freq[layer])

        h_ctx = modulate(rms_norm_2(ctx, norm_mix[layer]), c_shift1, c_scale1)
        if last:
            kc, vc = jnp.split(h_ctx @ w_in[layer][:, ATTN_WIDTH:ATTN_WIDTH + 2 * KV_WIDTH], 2, axis=-1)
        else:
            qc, kc, vc, hyc, gc = jnp.split(h_ctx @ w_in[layer], PROJ_SPLITS, axis=-1)
        kc = split_heads_norm(kc, k_norm[layer], N_KV_HEADS)
        vc = vc.reshape(b, vc.shape[1], N_KV_HEADS, HEAD_DIM_2)

        h = modulate(rms_norm_2(x, norm_mix[layer]), shift1, scale1)
        q, k, v, hy, g = jnp.split(h @ w_in[layer], PROJ_SPLITS, axis=-1)
        q = apply_rope(split_heads_norm(q, q_norm[layer], N_HEADS), cos, sin)
        k = apply_rope(split_heads_norm(k, k_norm[layer], N_KV_HEADS), cos, sin)
        v = v.reshape(b, length, N_KV_HEADS, HEAD_DIM_2)
        attn = latent_attention(q, k, v, kc, vc)
        hyo = hyena_mix(hy, conv_w[layer], conv_b[layer], *filt, hyena_bias[layer])
        x_mix = merge_branches(attn, hyo, g, w_o_attn[layer], w_o_hyena[layer], w_out[layer])

        if not last:
            attn_c = context_attention(split_heads_norm(qc, q_norm[layer], N_HEADS), kc, vc)
            hyo_c = hyena_mix(hyc, conv_w[layer], conv_b[layer], *filt, hyena_bias[layer])
            ctx_mix = merge_branches(attn_c, hyo_c, gc, w_o_attn[layer], w_o_hyena[layer], w_out[layer])
            ctx = ctx + c_gate1 * ctx_mix
            ctx = ctx + c_gate2 * swiglu_2(modulate(rms_norm_2(ctx, norm_ffn[layer]), c_shift2, c_scale2),
                                         w_gate_up[layer], w_down[layer])

        x = x + gate1 * x_mix
        x = x + gate2 * swiglu_2(modulate(rms_norm_2(x, norm_ffn[layer]), shift2, scale2),
                               w_gate_up[layer], w_down[layer])
    return rms_norm_2(x, norm_final)


def setup_inputs(seed=0):
    out = dict(first_inputs(seed))
    for name, value in second_inputs(seed + 1).items():
        if name != "x":
            out[name + "_2"] = value
    return out


def reference(
    x, p, rel_bias, ffn1_pre_g, ffn1_w_gu, ffn1_w_down, ffn1_post_g, attn_pre_g, w_in, b_in,
    sinks, w_out, b_out, attn_post_g, ffn2_pre_g, ffn2_w_gu, ffn2_w_down, ffn2_post_g,
    ple_pre_g, w_ple_gate, w_ple_proj, ple_post_g, c_2, ctx_2, c_ctx_2, w_mod_2, b_mod_2,
    norm_mix_2, w_in_2, q_norm_2, k_norm_2, conv_w_2, conv_b_2, filt_w1_2, filt_b1_2, filt_w2_2,
    filt_b2_2, filt_w3_2, filt_b3_2, filt_w4_2, filt_freq_2, hyena_bias_2, w_o_attn_2,
    w_o_hyena_2, w_out_2, norm_ffn_2, w_gate_up_2, w_down_2, norm_final_2,
):
    x = first_block(
        x, p, rel_bias, ffn1_pre_g, ffn1_w_gu, ffn1_w_down, ffn1_post_g, attn_pre_g, w_in, b_in,
        sinks, w_out, b_out, attn_post_g, ffn2_pre_g, ffn2_w_gu, ffn2_w_down, ffn2_post_g,
        ple_pre_g, w_ple_gate, w_ple_proj, ple_post_g,
    )
    return second_block(
        x, c_2, ctx_2, c_ctx_2, w_mod_2, b_mod_2, norm_mix_2, w_in_2, q_norm_2, k_norm_2,
        conv_w_2, conv_b_2, filt_w1_2, filt_b1_2, filt_w2_2, filt_b2_2, filt_w3_2, filt_b3_2,
        filt_w4_2, filt_freq_2, hyena_bias_2, w_o_attn_2, w_o_hyena_2, w_out_2, norm_ffn_2,
        w_gate_up_2, w_down_2, norm_final_2,
    )


_drawn_inputs = setup_inputs


def setup_inputs(seed=0):
    import zlib

    import numpy as np

    out = dict(_drawn_inputs(seed))
    spreads = {}
    factors = {'sinks': 8.0,
     'ffn2_post_g': 3.675,
     'ple_pre_g': 4.846,
     'ctx_2': 3.844,
     'b_mod_2': 4.042,
     'q_norm_2': 8.0,
     'k_norm_2': 8.0,
     'conv_b_2': 8.0,
     'filt_freq_2': 3.848}
    for name, (base, spread) in spreads.items():
        noise = np.random.default_rng([zlib.crc32(name.encode()), seed]).standard_normal(out[name].shape)
        drawn = base * np.exp(spread * noise) if base else spread * noise
        out[name] = jnp.asarray(drawn.astype(out[name].dtype))
    for name, factor in factors.items():
        out[name] = (out[name] * factor).astype(out[name].dtype)
    return out
```

```python
from contextlib import ExitStack

import numpy as np

import concourse.bass as bass
from concourse import mybir

F32 = mybir.dt.float32
F32R = mybir.dt.float32r
ALU = mybir.AluOpType
ACT = mybir.ActivationFunctionType
AX = mybir.AxisListType

P = 128
D = 1024
KT = D // P
TX = 256
TB = 2 * TX
DFF = 2816
FT = DFF // P
EPS = 1e-6
CH = 2048
RING = 3
AHEAD = 2
DH1 = 64
NBKT = 32
DH2 = 128
NH2 = 8
HW = 512
HT = HW // P
FH = 64
FE = 33
CTILES = TB // P
MAGIC = 12582912.0
TWO_PI_HI = 6.28125
TWO_PI_LO = 2.0 * np.pi - 6.28125
PI_IN = 3.1415925



def t5_buckets(n):
    d = np.arange(n)
    nf = np.maximum(d, 1).astype(np.float32)
    exact = NBKT // 2
    large = exact + (np.log(nf / np.float32(exact)) / np.float32(np.log(2048 / exact)) * np.float32(NBKT - exact)).astype(np.int32)
    return np.where(d < exact, d, np.minimum(large, NBKT - 1))


def shape_tables():
    t = {}
    t["ident"] = np.eye(P, dtype=np.float32)
    dist = np.arange(384) - 127
    bucket = t5_buckets(TX)
    onehot = np.zeros((NBKT, 384), np.float32)
    mask = np.full((16, 384), -1e30, np.float32)
    for i, d in enumerate(dist):
        if d < 0 or d >= TX:
            continue
        onehot[bucket[d], i] = 1.0
        if d <= 127:
            mask[:8, i] = 0.0
        count = int(d <= 128) + int(d % 4 == 0) + int(d % 16 == 0)
        if count:
            mask[8:, i] = np.log(count)
    t["onehot"], t["mask"] = onehot, mask
    row = np.repeat(np.arange(TX // 64, dtype=np.float32), 64)
    col = np.tile(np.arange(64, dtype=np.float32), TX // 64)
    inv = (np.float32(10000.0) ** (-np.arange(0, 64, 2, dtype=np.float32) / np.float32(64))).astype(np.float32)
    ang = np.concatenate([row[:, None] * inv, col[:, None] * inv], axis=-1)
    cs = np.stack([np.repeat(np.cos(ang), 2, axis=1).T, np.repeat(np.sin(ang), 2, axis=1).T], axis=1)
    t["rope"] = np.ascontiguousarray(cs.astype(np.float32))
    rot = np.zeros((P, P), np.float32)
    for i in range(0, P, 2):
        rot[i + 1, i] = -1.0
        rot[i, i + 1] = 1.0
    t["rot"] = rot
    lin = np.linspace(0.0, 1.0, TX, dtype=np.float32)[:, None]
    w = np.float32(2.0 * np.pi / TX) * np.arange(TX, dtype=np.float32)[:, None]
    f = np.linspace(1e-4, 15, 16, dtype=np.float32)[None, :]
    t["zfeat"] = np.ascontiguousarray(np.concatenate([lin, np.cos(f * w), -np.sin(f * w)], axis=-1).T.astype(np.float32))
    lo_, hi_ = np.log(1e-2) / 1.5, np.log(1e-2) / 0.3
    deltas = np.abs(np.linspace(lo_, hi_, HW, dtype=np.float32))
    t["decay"] = np.exp(-lin * deltas).astype(np.float32)
    n, k = np.arange(TX)[:, None].astype(np.float64), np.arange(TX)[None, :].astype(np.float64)
    ph = 2 * np.pi * n * k / TB
    alt = (-1.0) ** n
    fwd = np.concatenate([np.cos(ph), alt, -np.sin(ph)[:, 1:]], axis=1)
    bwd = np.concatenate([np.cos(ph), alt, np.sin(ph)[:, 1:]], axis=1)
    bwd[0] = 0.0
    scale = np.full((TX, 1), 2.0 / TB)
    scale[0] = 1.0 / TB
    im = -np.sin(ph).T * (2.0 / TB)
    im[0] = alt[:, 0] / TB
    t["dft"] = np.stack([fwd, bwd]).astype(np.float32)
    t["idft"] = np.concatenate([np.cos(ph).T * scale, im], axis=0).astype(np.float32)
    return t



def param_rows():
    tiles = [
        [("ffn1_pre_g", 8), ("ffn1_post_g", 8), ("attn_pre_g", 8), ("attn_post_g", 8), ("ffn2_pre_g", 8),
         ("ffn2_post_g", 8), ("ple_pre_g", 8), ("ple_post_g", 8), ("b_out", 8), ("b_in", 18),
         ("norm_mix_2", 16), ("norm_final_2", 8), ("q_norm_2", 2), ("k_norm_2", 2)],
        [("b_mod_2", 96), ("norm_ffn_2", 16), ("hyena_bias_2", 8)],
        [("conv_w_2", 72), ("conv_b_2", 24), ("c_2", 8), ("c_ctx_2", 8)],
        [("filt_b1_2", 2), ("filt_b2_2", 2), ("filt_b3_2", 2), ("filt_freq_2", 6)],
    ]
    at, used = {}, []
    for g, names in enumerate(tiles):
        row = 0
        for name, rows in names:
            at[name] = (g, row, rows)
            row += rows
        used.append(row)
    return at, used


PAR_AT, PAR_USED = param_rows()


STAGES = [("ffn1_gu", FT), ("ffn1_dn", FT // 2), ("b1_in", 9), ("b1_out", 4),
          ("ffn2_gu", FT), ("ffn2_dn", FT // 2), ("ple_gate", 4), ("ple_proj", 1)]
for _l in range(2):
    STAGES += [(f"qkv{_l}", 6), (f"hy{_l}", 6), (f"oh{_l}", 2), (f"mix{_l}", 12), (f"out{_l}", 4),
               (f"gu{_l}", FT), (f"dn{_l}", FT // 2)]
FIRST, TOTAL = {}, 0
for _name, _n in STAGES:
    FIRST[_name] = TOTAL
    TOTAL += _n
CHUNKS = dict(STAGES)
STAT_BANK = [0, 4, 0, 0, 0, 4, 0, 4, 6, 6, 6, 6, 6]
MODC = 24


def lin(i, step, const):
    return const if i is None else i * step + const


def steps(eng, stage, body, tail=0):
    n, c0 = CHUNKS[stage], FIRST[stage]
    head = 3 + (n - 3 - tail) % 3
    turns = (n - head - tail) // 3
    if turns < 2:
        head, turns, tail = n, 0, 0
    for j in range(head):
        body(None, j, c0 + j)
    if turns:
        with eng.Fori(0, turns) as i:
            for u in range(3):
                body(i, head + u, c0 + head + u)
    for j in range(n - tail, n):
        body(None, j, c0 + j)


def two_blocks_kernel(nc, d):
    with ExitStack() as ctx:
        sems = {}

        def S(name):
            if name not in sems:
                sems[name] = ctx.enter_context(nc.semaphore(name))
            return sems[name]

        K = 1024
        slab = 207 * K + 768
        nc.alloc_sbuf_tensor("slab", [P, slab // 4], F32)
        base = nc.sbuf_base - slab

        def at(name, shape, off, dt=F32):
            assert off + 4 * int(np.prod(shape[1:])) <= slab, name
            return nc.alloc_sbuf_tensor_at(name, shape, dt, offset=base + off)

        X = at("X", [P, KT, TB], 0)
        RAW = at("RAW", [P, RING, CH], 16 * K)
        WHI = at("WHI", [P, RING, CH], 40 * K, F32R)
        WLO = at("WLO", [P, RING, CH], 64 * K, F32R)
        AHI1, ALO1 = at("AHI1", [P, KT, TX], 88 * K, F32R), at("ALO1", [P, KT, TX], 104 * K, F32R)
        AHI2, ALO2 = at("AHI2", [P, KT, TB], 88 * K, F32R), at("ALO2", [P, KT, TB], 104 * K, F32R)
        BIAS = [at("BIAS0", [P, 8, TX], 96 * K), at("BIAS1", [P, 8, TX], 112 * K)]
        SHI1, SLO1 = at("SHI1", [P, RING, 2, TX], 120 * K, F32R), at("SLO1", [P, RING, 2, TX], 132 * K, F32R)
        SHI2, SLO2 = at("SHI2", [P, RING, 2, TB], 120 * K, F32R), at("SLO2", [P, RING, 2, TB], 132 * K, F32R)
        REL, ONEHOT = at("REL", [NBKT, 16], 126 * K), at("ONEHOT", [NBKT, 384], 127 * K)
        MASK, EXT = at("MASK", [16, 384], 138 * K), at("EXT", [16, 384], 140 * K)
        PHI, PLO = at("PHI", [P, 2, TX], 130 * K, F32R), at("PLO", [P, 2, TX], 142 * K, F32R)
        DFT = at("DFT", [P, 2, 2, TB], 120 * K)
        IDFT = at("IDFT", [P, CTILES, TX], 128 * K)
        KR = at("KR", [P, 2, HW], 132 * K)
        KIZ = at("KIZ", [P, 2, HW], 136 * K)
        KRX = at("KRX", [P, HW], 140 * K)
        ROT = at("ROT", [P, P], 142 * K)
        HHI, HLO = at("HHI", [P, HT, TB], 120 * K, F32R), at("HLO", [P, HT, TB], 132 * K, F32R)
        A = 144 * K
        XS, CS, PST = at("XS", [P, 2, D], A), at("CS", [P, 2, D], A + 8 * K), at("PST", [P, 2, TX], A + 16 * K)
        GS = at("GS", [P, 4, P], A + 18 * K)
        HB1, HB2 = at("HB1", [P, FT, TX], A), at("HB2", [P, FT, TB], A)
        MRAW = at("MRAW", [P, RING, CH], A + 24 * K)
        SQ1, SQ2 = at("SQ1", [P, KT, TX], A), at("SQ2", [P, KT, TB], A)
        FB, TU = at("FB", [P, KT, TX], A + 8 * K), at("TU", [P, KT, TX], A + 16 * K)
        PG = at("PG", [P, KT, TX], A + 16 * K)
        Z = at("Z", [P, 18, TX], A)
        VT1 = at("VT1", [P, 10, P], A + 18 * K)
        KS = at("KS", [P, TX], A + 23 * K)
        SB1 = [at(f"SB1{i}", [P, 4, TX], A + (24 + 6 * i) * K) for i in range(2)]
        SB0 = [at(f"SB0{i}", [P, 4, P], A + (28 + 6 * i) * K) for i in range(2)]
        PT1 = [at(f"PT1{i}", [P, 4, 3 * P], A + (36 + 6 * i) * K) for i in range(2)]
        QKV = at("QKV", [P, 12, TB], A)
        VT2 = at("VT2", [P, 8, P], A + 24 * K)
        HSQ = at("HSQ", [P, 4, TB], A + 28 * K)
        PB = at("PB", [P, 2, 2, TB], A + 28 * K)
        PT2 = at("PT2", [P, 2, 4, TX], A + 36 * K)
        BR = at("BR", [P, 2, TX], A + 44 * K)
        ROPE = at("ROPE", [P, 2, TX], A + 46 * K)
        FW4, DEC = at("FW4", [FH, 2 * HW], A + 16 * K), at("DEC", [P, 2, HW], A + 20 * K)
        HF = at("HF", [P, 2, 2, HW], A + 24 * K)
        ZF = at("ZF", [FE, TX], A + 32 * K)
        FW = [at(f"FW{i}", [FE if i == 0 else FH, FH], A + 33 * K + 256 * i) for i in range(3)]
        FU = at("FU", [FH, 5, TX], A + 34 * K)
        HA = at("HA", [FH, 3, TX], A + 39 * K)
        HY = at("HY", [P, 12, TB], A + 16 * K)
        YS = at("YS", [P, CTILES, HW], A + 24 * K)
        VTT = at("VTT", [P, 2, HW], A + 40 * K)
        YT2 = at("YT2", [P, 2, HW], A + 44 * K)
        A2HI, A2LO = at("A2HI", [P, KT, TB], A + 16 * K, F32R), at("A2LO", [P, KT, TB], A + 32 * K, F32R)
        MG = at("MG", [P, KT, TB], A)
        YF, OUTS = at("YF", [P, KT, TX], A + 16 * K), at("OUTS", [P, 2, D], A + 24 * K)
        GU = at("GU", [P, RING, 2, TX], 192 * K)
        SIL = at("SIL", [P, RING, TB], 192 * K)
        DG = at("DG", [P, 4, P], 192 * K)
        DGK = at("DGK", [P, 2, 4, P], 192 * K)
        SG = at("SG", [P, 2, 2, TB], 192 * K)
        YT1 = at("YT1", [P, 2, HW], 192 * K)
        P32 = at("P32", [P, 2, TX], 198 * K)
        RT = at("RT", [P, TB], 200 * K)
        PAR = at("PAR", [P, 4, P], 202 * K)
        IDENT, ONES = at("IDENT", [P, P], 204 * K), at("ONES", [P, P], 204 * K + 512)
        small = [205 * K]

        def sm(name, shape):
            t = at(name, shape, small[0])
            small[0] += (4 * int(np.prod(shape[1:])) + 31) // 32 * 32
            return t

        MOD = sm("MOD", [P, 2, 48, 2])
        GM = sm("GM", [P, 2, 2, 8, 2])
        HG = sm("HG", [P, 2, 8])
        SC = sm("SC", [P, 2, 8])
        STD, RC = sm("STD", [P, 40]), sm("RC", [P, 40])
        NM, SMX, RS = sm("NM", [P, 2, 8]), sm("SMX", [P, 2, 8]), sm("RS", [P, 2, 8])
        SINK, SE = sm("SINK", [P, 2, 8]), sm("SE", [P, 2, 8])
        EPSC = sm("EPSC", [P, 2])

        PS = ctx.enter_context(nc.psum_tensor("PS", [P, 8, 512], F32))
        bias_rows = nc.dram_tensor("bias_rows", (16, 384), F32).ap()

        def par(name, first=0, n=1):
            g, row, rows = PAR_AT[name]
            return PAR[:, g, row + first:row + first + n]

        def over_tokens(ap, n):
            return ap.unsqueeze(2).broadcast_to([P, ap.shape[1], n])

        def over_tiles(ap, n):
            return ap.unsqueeze(1).broadcast_to([P, n, ap.shape[1]])

        def ring1(j):
            return PS[:, 4 + j % 3, :].rearrange("p (t n) -> p t n", t=2)

        def ring2(j, n):
            s = 2 * (j % 3)
            return PS[:, s:s + 2, :] if n == TB else PS[:, s, :].rearrange("p (t n) -> p t n", t=2)

        def acc(m, n):
            return PS[:, m, :] if n == TB else PS[:, m // 2, m % 2 * TX:m % 2 * TX + TX]

        def stat_sum(n_norm, t):
            return PS[:, STAT_BANK[n_norm], 0:t]

        def stat_row(n_norm, t):
            return PS[:, STAT_BANK[n_norm] + 1, 0:P * t]

        block = ctx.enter_context(nc.Block())

        @block.sync
        def _(sp):
            def load(i, c, src, dst, half=lambda ap, t: ap[:, t * (ap.shape[1] // 2):(t + 1) * (ap.shape[1] // 2), :]):
                if c >= RING:
                    sp.wait_ge(S("lo_done"), lin(i, 3, c - RING + 1))
                for t in range(2):
                    sp.dma_start(half(dst(RAW[:, c % RING, :]), t), half(src, t)).then_inc(S(f"raw{c % RING}"), 16)

            def cols(w, n_first, k=KT, width=2 * P):
                return w.rearrange("(k p) n -> p k n", p=P)[:, :, bass.ds(n_first, width)]

            def by_k(k):
                return lambda r: r.rearrange("p (k n) -> p k n", k=k)

            def mod_load(layer, i, g):
                t = MODC * layer + g
                if t >= RING:
                    if i is None and layer == 1 and g == 0:
                        sp.wait_ge(S("act_lo"), 3 * KT)
                    sp.wait_ge(S("mod_used"), lin(i, 3, t - RING + 1))
                sp.dma_start(MRAW[:, g % RING, :].rearrange("p (k n) -> p k n", k=KT),
                             cols(d["w_mod_2"][layer], lin(i, 3 * 2 * P, g * 2 * P)))\
                  .then_inc(S(f"mod_raw{g % RING}"), 16)

            def gate_up(stage, w, layer=None):
                view = w.rearrange("(k p) (t n) -> p k t n", p=P, t=2)

                def body(i, j, c):
                    load(i, c, view[:, :, :, bass.ds(lin(i, 3 * P, j * P), P)],
                         lambda r: r.rearrange("p (k t n) -> p k t n", k=KT, t=2), lambda ap, t: ap[:, :, t, :])
                    if layer is not None:
                        mod_load(layer, i, j)
                steps(sp, stage, body)

            def down(stage, w, layer=None):
                view = w.rearrange("(k p) n -> p k n", p=P)

                def body(i, j, c):
                    load(i, c, view[:, bass.ds(lin(i, 6, 2 * j), 2), :], by_k(2))
                    if layer is not None and i is None and j < MODC - FT:
                        mod_load(layer, None, FT + j)
                steps(sp, stage, body, tail=2)

            def plain(stage, w, first=0):
                steps(sp, stage, lambda i, j, c: load(i, c, cols(w, lin(i, 6 * P, first + 2 * P * j)), by_k(KT)))

            sp.dma_start(IDENT[:, :], d["ident"]).then_inc(S("in_ident"), 16)
            sp.dma_start(XS[:, :, :], d["x"][0].rearrange("(t p) n -> p t n", p=P)).then_inc(S("in_x"), 16)
            gate_up("ffn1_gu", d["ffn1_w_gu"][0], 0)
            down("ffn1_dn", d["ffn1_w_down"][0], 0)
            plain("b1_in", d["w_in"][0])
            plain("b1_out", d["w_out"][0])
            gate_up("ffn2_gu", d["ffn2_w_gu"][0], 1)
            down("ffn2_dn", d["ffn2_w_down"][0], 1)
            plain("ple_gate", d["w_ple_gate"][0])
            load(None, FIRST["ple_proj"], d["w_ple_proj"][0].rearrange("(k p) n -> p k n", p=P), by_k(2))
            for layer in range(2):
                win = d["w_in_2"][layer]
                plain(f"qkv{layer}", win)
                plain(f"hy{layer}", win, 12 * P)
                woh = d["w_o_hyena_2"][layer].rearrange("(k p) n -> p k n", p=P)
                for j in range(2):
                    load(None, FIRST[f"oh{layer}"] + j, woh[:, :, 512 * j:512 * j + 512], by_k(HT))

                def mix(i, m):
                    c = FIRST[f"mix{layer}"] + 3 * m
                    n = lin(i, 2 * P, 2 * P * m)
                    load(i, c, cols(win, n + 32 * P), by_k(KT))
                    load(i, c + 1, cols(win, n + 24 * P), by_k(KT))
                    load(i, c + 2, cols(d["w_o_attn_2"][layer], n), by_k(KT))
                mix(None, 0)
                with sp.Fori(0, 3) as i:
                    mix(i, 1)
                plain(f"out{layer}", d["w_out_2"][layer])
                gate_up(f"gu{layer}", d["w_gate_up_2"][layer])
                down(f"dn{layer}", d["w_down_2"][layer])
            for t in range(2):
                sp.wait_ge(S("out_ev0"), t + 1)
                sp.wait_ge(S("out_ev1"), t + 1)
                sp.dma_start(d["out"][0, P * t:P * t + P, :], OUTS[:, t, :]).then_inc(S("out_dma"), 16)
            sp.wait_ge(S("out_dma"), 32)

        @block.gpsimd
        def _(pool):
            pool.wait_ge(S("ext_ev"), 1)
            pool.dma_start(bias_rows, EXT[:, :]).then_inc(S("bias_out"), 16)
            pool.wait_ge(S("bias_out"), 16)
            for b in range(2):
                src = bass.AP(tensor=bias_rows.tensor, offset=8 * b * 384, ap=[[1, P], [384, 8], [1, TX]])
                pool.dma_start(BIAS[b][:, :, :], src).then_inc(S("bias_in"), 16)

            def x_update(u):
                for k in range(KT):
                    pool.wait_ge(S("xt"), KT * u + k + 1)
                    pool.tensor_tensor(X[:, k, 0:TX], X[:, k, 0:TX], TU[:, k, :], ALU.add).then_inc(S("xu"), 1)

            x_update(0)
            pool.wait_ge(S("zt"), 18)
            for h in range(2):
                pool.dma_start(KS[64 - 64 * h:128 - 64 * h, :], Z[64 * h:64 * h + 64, 4, :]).then_inc(S("ks"), 16)
            x_update(1)
            x_update(2)
            x_update(3)
            for layer in range(2):
                if layer == 0:
                    pool.wait_ge(S("xu"), 4 * KT)
                else:
                    pool.wait_ge(S("xd"), 2 * KT)
                pool.wait_ge(S("pe_done"), FIRST[f"qkv{layer}"])
                loads = [(FW[0][:, :], d["filt_w1_2"][layer]), (ZF[:, :], d["zfeat"]),
                         (FW[1][:, :], d["filt_w2_2"][layer]), (FW[2][:, :], d["filt_w3_2"][layer]),
                         (FW4[:, :], d["filt_w4_2"][layer]), (DEC[:, :, :], d["decay"].rearrange("(t p) n -> p t n", p=P)),
                         (DFT[:, :, :, :], d["dft"].rearrange("r (t p) n -> p r t n", p=P)),
                         (IDFT[:, :, :], d["idft"].rearrange("(t p) n -> p t n", p=P)),
                         (ROPE[:, :, :], d["rope"]), (ROT[:, :], d["rot"])]
                for dst, src in loads:
                    pool.dma_start(dst, src).then_inc(S(f"tables{layer}"), 16)
                pool.wait_ge(S(f"tables{layer}"), 160)
                for j in range(10):
                    pool.wait_ge(S("h_rot"), 10 * layer + j + 1)
                    pool.tensor_tensor(QKV[:, j, 0:TX], QKV[:, j, 0:TX], ROPE[:, 0, :], ALU.mult).then_inc(S("h_cos"), 1)
                n = TB if layer == 0 else TX
                for m in range(HT):
                    pool.wait_ge(S("hy_taps"), 24 * layer + 16 + 2 * m + 2)
                    pool.tensor_tensor(HY[:, 8 + m, 0:n], HY[:, 8 + m, 0:n], HY[:, 4 + m, 0:n], ALU.mult).then_inc(S("hy_v"), 1)

        @block.scalar
        def _(act):
            def split_w(i, c):
                if c >= TOTAL:
                    return
                act.wait_ge(S(f"raw{c % RING}"), lin(i, 32, 32 * (c // RING + 1)))
                if c >= RING:
                    act.wait_ge(S("pe_done"), lin(i, 3, c - RING + 1))
                act.activation(WHI[:, c % RING, :], RAW[:, c % RING, :], ACT.Copy).then_inc(S("hi_done"), 1)

            def split_h(i, inst, stage, j, hb, shi, n):
                act.wait_ge(S("h"), lin(i, 6, FT * inst + 2 * j + 2))
                if j >= RING:
                    act.wait_ge(S("pe_done"), lin(i, 3, FIRST[stage] + j - RING + 1))
                act.activation(shi[:, j % RING, :, 0:n], hb[:, bass.ds(lin(i, 6, 2 * j), 2), 0:n], ACT.Copy)\
                   .then_inc(S("hs_hi"), 1)

            def down(stage, inst, hb, shi, n):
                split_h(None, inst, stage, 0, hb, shi, n)
                split_h(None, inst, stage, 1, hb, shi, n)

                def body(i, j, c):
                    split_w(i, c + AHEAD)
                    if i is not None or j + AHEAD < FT // 2:
                        split_h(i, inst, stage, j + AHEAD, hb, shi, n)
                steps(act, stage, body, tail=2)

            def norm_std(n_norm, t):
                act.wait_ge(S("n_ss"), n_norm + 1)
                act.activation(STD[:, 0:t], stat_sum(n_norm, t), ACT.Sqrt, scale=1.0 / D, bias=EPSC[:, 0:1])\
                   .then_inc(S("n_std"), 1)

            def squares(src, dst, n_before, ready):
                for k in range(KT):
                    ready(k)
                    act.activation(dst(k), src(k), ACT.Square).then_inc(S("n_sq"), 1)

            def gained(name, ready):
                for k in range(KT):
                    ready(k)
                    act.activation(AHI1[:, k, :], X[:, k, 0:TX], ACT.Identity, scale=par(name, k)).then_inc(S("act_hi"), 1)
                    act.activation(SQ1[:, k, :], X[:, k, 0:TX], ACT.Square).then_inc(S("n_sq"), 1)

            def silus1(stage, inst):
                def body(i, j, c):
                    split_w(i, c + AHEAD)
                    act.wait_ge(S("gu"), lin(i, 3, FT * inst + j + 1))
                    act.activation(GU[:, j % RING, 0, :], GU[:, j % RING, 0, :], ACT.Silu).then_inc(S("sil"), 1)
                steps(act, stage, body)

            for g, names in enumerate([[n for n in PAR_AT if PAR_AT[n][0] == g] for g in range(4)]):
                for name in names:
                    _, row, rows = PAR_AT[name]
                    width = FH if g == 3 else P
                    src = d[name]
                    dims = " ".join("abc"[:len(src.shape)])
                    flat = src.rearrange(f"{dims} -> ({dims})") if len(src.shape) > 1 else src
                    if g == 3:
                        act.wait_ge(S("gs_clear"), 1)
                    act.dma_start(GS[row:row + rows, g, 0:width], flat.rearrange("(r n) -> r n", n=width))\
                       .then_inc(S("in_par"), 16)
            act.dma_start(PST[:, :, :], d["p"][0, 0].rearrange("(t p) n -> p t n", p=P)).then_inc(S("in_p"), 16)
            for dst, src in ((REL[:, :], d["rel_bias"]), (ONEHOT[:, :], d["onehot"]), (MASK[:, :], d["mask"])):
                act.dma_start(dst, src).then_inc(S("in_bias"), 16)
            act.dma_start(SINK[:, 0, :], d["sinks"].broadcast_to([P, 8])).then_inc(S("in_sink"), 16)
            act.dma_start(CS[:, :, :], d["ctx_2"][0].rearrange("(t p) n -> p t n", p=P)).then_inc(S("in_ctx"), 16)

            for b in range(4):
                act.wait_ge(S("tr_x"), b + 1)
                act.activation(X[:, 2 * b:2 * b + 2, 0:TX], PS[:, b, :].rearrange("p (t n) -> p t n", t=2), ACT.Copy)\
                   .then_inc(S("x_ev"), 1)
            split_w(None, 0)
            act.wait_ge(S("par_ev"), 4)
            gained("ffn1_pre_g", lambda k: act.wait_ge(S("x_ev"), k // 2 + 1))
            for v, name in enumerate(("c_2", "c_ctx_2")):
                act.activation(SC[:, v, :], par(name, 0, 8), ACT.Silu).then_inc(S("sc"), 1)
            split_w(None, 1)
            act.wait_ge(S("p_ev"), 1)
            act.activation(PHI[:, :, :], P32[:, :, :], ACT.Copy).then_inc(S("p_hi"), 1)

            for inst, (pre, post) in enumerate(((0, 1), (4, 5))):
                f = f"ffn{inst + 1}"
                norm_std(pre, 2)
                silus1(f + "_gu", inst)
                down(f + "_dn", inst, HB1, SHI1, TX)
                act.wait_ge(S("pe_done"), FIRST[f + "_dn"] + FT // 2)
                squares(lambda k: acc(k, TX), lambda k: SQ1[:, k, :], 0, lambda k: None)
                norm_std(post, 2)
                if inst == 1:
                    break
                gained("attn_pre_g", lambda k: act.wait_ge(S("xu"), k + 1))
                norm_std(2, 2)
                steps(act, "b1_in", lambda i, j, c: split_w(i, c + AHEAD))

                def keys_out(g):
                    act.wait_ge(S("a_tr"), g + 1)
                    act.activation(PT1[g % 2][:, :, :], PS[:, 3:7, 0:3 * P], ACT.Copy).then_inc(S("a_pt"), 1)

                def mixed_hi(g):
                    act.wait_ge(S("a_pv"), g + 1)
                    act.activation(AHI1[:, 2 * g:2 * g + 2, :], PS[:, 7, :].rearrange("p (t n) -> p t n", t=2), ACT.Copy)\
                       .then_inc(S("act_hi"), 2)
                for g in range(4):
                    s = g % 2
                    act.wait_ge(S("a_nm"), g + 1)
                    for b in range(8):
                        src = SB1[s][:, b, :] if b < 4 else SB0[s][:, b - 4, :]
                        act.activation(src, src, ACT.Exp, bias=NM[:, s, b:b + 1], accum_out=SMX[:, s, b:b + 1])\
                           .then_inc(S("a_ex"), 1)
                    if g < 2:
                        act.wait_ge(S("a_se0"), g + 1)
                        act.activation(SE[:, g, :], SE[:, g, :], ACT.Exp).then_inc(S("a_sink"), 1)
                    if g >= 1:
                        keys_out(g - 1)
                        mixed_hi(g - 1)
                keys_out(3)
                mixed_hi(3)
                for j in range(4):
                    split_w(None, FIRST["b1_out"] + j + AHEAD)
                squares(lambda k: FB[:, k, :], lambda k: SQ1[:, k, :], 0, lambda k: act.wait_ge(S("f_ev"), k // 2 + 1))
                norm_std(3, 2)
                gained("ffn2_pre_g", lambda k: act.wait_ge(S("xu"), KT + k + 1))

            gained("ple_pre_g", lambda k: act.wait_ge(S("xu"), 2 * KT + k + 1))
            norm_std(6, 2)
            for j in range(4):
                split_w(None, FIRST["ple_gate"] + j + AHEAD)
                act.wait_ge(S("pg"), j + 1)
                act.activation(PG[:, 2 * j:2 * j + 2, :], GU[:, j % RING, :, :], ACT.Sigmoid).then_inc(S("pg_sig"), 1)
            split_w(None, FIRST["ple_proj"] + AHEAD)
            squares(lambda k: FB[:, k, :], lambda k: SQ1[:, k, :], 0, lambda k: act.wait_ge(S("f_ev"), 5))
            norm_std(7, 2)

            def mod_tile(first, k, v):
                return MOD[:, layer, first + k, v:v + 1]

            def modulated(n_norm, inst, which, shift, t, ready):
                n = P * t
                squares(lambda k: X[:, k, 0:n], lambda k: SQ2[:, k, 0:n], 0, ready)
                norm_std(n_norm, t)
                for k in range(KT):
                    if t == 4:
                        act.wait_ge(S("xr"), KT * inst + k + 1)
                        act.activation(SQ2[:, k, TX:TB], SQ2[:, k, TX:TB], ACT.Identity,
                                       scale=GM[:, layer, which, k, 1:2], bias=mod_tile(shift, k, 1)).then_inc(S("xm_ctx"), 1)
                        act.wait_ge(S("xm_ctx"), KT * inst + k + 1)
                    act.wait_ge(S("xm"), KT * inst + k + 1)
                    act.activation(AHI2[:, k, 0:n], SQ2[:, k, 0:n], ACT.Copy).then_inc(S("act_hi"), 1)

            for layer in range(2):
                nt = TB if layer == 0 else TX
                for l in range(3):
                    act.wait_ge(S("f_arg"), 6 * (3 * layer + l + 1))
                    act.activation(HA[:, l, :], FU[:, 4, :], ACT.Sin).then_inc(S("f_h"), 1)
                act.wait_ge(S("f_k"), layer + 1)
                act.activation(KR[:, :, :], PS[:, 4:6, :], ACT.Copy).then_inc(S("f_kc"), 1)
                act.activation(KIZ[:, :, :], PS[:, 6:8, :], ACT.Copy).then_inc(S("f_kc"), 1)
                act.activation(KRX[:, :], PS[:, 4, :], ACT.Copy).then_inc(S("f_kc"), 1)

                if layer == 0:
                    modulated(8, 0, 0, 0, 4, lambda k: (act.wait_ge(S("xu"), 4 * KT), act.wait_ge(S("c_ev"), 4)))
                else:
                    modulated(10, 2, 0, 0, 4, lambda k: act.wait_ge(S("xd"), 2 * (k + 1)))
                for q in range(6):
                    n = TB if layer == 0 or q >= 4 else TX
                    c = FIRST[f"qkv{layer}"] + q
                    split_w(None, c + AHEAD)
                    act.wait_ge(S("pe_done"), c + 1)
                    act.activation(QKV[:, 2 * q:2 * q + 2, 0:n], ring2(q, n), ACT.Copy).then_inc(S("qkv_ev"), 1)
                for j in range(10):
                    n = nt if j < 8 else TB
                    act.wait_ge(S("qkv_ev"), 6 * layer + j // 2 + 1)
                    if j >= 4:
                        act.wait_ge(S("h_ss"), 10 * layer + j - 3)
                    act.activation(HSQ[:, j % 4, 0:n], QKV[:, j, 0:n], ACT.Square).then_inc(S("h_sq"), 1)
                    act.activation(QKV[:, j, 0:n], QKV[:, j, 0:n], ACT.Identity,
                                   scale=par("q_norm_2" if j < 8 else "k_norm_2", layer)).then_inc(S("h_gain"), 1)
                act.wait_ge(S("h_ss"), 10 * layer + 10)
                tq = nt // P
                act.activation(STD[:, 0:8 * tq], PS[:, 6, 0:8 * tq], ACT.Sqrt, bias=EPSC[:, 1:2]).then_inc(S("h_std"), 1)
                act.activation(STD[:, 32:40], PS[:, 6, 32:40], ACT.Sqrt, scale=1.0 / DH2, bias=EPSC[:, 0:1])\
                   .then_inc(S("h_std"), 1)
                act.wait_ge(S("v_tr"), layer + 1)
                act.activation(VT2[:, :, :], PS[:, 2:4, :].rearrange("p a (b n) -> p (a b) n", n=P), ACT.Copy)\
                   .then_inc(S("v_ev"), 1)

                units = [(0, h) for h in range(NH2)] + ([(1, h) for h in range(NH2)] if layer == 0 else [])
                u0 = 2 * NH2 * layer

                def exps(u):
                    grp, h = units[u]
                    s = u % 2
                    act.wait_ge(S("b_nm"), 2 * (u0 + u) + 2)
                    for t in range(2):
                        src = PS[:, 2 * s + t, :] if grp == 0 else PS[:, 2 * s, TX * t:TX * t + TX]
                        n = TB if grp == 0 else TX
                        col = h * tq + 2 * grp + t
                        act.activation(PB[:, s, t, 0:n], src, ACT.Exp, scale=RC[:, col:col + 1],
                                       bias=NM[:, s, t:t + 1], accum_out=SMX[:, s, t:t + 1]).then_inc(S("b_ex"), 1)

                exps(0)
                for u, (grp, h) in enumerate(units):
                    if u + 1 < len(units):
                        exps(u + 1)
                    kts = 4 if grp == 0 else 2
                    act.wait_ge(S("b_tr"), u0 + u + 1)
                    act.activation(PT2[:, u % 2, 0:kts, :],
                                   PS[:, 4:4 + kts // 2, :].rearrange("p a (b n) -> p (a b) n", n=TX), ACT.Copy)\
                       .then_inc(S("b_pt"), 1)

                for q in range(6):
                    c = FIRST[f"hy{layer}"] + q
                    split_w(None, c + AHEAD)
                    act.wait_ge(S("pe_done"), c + 1)
                    for t in range(2):
                        m = 2 * q + t
                        act.activation(HY[:, m, 0:nt], ring2(q, nt)[:, t, :], ACT.Identity,
                                       scale=par("conv_w_2", 36 * layer + 12 + m), bias=par("conv_b_2", 12 * layer + m))\
                           .then_inc(S("hy_mid"), 1)
                for grp in range(nt // TX):
                    y = 2 * layer + grp
                    act.wait_ge(S("y_tr"), y + 1)
                    if grp:
                        act.wait_ge(S("y_fwd"), y)
                    act.activation(VTT[:, :, :], PS[:, 0:2, :], ACT.Copy).then_inc(S("y_vt"), 1)
                act.wait_ge(S("y_h"), 8 * (2 if layer == 0 else 3))
                for m in range(HT):
                    act.activation(HHI[:, m, 0:nt], HY[:, 8 + m, 0:nt], ACT.Copy).then_inc(S("hh_hi"), 1)
                for k in range(KT):
                    act.activation(A2HI[:, k, 0:nt], QKV[:, k, 0:nt], ACT.Copy).then_inc(S("a2_hi"), 1)
                for j in range(2):
                    c = FIRST[f"oh{layer}"] + j
                    split_w(None, c + AHEAD)
                    act.wait_ge(S("pe_done"), c + 1)
                    act.wait_ge(S("a2_lo"), KT * (layer + 1))
                    src = PS[:, 4 * j:4 * j + 4, 0:nt]
                    act.activation(MG[:, 4 * j:4 * j + 4, 0:nt], src, ACT.Copy).then_inc(S("oh_ev"), 1)

                def mix(i, m):
                    c = FIRST[f"mix{layer}"] + 3 * m
                    for g in range(2):
                        split_w(i, c + g + AHEAD)
                        act.wait_ge(S("pe_done"), lin(i, 3, c + g + 1))
                        if layer + m:
                            act.wait_ge(S("merge"), lin(i, 3, 12 * layer + 3 * (m - 1) + (1 if g == 0 else 3)))
                        act.activation(SG[:, g, :, 0:nt], ring2(g, nt), ACT.Sigmoid).then_inc(S("gate"), 1)
                    split_w(i, c + 2 + AHEAD)
                mix(None, 0)
                with act.Fori(0, 3) as i:
                    mix(i, 1)
                act.wait_ge(S("pe_done"), FIRST[f"out{layer}"])
                act.wait_ge(S("merge"), 12 * (layer + 1))
                for k in range(KT):
                    act.activation(AHI2[:, k, 0:nt], MG[:, k, 0:nt], ACT.Copy).then_inc(S("mg_hi"), 1)
                for j in range(4):
                    split_w(None, FIRST[f"out{layer}"] + j + AHEAD)

                t = nt // P
                per = nt // TX
                xo0 = 2 * KT * layer
                modulated(9 + 2 * layer, 1 + 2 * layer, 1, 24, t, lambda k: act.wait_ge(S("xo"), xo0 + per * (k + 1)))
                inst = 2 + layer

                def silus2(i, j, c):
                    split_w(i, c + AHEAD)
                    act.wait_ge(S("pe_done"), lin(i, 3, c + 1))
                    if j >= RING:
                        act.wait_ge(S("h"), lin(i, 3, FT * inst + j - RING + 1))
                    act.activation(SIL[:, j % RING, 0:nt], ring2(j, nt)[:, 0, :], ACT.Silu).then_inc(S("sil"), 1)
                steps(act, f"gu{layer}", silus2)
                down(f"dn{layer}", inst, HB2, SHI2, nt)

            squares(lambda k: X[:, k, 0:TX], lambda k: SQ1[:, k, :], 0, lambda k: act.wait_ge(S("xd"), 2 * KT + k + 1))
            norm_std(12, 2)
            for t in range(2):
                act.wait_ge(S("out_tr"), 2 * t + 2)
                act.activation(OUTS[:, t, 512:], PS[:, 2 * t + 1, :], ACT.Copy).then_inc(S("out_ev1"), 1)

        @block.vector
        def _(dve):
            def split_w(i, c):
                if c >= TOTAL:
                    return
                dve.wait_ge(S("hi_done"), lin(i, 3, c + 1))
                dve.tensor_tensor(WLO[:, c % RING, :], RAW[:, c % RING, :], WHI[:, c % RING, :].bitcast(F32), ALU.subtract)\
                   .then_inc(S("lo_done"), 1)

            def split_h(i, inst, j, hb, shi, slo, n):
                dve.wait_ge(S("hs_hi"), lin(i, 3, FT // 2 * inst + j + 1))
                dve.tensor_tensor(slo[:, j % RING, :, 0:n], hb[:, bass.ds(lin(i, 6, 2 * j), 2), 0:n],
                                  shi[:, j % RING, :, 0:n].bitcast(F32), ALU.subtract).then_inc(S("hs_lo"), 1)

            def down(stage, inst, hb, shi, slo, n):
                split_h(None, inst, 0, hb, shi, slo, n)
                split_h(None, inst, 1, hb, shi, slo, n)

                def body(i, j, c):
                    split_w(i, c + AHEAD)
                    if i is not None or j + AHEAD < FT // 2:
                        split_h(i, inst, j + AHEAD, hb, shi, slo, n)
                steps(dve, stage, body, tail=2)

            def norm_row(n_norm, t):
                dve.wait_ge(S("n_std"), n_norm + 1)
                dve.reciprocal(RC[:, 0:t], STD[:, 0:t]).then_inc(S("n_rc"), 1)
                dve.wait_ge(S("n_rc"), n_norm + 1)
                dve.tensor_tensor(DG[:, 0:t, :], over_tiles(IDENT[:, :], t), over_tokens(RC[:, 0:t], P), ALU.mult)\
                   .then_inc(S("n_dg"), 1)
                dve.wait_ge(S("n_rb"), n_norm + 1)
                dve.tensor_copy(RT[:, 0:P * t], stat_row(n_norm, t)).then_inc(S("n_rt"), 1)
                dve.wait_ge(S("n_rt"), n_norm + 1)

            def gained_lo(inst, name):
                for k in range(KT):
                    dve.wait_ge(S("act_hi"), KT * inst + k + 1)
                    dve.scalar_tensor_tensor(out=ALO1[:, k, :], in0=X[:, k, 0:TX], scalar=par(name, k),
                                             in1=AHI1[:, k, :].bitcast(F32), op0=ALU.mult, op1=ALU.subtract)\
                       .then_inc(S("act_lo"), 1)

            def branch(src, gain):
                for k in range(KT):
                    dve.scalar_tensor_tensor(out=TU[:, k, :], in0=src(k), scalar=gain(k), in1=RT[:, 0:TX],
                                             op0=ALU.mult, op1=ALU.mult).then_inc(S("xt"), 1)

            dve.memset(GS[:, 3, :], 0.0).then_inc(S("gs_clear"), 1)
            dve.memset(ONES[:, :], 1.0).then_inc(S("const"), 1)
            dve.memset(EPSC[:, 0:1], EPS).then_inc(S("const"), 1)
            dve.memset(EPSC[:, 1:2], EPS * DH2).then_inc(S("const"), 1)
            dve.wait_ge(S("tr_par"), 1)
            for g in range(4):
                dve.tensor_copy(PAR[:, g, 0:PAR_USED[g]], PS[:, 4, g * P:g * P + PAR_USED[g]]).then_inc(S("par_ev"), 1)
            split_w(None, 0)
            gained_lo(0, "ffn1_pre_g")
            split_w(None, 1)
            dve.wait_ge(S("tr_p"), 1)
            dve.tensor_copy(P32[:, :, :], PS[:, 5, :].rearrange("p (t n) -> p t n", t=2)).then_inc(S("p_ev"), 1)
            dve.wait_ge(S("in_bias"), 48)
            dve.wait_ge(S("mm_ext"), 1)
            dve.tensor_tensor(EXT[:, :], PS[0:16, 6, 0:384], MASK[:, :], ALU.add).then_inc(S("ext_ev"), 1)
            dve.wait_ge(S("p_hi"), 1)
            dve.tensor_tensor(PLO[:, :, :], P32[:, :, :], PHI[:, :, :].bitcast(F32), ALU.subtract).then_inc(S("p_lo"), 1)
            dve.wait_ge(S("par_ev"), 4)
            dve.tensor_scalar(HG[:, 0, :], par("ffn1_post_g", 0, 8), 0.5, None, ALU.mult).then_inc(S("hg"), 1)
            dve.tensor_scalar(HG[:, 1, :], par("ffn2_post_g", 0, 8), 0.5, None, ALU.mult).then_inc(S("hg"), 1)
            dve.wait_ge(S("in_sink"), 16)
            dve.tensor_scalar(SINK[:, 1, :], SINK[:, 0, :], -1.0, None, ALU.mult).then_inc(S("nsink"), 1)
            for b in range(4):
                dve.wait_ge(S("tr_c"), b + 1)
                dve.tensor_copy(X[:, 2 * b:2 * b + 2, TX:TB], PS[:, b, :].rearrange("p (t n) -> p t n", t=2))\
                   .then_inc(S("c_ev"), 1)

            for inst, (pre, post) in enumerate(((0, 1), (4, 5))):
                f = f"ffn{inst + 1}"

                def hidden1(i, j, c):
                    split_w(i, c + AHEAD)
                    if i is None and j == 0:
                        norm_row(pre, 2)
                    dve.wait_ge(S("pe_done"), lin(i, 3, c + 1))
                    dve.tensor_tensor(GU[:, j % RING, :, :], ring1(j), over_tiles(RT[:, 0:TX], 2), ALU.mult)\
                       .then_inc(S("gu"), 1)
                    dve.wait_ge(S("sil"), lin(i, 3, FT * inst + j + 1))
                    dve.tensor_tensor(HB1[:, bass.ds(lin(i, 3, j), 1), :], GU[:, j % RING, 0:1, :], GU[:, j % RING, 1:2, :],
                                      ALU.mult).then_inc(S("h"), 1)
                steps(dve, f + "_gu", hidden1)
                down(f + "_dn", inst, HB1, SHI1, SLO1, TX)
                dve.wait_ge(S("mod_used"), MODC * (inst + 1))
                dve.tensor_tensor(MOD[:, inst, :, :], PS[:, 7, 96 * inst:96 * inst + 96].rearrange("p (m v) -> p m v", v=2),
                                  over_tokens(par("b_mod_2", 48 * inst, 48), 2), ALU.add).then_inc(S("mod_ev"), 1)
                dve.wait_ge(S("mod_ev"), 3 * inst + 1)
                for w, (first, name) in enumerate(((8, "norm_mix_2"), (32, "norm_ffn_2"))):
                    dve.scalar_tensor_tensor(out=GM[:, inst, w, :, :], in0=MOD[:, inst, first:first + 8, :], scalar=1.0,
                                             in1=over_tokens(par(name, 8 * inst, 8), 2), op0=ALU.add, op1=ALU.mult)\
                       .then_inc(S("mod_ev"), 1)
                norm_row(post, 2)
                dve.wait_ge(S("hg"), 2)
                branch(lambda k: acc(k, TX), lambda k: HG[:, inst, k:k + 1])
                if inst == 1:
                    break
                gained_lo(1, "attn_pre_g")

                def z_tiles(i, j, c):
                    split_w(i, c + AHEAD)
                    if i is None and j == 0:
                        norm_row(2, 2)
                    dve.wait_ge(S("pe_done"), lin(i, 3, c + 1))
                    dve.tensor_tensor(GU[:, j % RING, :, :], ring1(j), over_tiles(RT[:, 0:TX], 2), ALU.mult)\
                       .then_inc(S("zt"), 1)
                    dve.wait_ge(S("zt"), lin(i, 6, 2 * j + 1))
                    g, row, _ = PAR_AT["b_in"]
                    bias = PAR[:, g, bass.ds(lin(i, 6, row + 2 * j), 2)]
                    dve.tensor_tensor(Z[:, bass.ds(lin(i, 6, 2 * j), 2), :], GU[:, j % RING, :, :], over_tokens(bias, TX),
                                      ALU.add).then_inc(S("zt"), 1)
                steps(dve, "b1_in", z_tiles)

                for b in range(3):
                    dve.wait_ge(S("vt_tr"), b + 1)
                    n = 4 if b < 2 else 2
                    dve.tensor_copy(VT1[:, 4 * b:4 * b + n, :], PS[:, b, 0:n * P].rearrange("p (a n) -> p a n", n=P))\
                       .then_inc(S("vt_ev"), 1)

                def scores_in(g):
                    s = g % 2
                    dve.wait_ge(S("a_s"), g + 1)
                    heads = BIAS[g // 2][:, 4 * (g % 2):4 * (g % 2) + 4, ::-1]
                    for a in range(2):
                        dve.scalar_tensor_tensor(out=SB1[s][:, a::2, :], in0=PS[:, a, :].rearrange("p (b n) -> p b n", n=TX),
                                                 scalar=DH1 ** -0.5, in1=heads[:, a::2, :], op0=ALU.mult, op1=ALU.add)\
                           .then_inc(S("a_sb"), 1)
                    dve.scalar_tensor_tensor(out=SB0[s][:, :, :], in0=PS[:, 2, :].rearrange("p (b n) -> p b n", n=P),
                                             scalar=DH1 ** -0.5, in1=heads[:, :, P:TX], op0=ALU.mult, op1=ALU.add)\
                       .then_inc(S("a_sb"), 1)
                    dve.wait_ge(S("a_sb"), 3 * g + 3)
                    dve.tensor_reduce(SE[:, s, 0:4] if g < 2 else NM[:, s, 0:4], SB1[s][:, :, :], AX.X, ALU.max, negate=True)\
                       .then_inc(S("a_mx"), 1)
                    last = dve.tensor_reduce(SE[:, s, 4:8] if g < 2 else NM[:, s, 4:8], SB0[s][:, :, :], AX.X, ALU.max,
                                             negate=True)
                    if g >= 2:
                        last.then_inc(S("a_nm"), 1)
                        return
                    last.then_inc(S("a_mx"), 1)
                    dve.wait_ge(S("a_mx"), 2 * g + 2)
                    dve.wait_ge(S("nsink"), 1)
                    sinks = over_tiles(SINK[:, 1, 4 * g:4 * g + 4], 2)
                    dve.tensor_tensor(NM[:, s, :].rearrange("p (t h) -> p t h", t=2), SE[:, s, :].rearrange("p (t h) -> p t h", t=2),
                                      sinks, ALU.min).then_inc(S("a_nm"), 1)
                    dve.wait_ge(S("a_nm"), g + 1)
                    dve.tensor_tensor(SE[:, s, :].rearrange("p (t h) -> p t h", t=2), NM[:, s, :].rearrange("p (t h) -> p t h", t=2),
                                      sinks, ALU.subtract).then_inc(S("a_se0"), 1)

                def normalise(g):
                    s = g % 2
                    dve.wait_ge(S("a_ex"), 8 * g + 8)
                    if g < 2:
                        dve.wait_ge(S("a_sink"), g + 1)
                        dve.tensor_tensor(SMX[:, s, :], SMX[:, s, :], SE[:, s, :], ALU.add).then_inc(S("a_tot"), 1)
                        dve.wait_ge(S("a_tot"), g + 1)
                    dve.reciprocal(RS[:, s, :], SMX[:, s, :]).then_inc(S("a_rs"), 1)
                    dve.wait_ge(S("a_rs"), g + 1)
                    dve.tensor_tensor(SB1[s][:, :, :], SB1[s][:, :, :], over_tokens(RS[:, s, 0:4], TX), ALU.mult)\
                       .then_inc(S("a_p"), 1)
                    dve.tensor_tensor(SB0[s][:, :, :], SB0[s][:, :, :], over_tokens(RS[:, s, 4:8], P), ALU.mult)\
                       .then_inc(S("a_p"), 1)

                def mixed_lo(g):
                    dve.wait_ge(S("act_hi"), 2 * KT + 2 * g + 2)
                    dve.tensor_tensor(ALO1[:, 2 * g:2 * g + 2, :], PS[:, 7, :].rearrange("p (t n) -> p t n", t=2),
                                      AHI1[:, 2 * g:2 * g + 2, :].bitcast(F32), ALU.subtract).then_inc(S("act_lo"), 2)

                dve.wait_ge(S("bias_in"), 32)
                scores_in(0)
                for g in range(4):
                    normalise(g)
                    if g < 3:
                        scores_in(g + 1)
                    if g >= 1:
                        mixed_lo(g - 1)
                mixed_lo(3)
                for j in range(4):
                    c = FIRST["b1_out"] + j
                    split_w(None, c + AHEAD)
                    dve.wait_ge(S("pe_done"), c + 1)
                    dve.tensor_tensor(FB[:, 2 * j:2 * j + 2, :], ring1(j), over_tokens(par("b_out", 2 * j, 2), TX), ALU.add)\
                       .then_inc(S("f_ev"), 1)
                norm_row(3, 2)
                dve.wait_ge(S("f_ev"), 4)
                branch(lambda k: FB[:, k, :], lambda k: par("attn_post_g", k))
                gained_lo(3, "ffn2_pre_g")

            gained_lo(4, "ple_pre_g")
            for j in range(4):
                c = FIRST["ple_gate"] + j
                split_w(None, c + AHEAD)
                if j == 0:
                    norm_row(6, 2)
                dve.wait_ge(S("pe_done"), c + 1)
                if j >= RING:
                    dve.wait_ge(S("pg_sig"), j - RING + 1)
                dve.tensor_tensor(GU[:, j % RING, :, :], ring1(j), over_tiles(RT[:, 0:TX], 2), ALU.mult).then_inc(S("pg"), 1)
            split_w(None, FIRST["ple_proj"] + AHEAD)
            dve.wait_ge(S("pe_done"), FIRST["ple_proj"] + 1)
            dve.wait_ge(S("pg_sig"), 4)
            dve.tensor_tensor(FB[:, :, :], PG[:, :, :], PS[:, 0:4, :].rearrange("p a (b n) -> p (a b) n", n=TX), ALU.mult)\
               .then_inc(S("f_ev"), 1)
            norm_row(7, 2)
            dve.wait_ge(S("f_ev"), 5)
            branch(lambda k: FB[:, k, :], lambda k: par("ple_post_g", k))

            def modulated(n_norm, inst, a_inst, which, shift, t):
                n = P * t
                norm_row(n_norm, t)

                def low(k):
                    dve.wait_ge(S("act_hi"), KT * a_inst + k + 1)
                    dve.tensor_tensor(ALO2[:, k, 0:n], SQ2[:, k, 0:n], AHI2[:, k, 0:n].bitcast(F32), ALU.subtract)\
                       .then_inc(S("act_lo"), 1)
                for k in range(KT):
                    dve.tensor_tensor(SQ2[:, k, 0:n], X[:, k, 0:n], RT[:, 0:n], ALU.mult).then_inc(S("xr"), 1)
                    dve.wait_ge(S("xr"), KT * inst + k + 1)
                    dve.tensor_scalar(SQ2[:, k, 0:TX], SQ2[:, k, 0:TX], GM[:, layer, which, k, 0:1],
                                      MOD[:, layer, shift + k, 0:1], ALU.mult, ALU.add).then_inc(S("xm"), 1)
                    if k:
                        low(k - 1)
                low(KT - 1)

            for layer in range(2):
                nt = TB if layer == 0 else TX
                for l in range(3):
                    a0 = 6 * (3 * layer + l)
                    dve.wait_ge(S("f_mm"), 3 * layer + l + 1)
                    bias = PAR[0:FH, 3, PAR_AT[f"filt_b{l + 1}_2"][1] + layer:PAR_AT[f"filt_b{l + 1}_2"][1] + layer + 1]
                    fr = PAR_AT["filt_freq_2"][1] + 3 * layer + l
                    dve.tensor_scalar(FU[:, 0, :], PS[0:FH, 4, 0:TX], bias, PAR[0:FH, 3, fr:fr + 1], ALU.add, ALU.mult)\
                       .then_inc(S("f_arg"), 1)
                    dve.wait_ge(S("f_arg"), a0 + 1)
                    dve.tensor_scalar(FU[:, 1, :], FU[:, 0, :], 1.0 / (2.0 * np.pi), MAGIC, ALU.mult, ALU.add)\
                       .then_inc(S("f_arg"), 1)
                    dve.wait_ge(S("f_arg"), a0 + 2)
                    dve.tensor_scalar(FU[:, 2, :], FU[:, 1, :], -MAGIC, None, ALU.add).then_inc(S("f_arg"), 1)
                    dve.wait_ge(S("f_arg"), a0 + 3)
                    dve.scalar_tensor_tensor(out=FU[:, 3, :], in0=FU[:, 2, :], scalar=-TWO_PI_HI, in1=FU[:, 0, :],
                                             op0=ALU.mult, op1=ALU.add).then_inc(S("f_arg"), 1)
                    dve.wait_ge(S("f_arg"), a0 + 4)
                    dve.scalar_tensor_tensor(out=FU[:, 0, :], in0=FU[:, 2, :], scalar=-TWO_PI_LO, in1=FU[:, 3, :],
                                             op0=ALU.mult, op1=ALU.add).then_inc(S("f_arg"), 1)
                    dve.wait_ge(S("f_arg"), a0 + 5)
                    dve.tensor_scalar(FU[:, 4, :], FU[:, 0, :], PI_IN, -PI_IN, ALU.min, ALU.max).then_inc(S("f_arg"), 1)
                dve.wait_ge(S("f_taps"), layer + 1)
                for t in range(2):
                    for r in range(2):
                        dve.tensor_tensor(HF[:, t, r, :], PS[:, 2 * t + r, :], DEC[:, t, :], ALU.mult).then_inc(S("f_dec"), 1)
                dve.wait_ge(S("f_kc"), 3 * layer + 3)
                dve.tensor_copy(KRX[0:1, :], PS[0:1, 6, :]).then_inc(S("f_fix"), 1)
                dve.memset(KIZ[0:1, 0, :], 0.0).then_inc(S("f_fix"), 1)

                modulated(8 + 2 * layer, 2 * layer, 5 + 2 * layer, 0, 0, 4)
                for q in range(6):
                    split_w(None, FIRST[f"qkv{layer}"] + q + AHEAD)

                for j in range(10):
                    dve.wait_ge(S("h_rot"), 10 * layer + j + 1)
                    dve.tensor_tensor(BR[:, j % 2, :], PS[:, j % 2, 0:TX], ROPE[:, 1, :], ALU.mult).then_inc(S("h_sin"), 1)
                    dve.wait_ge(S("h_sin"), 10 * layer + j + 1)
                    dve.wait_ge(S("h_cos"), 10 * layer + j + 1)
                    dve.tensor_tensor(QKV[:, j, 0:TX], QKV[:, j, 0:TX], BR[:, j % 2, :], ALU.add).then_inc(S("h_sum"), 1)
                tq = nt // P
                dve.wait_ge(S("h_std"), 2 * layer + 1)
                dve.reciprocal(RC[:, 0:8 * tq], STD[:, 0:8 * tq]).then_inc(S("h_rc"), 1)
                dve.wait_ge(S("h_std"), 2 * layer + 2)
                dve.reciprocal(RC[:, 32:40], STD[:, 32:40]).then_inc(S("h_rc"), 1)
                dve.wait_ge(S("h_rc"), 2 * layer + 2)
                for kv in range(2):
                    dve.tensor_tensor(DGK[:, kv, :, :], over_tiles(IDENT[:, :], 4),
                                      over_tokens(RC[:, 32 + 4 * kv:36 + 4 * kv], P), ALU.mult).then_inc(S("h_dg"), 1)
                dve.wait_ge(S("h_sum"), 10 * layer + 10)
                for kv in range(2):
                    dve.wait_ge(S("h_rb"), 2 * layer + kv + 1)
                    dve.tensor_tensor(QKV[:, 8 + kv, :], QKV[:, 8 + kv, :], PS[:, 5 + 2 * kv, :], ALU.mult).then_inc(S("h_key"), 1)

                units = [(0, h) for h in range(NH2)] + ([(1, h) for h in range(NH2)] if layer == 0 else [])
                u0 = 2 * NH2 * layer

                def maxima(u):
                    grp, h = units[u]
                    s = u % 2
                    dve.wait_ge(S("b_s"), u0 + u + 1)
                    src = PS[:, 2 * s:2 * s + 2, :] if grp == 0 else PS[:, 2 * s, :].rearrange("p (t n) -> p t n", t=2)
                    dve.tensor_reduce(NM[:, s, 2:4], src, AX.X, ALU.max, negate=True).then_inc(S("b_nm"), 1)
                    dve.wait_ge(S("b_nm"), 2 * (u0 + u) + 1)
                    col = h * tq + 2 * grp
                    dve.tensor_tensor(NM[:, s, 0:2], NM[:, s, 2:4], RC[:, col:col + 2], ALU.mult).then_inc(S("b_nm"), 1)

                def normalise2(u):
                    s = u % 2
                    n = TB if units[u][0] == 0 else TX
                    dve.wait_ge(S("b_ex"), 2 * (u0 + u) + 2)
                    dve.reciprocal(RS[:, s, 0:2], SMX[:, s, 0:2]).then_inc(S("b_rs"), 1)
                    dve.wait_ge(S("b_rs"), u0 + u + 1)
                    for t in range(2):
                        dve.tensor_scalar(PB[:, s, t, 0:n], PB[:, s, t, 0:n], RS[:, s, t:t + 1], None, ALU.mult)\
                           .then_inc(S("b_p"), 1)

                def attended(u):
                    grp, h = units[u]
                    dve.wait_ge(S("b_pv"), u0 + u + 1)
                    dve.tensor_copy(QKV[:, h, TX * grp:TX * grp + TX], PS[:, 6 + u % 2, 0:TX]).then_inc(S("b_o"), 1)

                maxima(0)
                for u in range(len(units)):
                    if u + 1 < len(units):
                        maxima(u + 1)
                    normalise2(u)
                    if u:
                        attended(u - 1)
                attended(len(units) - 1)

                for q in range(6):
                    c = FIRST[f"hy{layer}"] + q
                    split_w(None, c + AHEAD)
                    for t in range(2):
                        m = 2 * q + t
                        dve.wait_ge(S("hy_mid"), 12 * layer + 2 * q + 2)
                        u3 = ring2(q, nt)[:, t, :].rearrange("p (g n) -> p g n", n=TX)
                        y3 = HY[:, m, 0:nt].rearrange("p (g n) -> p g n", n=TX)
                        dve.scalar_tensor_tensor(out=y3[:, :, 1:TX], in0=u3[:, :, 0:TX - 1], scalar=par("conv_w_2", 36 * layer + m),
                                                 in1=y3[:, :, 1:TX], op0=ALU.mult, op1=ALU.add).then_inc(S("hy_taps"), 1)
                        dve.wait_ge(S("hy_taps"), 24 * layer + 2 * m + 1)
                        dve.scalar_tensor_tensor(out=y3[:, :, 0:TX - 1], in0=u3[:, :, 1:TX],
                                                 scalar=par("conv_w_2", 36 * layer + 24 + m), in1=y3[:, :, 0:TX - 1],
                                                 op0=ALU.mult, op1=ALU.add).then_inc(S("hy_taps"), 1)
                dve.wait_ge(S("f_fix"), 2 * layer + 2)
                for grp in range(nt // TX):
                    y = 2 * layer + grp
                    re, im = PS[:, 2:4, :], PS[:, 4:6, :]
                    if y:
                        dve.wait_ge(S("y_h"), 8 * y)
                    dve.wait_ge(S("y_fwd"), y + 1)
                    dve.tensor_tensor(YT1[:, :, :], re, KR[:, :, :], ALU.mult).then_inc(S("y_mul"), 1)
                    dve.tensor_tensor(YT2[:, :, :], im, KIZ[:, :, :], ALU.mult).then_inc(S("y_mul"), 1)
                    dve.wait_ge(S("y_mul"), 7 * y + 2)
                    dve.tensor_tensor(YS[:, 0:2, :], YT1[:, :, :], YT2[:, :, :], ALU.subtract).then_inc(S("y_mul"), 1)
                    dve.wait_ge(S("y_mul"), 7 * y + 3)
                    dve.tensor_tensor(YT1[:, :, :], re, KIZ[:, :, :], ALU.mult).then_inc(S("y_mul"), 1)
                    dve.tensor_tensor(YT2[:, 0, :], im[:, 0, :], KRX[:, :], ALU.mult).then_inc(S("y_mul"), 1)
                    dve.tensor_tensor(YT2[:, 1, :], im[:, 1, :], KR[:, 1, :], ALU.mult).then_inc(S("y_mul"), 1)
                    dve.wait_ge(S("y_mul"), 7 * y + 6)
                    dve.tensor_tensor(YS[:, 2:4, :], YT1[:, :, :], YT2[:, :, :], ALU.add).then_inc(S("y_mul"), 1)
                    dve.wait_ge(S("y_mul"), 7 * y + 7)
                    dve.wait_ge(S("y_inv"), y + 1)
                    g = slice(TX * grp, TX * grp + TX)
                    for m in range(HT):
                        tmp = YT1[:, m // 2, m % 2 * TX:m % 2 * TX + TX]
                        out = PS[:, 6 + m // 2, m % 2 * TX:m % 2 * TX + TX]
                        dve.scalar_tensor_tensor(out=tmp, in0=HY[:, 8 + m, g], scalar=par("hyena_bias_2", 4 * layer + m), in1=out,
                                                 op0=ALU.mult, op1=ALU.add).then_inc(S("y_h"), 1)
                        dve.wait_ge(S("y_h"), 8 * y + 2 * m + 1)
                        dve.tensor_tensor(HY[:, 8 + m, g], tmp, HY[:, m, g], ALU.mult).then_inc(S("y_h"), 1)
                for m in range(HT):
                    dve.wait_ge(S("hh_hi"), HT * layer + m + 1)
                    dve.tensor_tensor(HLO[:, m, 0:nt], HY[:, 8 + m, 0:nt], HHI[:, m, 0:nt].bitcast(F32), ALU.subtract)\
                       .then_inc(S("hh_lo"), 1)
                dve.wait_ge(S("hh_lo"), HT * (layer + 1))
                for k in range(KT):
                    dve.wait_ge(S("a2_hi"), KT * layer + k + 1)
                    dve.tensor_tensor(A2LO[:, k, 0:nt], QKV[:, k, 0:nt], A2HI[:, k, 0:nt].bitcast(F32), ALU.subtract)\
                       .then_inc(S("a2_lo"), 1)
                for j in range(2):
                    split_w(None, FIRST[f"oh{layer}"] + j + AHEAD)

                def mix(i, m):
                    c = FIRST[f"mix{layer}"] + 3 * m
                    b = 12 * layer + 3 * m
                    mg = MG[:, bass.ds(lin(i, 2, 2 * m), 2), 0:nt]
                    split_w(i, c + AHEAD)
                    dve.wait_ge(S("gate"), lin(i, 2, 8 * layer + 2 * m + 1))
                    dve.tensor_tensor(mg, mg, SG[:, 0, :, 0:nt], ALU.mult).then_inc(S("merge"), 1)
                    split_w(i, c + 1 + AHEAD)
                    split_w(i, c + 2 + AHEAD)
                    dve.wait_ge(S("gate"), lin(i, 2, 8 * layer + 2 * m + 2))
                    dve.wait_ge(S("pe_done"), lin(i, 3, c + 3))
                    dve.tensor_tensor(SG[:, 1, :, 0:nt], SG[:, 1, :, 0:nt], ring2(2, nt), ALU.mult).then_inc(S("merge"), 1)
                    dve.wait_ge(S("merge"), lin(i, 3, b + 2))
                    dve.tensor_tensor(mg, mg, SG[:, 1, :, 0:nt], ALU.add).then_inc(S("merge"), 1)
                mix(None, 0)
                with dve.Fori(0, 3) as i:
                    mix(i, 1)
                for k in range(KT):
                    dve.wait_ge(S("mg_hi"), KT * layer + k + 1)
                    dve.tensor_tensor(ALO2[:, k, 0:nt], MG[:, k, 0:nt], AHI2[:, k, 0:nt].bitcast(F32), ALU.subtract)\
                       .then_inc(S("mg_lo"), 1)

                def gated_update(src, m, gate, sem):
                    for v in range(nt // TX):
                        g = slice(TX * v, TX * v + TX)
                        dve.scalar_tensor_tensor(out=X[:, m, g], in0=src[:, g], scalar=MOD[:, layer, gate + m, v:v + 1],
                                                 in1=X[:, m, g], op0=ALU.mult, op1=ALU.add).then_inc(S(sem), 1)
                for j in range(4):
                    c = FIRST[f"out{layer}"] + j
                    split_w(None, c + AHEAD)
                    dve.wait_ge(S("pe_done"), c + 1)
                    for t in range(2):
                        gated_update(ring2(j, nt)[:, t, :], 2 * j + t, 16, "xo")
                xo_now = 2 * KT if layer == 0 else 3 * KT
                dve.wait_ge(S("xo"), xo_now)
                modulated(9 + 2 * layer, 1 + 2 * layer, 6 + 2 * layer, 1, 24, nt // P)
                inst = 2 + layer

                def hidden2(i, j, c):
                    split_w(i, c + AHEAD)
                    dve.wait_ge(S("sil"), lin(i, 3, FT * inst + j + 1))
                    dve.tensor_tensor(HB2[:, bass.ds(lin(i, 3, j), 1), 0:nt], SIL[:, j % RING:j % RING + 1, 0:nt],
                                      ring2(j, nt)[:, 1:2, :], ALU.mult).then_inc(S("h"), 1)
                steps(dve, f"gu{layer}", hidden2)
                down(f"dn{layer}", inst, HB2, SHI2, SLO2, nt)
                dve.wait_ge(S("pe_done"), FIRST[f"dn{layer}"] + FT // 2)
                for m in range(KT):
                    gated_update(acc(m, nt), m, 40, "xd")

            dve.wait_ge(S("xd"), 3 * KT)
            norm_row(12, 2)
            for k in range(KT):
                dve.scalar_tensor_tensor(out=YF[:, k, :], in0=X[:, k, 0:TX], scalar=par("norm_final_2", k), in1=RT[:, 0:TX],
                                         op0=ALU.mult, op1=ALU.mult).then_inc(S("yf"), 1)
            for t in range(2):
                dve.wait_ge(S("out_tr"), 2 * t + 1)
                dve.tensor_copy(OUTS[:, t, 0:512], PS[:, 2 * t, :]).then_inc(S("out_ev0"), 1)

        @block.tensor
        def _(pe):
            def product(out, whi, wlo, xhi, xlo, first, last, shared=False):
                pe.matmul(out, whi, xhi, start=first, stop=False, skip_group_check=shared)
                pe.matmul(out, whi, xlo, start=False, stop=False, skip_group_check=shared)
                return pe.matmul(out, wlo, xhi, start=False, stop=last, skip_group_check=shared)

            def weights(c, t, k, width):
                a = k * width + t * P
                return WHI[:, c % RING, a:a + P], WLO[:, c % RING, a:a + P]

            def chunk_ready(i, c):
                pe.wait_ge(S("lo_done"), lin(i, 3, c + 1))

            def by_columns(i, c, outs, hi, lo, n, k_tiles=KT, width=2 * P, ready=None):
                chunk_ready(i, c)
                for t, out in enumerate(outs):
                    for k in range(k_tiles):
                        if ready and t == 0:
                            ready(k)
                        last = product(out, *weights(c, t, k, width), hi[:, k, 0:n], lo[:, k, 0:n], k == 0, k == k_tiles - 1)
                last.then_inc(S("pe_done"), 1)

            def down(stage, inst, shi, slo, n):
                def body(i, j, c):
                    chunk_ready(i, c)
                    pe.wait_ge(S("hs_lo"), lin(i, 3, FT // 2 * inst + j + 1))
                    end = i is None and j == FT // 2 - 1
                    for m in range(KT):
                        for kk in range(2):
                            start = i is None and j == 0 and kk == 0 and (n == TB or m % 2 == 0)
                            last = product(acc(m, n), *weights(c, m, kk, D), shi[:, j % RING, kk, 0:n],
                                           slo[:, j % RING, kk, 0:n], start, end and kk == 1, shared=True)
                    last.then_inc(S("pe_done"), 1)
                    if stage in ("ffn1_dn", "ffn2_dn") and i is None and j < MODC - FT:
                        modulation(inst, None, FT + j)
                steps(pe, stage, body, tail=2)

            def modulation(layer, i, g):
                pe.wait_ge(S(f"mod_raw{g % RING}"), lin(i, 16, 16 * (MODC // RING * layer + g // RING + 1)))
                for t in range(2):
                    out = PS[:, 7, bass.ds(lin(i, 12, 96 * layer + 4 * g + 2 * t), 2)]
                    for k in range(KT):
                        last = pe.matmul(out, MRAW[:, g % RING, k * 2 * P + t * P:k * 2 * P + t * P + P], SC[:, :, k],
                                         start=k == 0, stop=k == KT - 1)
                last.then_inc(S("mod_used"), 1)

            def norm_sums(n_norm, t, src):
                pe.wait_ge(S("n_sq"), KT * (n_norm + 1))
                sums = stat_sum(n_norm, t)
                for tt in range(t):
                    for k in range(KT):
                        last = pe.matmul(sums[:, tt:tt + 1], src[:, k, tt * P:tt * P + P], ONES[:, 0:1],
                                         start=k == 0, stop=k == KT - 1)
                last.then_inc(S("n_ss"), 1)

            def norm_rows(n_norm, t):
                pe.wait_ge(S("n_dg"), n_norm + 1)
                row = stat_row(n_norm, t)
                for tt in range(t):
                    last = pe.matmul(row[:, tt * P:tt * P + P], ONES[:, :], DG[:, tt, :], start=True, stop=True)
                last.then_inc(S("n_rb"), 1)

            def wait_k(sem, before):
                return lambda k: pe.wait_ge(S(sem), before + k + 1)

            pe.wait_ge(S("in_ident"), 16)
            pe.wait_ge(S("in_x"), 16)
            for b in range(4):
                for k in (2 * b, 2 * b + 1):
                    for t in range(2):
                        last = pe.transpose(PS[:, b, k % 2 * TX + t * P:k % 2 * TX + t * P + P], XS[:, t, k * P:k * P + P], IDENT[:, :])
                last.then_inc(S("tr_x"), 1)
            pe.wait_ge(S("gs_clear"), 1)
            pe.wait_ge(S("in_par"), 16 * len(PAR_AT))
            for g in range(4):
                n = PAR_USED[g]
                last = pe.transpose(PS[:, 4, g * P:g * P + n], GS[0:n, g, :], IDENT[0:n, 0:n])
            last.then_inc(S("tr_par"), 1)
            pe.wait_ge(S("in_p"), 16)
            for k in range(2):
                for t in range(2):
                    last = pe.transpose(PS[:, 5, k * TX + t * P:k * TX + t * P + P], PST[:, t, k * P:k * P + P], IDENT[:, :])
            last.then_inc(S("tr_p"), 1)
            pe.wait_ge(S("in_bias"), 48)
            pe.matmul(PS[0:16, 6, 0:384], REL[:, :], ONEHOT[:, :], start=True, stop=True).then_inc(S("mm_ext"), 1)
            pe.wait_ge(S("in_ctx"), 16)
            for b in range(4):
                pe.wait_ge(S("x_ev"), b + 1)
                for k in (2 * b, 2 * b + 1):
                    for t in range(2):
                        last = pe.transpose(PS[:, b, k % 2 * TX + t * P:k % 2 * TX + t * P + P], CS[:, t, k * P:k * P + P], IDENT[:, :])
                last.then_inc(S("tr_c"), 1)
            pe.wait_ge(S("const"), 3)

            for inst, (pre, post) in enumerate(((0, 1), (4, 5))):
                f = f"ffn{inst + 1}"

                def gate_up(i, j, c):
                    first = i is None and j == 0
                    if first and inst == 0:
                        pe.wait_ge(S("par_ev"), 4)
                        pe.wait_ge(S("p_ev"), 1)
                        pe.wait_ge(S("ext_ev"), 1)
                    if j >= RING:
                        pe.wait_ge(S("gu"), lin(i, 3, FT * inst + j - RING + 1))
                    out = ring1(j)
                    by_columns(i, c, [out[:, 0, :], out[:, 1, :]], AHI1, ALO1, TX,
                               ready=wait_k("act_lo", 3 * KT * inst) if first else None)
                    if i is None and j == 0:
                        pe.wait_ge(S("c_ev"), 4)
                        norm_sums(pre, 2, SQ1)
                        pe.wait_ge(S("sc"), 2)
                    if i is None and j == 1:
                        norm_rows(pre, 2)
                    modulation(inst, i, j)
                steps(pe, f + "_gu", gate_up)
                down(f + "_dn", inst, SHI1, SLO1, TX)
                norm_sums(post, 2, SQ1)
                norm_rows(post, 2)
                if inst == 1:
                    break

                def project(i, j, c):
                    if j >= RING:
                        pe.wait_ge(S("zt"), lin(i, 6, 2 * (j - RING) + 1))
                    out = ring1(j)
                    by_columns(i, c, [out[:, 0, :], out[:, 1, :]], AHI1, ALO1, TX,
                               ready=wait_k("act_lo", KT) if i is None and j == 0 else None)
                    if i is None and j == 0:
                        norm_sums(2, 2, SQ1)
                    if i is None and j == 1:
                        norm_rows(2, 2)
                steps(pe, "b1_in", project)

                pe.wait_ge(S("zt"), 18)
                for b in range(3):
                    for a in range(4 * b, min(4 * b + 4, 10)):
                        tile = 5 if a < 2 else 13 + a // 2
                        last = pe.transpose(PS[:, b, a % 4 * P:a % 4 * P + P], Z[:, tile, a % 2 * P:a % 2 * P + P], IDENT[:, :])
                    last.then_inc(S("vt_tr"), 1)

                def scores(g):
                    if g:
                        pe.wait_ge(S("a_sb"), 3 * g)
                    else:
                        pe.wait_ge(S("vt_ev"), 3)
                    for hl in (0, 2, 1, 3):
                        h = 4 * g + hl
                        p0 = 64 * (h % 2)
                        if hl == 1:
                            pe.wait_ge(S("a_even"), g + 1)
                        if h < 8:
                            q = Z[p0:p0 + 64, h // 2, :]
                            k = Z[p0:p0 + 64, 4, :] if h // 4 == h % 2 else KS[p0:p0 + 64, :]
                        else:
                            q, k = Z[p0:p0 + 64, 6 + (h - 8) // 2, :], Z[p0:p0 + 64, 10 + (h - 8) // 2, :]
                        pe.matmul(PS[:, hl % 2, hl // 2 * TX:hl // 2 * TX + TX], q[:, P:TX], k[:, :], start=True, stop=True)
                        last = pe.matmul(PS[:, 2, hl * P:hl * P + P], q[:, 0:P], k[:, 0:P], start=True, stop=True)
                        if hl == 2:
                            last.then_inc(S("a_even"), 1)
                    last.then_inc(S("a_s"), 1)

                pe.wait_ge(S("ks"), 32)
                scores(0)
                for g in range(4):
                    s = g % 2
                    if g < 3:
                        scores(g + 1)
                    pe.wait_ge(S("a_p"), 2 * g + 2)
                    if g:
                        pe.wait_ge(S("a_pt"), g)
                    for hl in range(4):
                        for src, col in ((SB0[s][:, hl, :], 0), (SB1[s][:, hl, 0:P], P), (SB1[s][:, hl, P:TX], 2 * P)):
                            last = pe.transpose(PS[:, 3 + hl, col:col + P], src, IDENT[:, :])
                    last.then_inc(S("a_tr"), 1)
                    pe.wait_ge(S("a_pt"), g + 1)
                    if g:
                        pe.wait_ge(S("act_lo"), 2 * KT + 2 * g)
                    for hl in range(4):
                        h = 4 * g + hl
                        p0 = 64 * (h % 2)
                        v, c0 = (0, 64 * g) if h < 8 else (2 + 2 * ((h - 8) // 2), p0)
                        out = PS[p0:p0 + 64, 7, hl // 2 * TX:hl // 2 * TX + TX]
                        pe.matmul(out, VT1[:, v, c0:c0 + 64], PT1[s][:, hl, 0:TX], start=True, stop=False)
                        last = pe.matmul(out[:, P:TX], VT1[:, v + 1, c0:c0 + 64], PT1[s][:, hl, TX:3 * P], start=False, stop=True)
                    last.then_inc(S("a_pv"), 1)

                for j in range(4):
                    if j >= RING:
                        pe.wait_ge(S("f_ev"), j - RING + 1)
                    out = ring1(j)
                    by_columns(None, FIRST["b1_out"] + j, [out[:, 0, :], out[:, 1, :]], AHI1, ALO1, TX,
                               ready=wait_k("act_lo", 2 * KT) if j == 0 else None)
                norm_sums(3, 2, SQ1)
                norm_rows(3, 2)

            for j in range(4):
                if j >= RING:
                    pe.wait_ge(S("pg"), j - RING + 1)
                out = ring1(j)
                by_columns(None, FIRST["ple_gate"] + j, [out[:, 0, :], out[:, 1, :]], AHI1, ALO1, TX,
                           ready=wait_k("act_lo", 4 * KT) if j == 0 else None)
                if j == 0:
                    norm_sums(6, 2, SQ1)
                if j == 1:
                    norm_rows(6, 2)
            pe.wait_ge(S("p_lo"), 1)
            by_columns(None, FIRST["ple_proj"], [acc(m, TX) for m in range(KT)], PHI, PLO, TX, k_tiles=2, width=D)
            norm_sums(7, 2, SQ1)
            norm_rows(7, 2)

            for layer in range(2):
                nt = TB if layer == 0 else TX
                pe.wait_ge(S(f"tables{layer}"), 160)
                for l in range(3):
                    if l:
                        pe.wait_ge(S("f_h"), 3 * layer + l)
                    pe.matmul(PS[0:FH, 4, 0:TX], FW[l][:, :], ZF[:, :] if l == 0 else HA[:, l - 1, :], start=True, stop=True)\
                      .then_inc(S("f_mm"), 1)
                pe.wait_ge(S("f_h"), 3 * layer + 3)
                for t in range(2):
                    for r in range(2):
                        last = pe.matmul(PS[:, 2 * t + r, :], HA[:, 2, t * P:t * P + P], FW4[:, r * HW:r * HW + HW],
                                         start=True, stop=True)
                last.then_inc(S("f_taps"), 1)
                pe.wait_ge(S("f_dec"), 4 * (layer + 1))
                for ct in range(CTILES):
                    for r in range(2):
                        for t in range(2):
                            last = pe.matmul(PS[:, 4 + ct, :], DFT[:, r, t, ct * P:ct * P + P], HF[:, t, r, :],
                                             start=r + t == 0, stop=r + t == 2)
                last.then_inc(S("f_k"), 1)
                pe.wait_ge(S("f_fix"), 2 * layer + 2)

                norm_sums(8 + 2 * layer, 4, SQ2)
                norm_rows(8 + 2 * layer, 4)
                for q in range(6):
                    n = TB if layer == 0 or q >= 4 else TX
                    if q >= RING:
                        pe.wait_ge(S("qkv_ev"), 6 * layer + q - RING + 1)
                    out = ring2(q, n)
                    by_columns(None, FIRST[f"qkv{layer}"] + q, [out[:, 0, :], out[:, 1, :]], AHI2, ALO2, n,
                               ready=wait_k("act_lo", KT * (5 + 2 * layer)) if q == 0 else None)
                pe.wait_ge(S("qkv_ev"), 6 * layer + 6)
                for a in range(8):
                    last = pe.transpose(PS[:, 2 + a // 4, a % 4 * P:a % 4 * P + P], QKV[:, 10 + a % 2, a // 2 * P:a // 2 * P + P],
                                        IDENT[:, :])
                last.then_inc(S("v_tr"), 1)
                tq = nt // P
                for j in range(10):
                    cols = [j * tq + t for t in range(tq)] if j < 8 else [32 + 4 * (j - 8) + t for t in range(4)]
                    pe.wait_ge(S("h_sq"), 10 * layer + j + 1)
                    for t, col in enumerate(cols):
                        last = pe.matmul(PS[:, 6, col:col + 1], HSQ[:, j % 4, t * P:t * P + P], ONES[:, 0:1], start=True, stop=True)
                    last.then_inc(S("h_ss"), 1)
                    pe.wait_ge(S("h_gain"), 10 * layer + j + 1)
                    if j >= 2:
                        pe.wait_ge(S("h_sin"), 10 * layer + j - 1)
                    pe.matmul(PS[:, j % 2, 0:TX], ROT[:, :], QKV[:, j, 0:TX], start=True, stop=True).then_inc(S("h_rot"), 1)
                for kv in range(2):
                    pe.wait_ge(S("h_dg"), 2 * layer + kv + 1)
                    for t in range(4):
                        last = pe.matmul(PS[:, 5 + 2 * kv, t * P:t * P + P], ONES[:, :], DGK[:, kv, t, :], start=True, stop=True)
                    last.then_inc(S("h_rb"), 1)

                units = [(0, h) for h in range(NH2)] + ([(1, h) for h in range(NH2)] if layer == 0 else [])
                u0 = 2 * NH2 * layer

                def scores2(u):
                    grp, h = units[u]
                    if u >= 2:
                        pe.wait_ge(S("b_ex"), 2 * (u0 + u - 1))
                    for t in range(2):
                        q = QKV[:, h, TX * grp + t * P:TX * grp + t * P + P]
                        if grp == 0:
                            last = pe.matmul(PS[:, 2 * (u % 2) + t, :], q, QKV[:, 8 + h // 4, :], start=True, stop=True)
                        else:
                            last = pe.matmul(PS[:, 2 * (u % 2), TX * t:TX * t + TX], q, QKV[:, 8 + h // 4, TX:TB], start=True, stop=True)
                    last.then_inc(S("b_s"), 1)

                def values(u):
                    grp, h = units[u]
                    pe.wait_ge(S("b_pt"), u0 + u + 1)
                    if u >= 2:
                        pe.wait_ge(S("b_o"), u0 + u - 1)
                    kts = range(4) if grp == 0 else range(2, 4)
                    for a, kt in enumerate(kts):
                        last = pe.matmul(PS[:, 6 + u % 2, 0:TX], VT2[:, 2 * kt + h // 4, :], PT2[:, u % 2, a, :],
                                         start=a == 0, stop=a == len(kts) - 1)
                    last.then_inc(S("b_pv"), 1)

                pe.wait_ge(S("v_ev"), layer + 1)
                pe.wait_ge(S("h_key"), 2 * layer + 2)
                scores2(0)
                for u, (grp, h) in enumerate(units):
                    if u + 1 < len(units):
                        scores2(u + 1)
                    if u:
                        values(u - 1)
                    pe.wait_ge(S("b_p"), 2 * (u0 + u) + 2)
                    for a in range(4 if grp == 0 else 2):
                        for t in range(2):
                            last = pe.transpose(PS[:, 4 + a // 2, a % 2 * TX + t * P:a % 2 * TX + t * P + P],
                                                PB[:, u % 2, t, a * P:a * P + P], IDENT[:, :])
                    last.then_inc(S("b_tr"), 1)
                values(len(units) - 1)

                for q in range(6):
                    if q >= RING:
                        pe.wait_ge(S("hy_taps"), 24 * layer + 4 * (q - RING + 1))
                    out = ring2(q, nt)
                    by_columns(None, FIRST[f"hy{layer}"] + q, [out[:, 0, :], out[:, 1, :]], AHI2, ALO2, nt)
                groups = nt // TX

                def turned(grp):
                    pe.wait_ge(S("hy_v"), HT * (layer + 1))
                    pe.wait_ge(S("hy_taps"), 24 * (layer + 1))
                    if grp:
                        pe.wait_ge(S("y_vt"), 2 * layer + grp)
                    for t in range(2):
                        for m in range(HT):
                            last = pe.transpose(PS[:, t, m * P:m * P + P], HY[:, 8 + m, TX * grp + t * P:TX * grp + t * P + P],
                                                IDENT[:, :])
                    last.then_inc(S("y_tr"), 1)

                def forward(grp):
                    y = 2 * layer + grp
                    pe.wait_ge(S("y_vt"), y + 1)
                    if grp:
                        pe.wait_ge(S("y_mul"), 7 * y)
                    for ct in range(CTILES):
                        for t in range(2):
                            last = pe.matmul(PS[:, 2 + ct, :], DFT[:, 0, t, ct * P:ct * P + P], VTT[:, t, :], start=t == 0, stop=t == 1)
                    last.then_inc(S("y_fwd"), 1)

                def inverse(grp):
                    y = 2 * layer + grp
                    pe.wait_ge(S("y_mul"), 7 * y + 7)
                    if grp:
                        pe.wait_ge(S("y_h"), 8 * y)
                    for m in range(HT):
                        for ct in range(CTILES):
                            last = pe.matmul(PS[:, 6 + m // 2, m % 2 * TX:m % 2 * TX + TX], YS[:, ct, m * P:m * P + P], IDFT[:, ct, :],
                                             start=ct == 0, stop=ct == CTILES - 1)
                    last.then_inc(S("y_inv"), 1)

                turned(0)
                forward(0)
                if groups == 2:
                    turned(1)
                inverse(0)
                if groups == 2:
                    forward(1)
                    inverse(1)

                for j in range(2):
                    if j == 0:
                        pe.wait_ge(S("y_h"), 8 * (2 if layer == 0 else 3))
                    outs = [PS[:, 4 * j + t, 0:nt] for t in range(4)]
                    by_columns(None, FIRST[f"oh{layer}"] + j, outs, HHI, HLO, nt, k_tiles=HT, width=4 * P,
                               ready=wait_k("hh_lo", HT * layer) if j == 0 else None)

                def mix(i, m):
                    c = FIRST[f"mix{layer}"] + 3 * m
                    for g, (hi, lo) in enumerate(((AHI2, ALO2), (AHI2, ALO2), (A2HI, A2LO))):
                        if m == 0:
                            if g == 0:
                                pe.wait_ge(S("oh_ev"), 2 * (layer + 1))
                            if g == 2:
                                pe.wait_ge(S("a2_lo"), KT * (layer + 1))
                        elif g < 2:
                            pe.wait_ge(S("gate"), lin(i, 2, 8 * layer + 2 * (m - 1) + g + 1))
                        else:
                            pe.wait_ge(S("merge"), lin(i, 3, 12 * layer + 3 * (m - 1) + 2))
                        out = ring2(g, nt)
                        by_columns(i, c + g, [out[:, 0, :], out[:, 1, :]], hi, lo, nt)
                mix(None, 0)
                with pe.Fori(0, 3) as i:
                    mix(i, 1)
                pe.wait_ge(S("merge"), 12 * (layer + 1))
                for j in range(4):
                    if j >= RING:
                        pe.wait_ge(S("xo"), 2 * KT * layer + 2 * (nt // TX))
                    out = ring2(j, nt)
                    by_columns(None, FIRST[f"out{layer}"] + j, [out[:, 0, :], out[:, 1, :]], AHI2, ALO2, nt,
                               ready=wait_k("mg_lo", KT * layer) if j == 0 else None)
                norm_sums(9 + 2 * layer, nt // P, SQ2)
                norm_rows(9 + 2 * layer, nt // P)
                inst = 2 + layer

                def gate_up2(i, j, c):
                    if j >= RING:
                        pe.wait_ge(S("h"), lin(i, 3, FT * inst + j - RING + 1))
                    out = ring2(j, nt)
                    by_columns(i, c, [out[:, 0, :], out[:, 1, :]], AHI2, ALO2, nt,
                               ready=wait_k("act_lo", KT * (6 + 2 * layer)) if i is None and j == 0 else None)
                steps(pe, f"gu{layer}", gate_up2)
                pe.wait_ge(S("h"), FT * (inst + 1))
                down(f"dn{layer}", inst, SHI2, SLO2, nt)

            pe.wait_ge(S("xd"), 3 * KT)
            norm_sums(12, 2, SQ1)
            norm_rows(12, 2)
            for t in range(2):
                for a in range(2):
                    for k in range(4 * a, 4 * a + 4):
                        pe.wait_ge(S("yf"), k + 1)
                        last = pe.transpose(PS[:, 2 * t + a, k % 4 * P:k % 4 * P + P], YF[:, k, t * P:t * P + P], IDENT[:, :])
                    last.then_inc(S("out_tr"), 1)


_NAMES = ["x", "p", "rel_bias", "ffn1_pre_g", "ffn1_w_gu", "ffn1_w_down", "ffn1_post_g", "attn_pre_g", "w_in", "b_in",
          "sinks", "w_out", "b_out", "attn_post_g", "ffn2_pre_g", "ffn2_w_gu", "ffn2_w_down", "ffn2_post_g",
          "ple_pre_g", "w_ple_gate", "w_ple_proj", "ple_post_g", "c_2", "ctx_2", "c_ctx_2", "w_mod_2", "b_mod_2",
          "norm_mix_2", "w_in_2", "q_norm_2", "k_norm_2", "conv_w_2", "conv_b_2", "filt_w1_2", "filt_b1_2",
          "filt_w2_2", "filt_b2_2", "filt_w3_2", "filt_b3_2", "filt_w4_2", "filt_freq_2", "hyena_bias_2",
          "w_o_attn_2", "w_o_hyena_2", "w_out_2", "norm_ffn_2", "w_gate_up_2", "w_down_2", "norm_final_2"]


def kernel(**inputs):
    import concourse.bacc as bacc
    from concourse.bass_utils import run_bass_kernel_spmd

    nc = bacc.Bacc("TRN2", target_bir_lowering=False, num_devices=1)
    tensors = {n: np.ascontiguousarray(inputs[n]) for n in _NAMES}
    tensors.update({f"{n}": a for n, a in shape_tables().items()})
    arrays, aps = {}, {}
    for name, a in tensors.items():
        arrays[f"in_{name}_dram"] = a
        aps[name] = nc.dram_tensor(f"in_{name}_dram", a.shape, mybir.dt.from_np(a.dtype), kind="ExternalInput").ap()
    aps["out"] = nc.dram_tensor("out_0_dram", (1, TX, D), F32, kind="ExternalOutput").ap()
    two_blocks_kernel(nc, aps)
    r = run_bass_kernel_spmd(nc, [arrays], core_ids=[0])
    return r.results[0]["out_0_dram"]
```

```python
from contextlib import ExitStack

import numpy as np

import concourse.bass as bass
from concourse import mybir

F32 = mybir.dt.float32
F32R = mybir.dt.float32r
ALU = mybir.AluOpType
ACT = mybir.ActivationFunctionType
AX = mybir.AxisListType

P = 128
D = 1024
KT = D // P
TX = 256
TB = 2 * TX
DFF = 2816
FT = DFF // P
EPS = 1e-6
CH = 2048
RING = 3
AHEAD = 2
DH1 = 64
NBKT = 32
DH2 = 128
NH2 = 8
HW = 512
HT = HW // P
FH = 64
FE = 33
CTILES = TB // P
MAGIC = 12582912.0
TWO_PI_HI = 6.28125
TWO_PI_LO = 2.0 * np.pi - 6.28125
PI_IN = 3.1415925



def t5_buckets(n):
    d = np.arange(n)
    nf = np.maximum(d, 1).astype(np.float32)
    exact = NBKT // 2
    large = exact + (np.log(nf / np.float32(exact)) / np.float32(np.log(2048 / exact)) * np.float32(NBKT - exact)).astype(np.int32)
    return np.where(d < exact, d, np.minimum(large, NBKT - 1))


def shape_tables():
    t = {}
    t["ident"] = np.eye(P, dtype=np.float32)
    dist = np.arange(384) - 127
    bucket = t5_buckets(TX)
    onehot = np.zeros((NBKT, 384), np.float32)
    mask = np.full((16, 384), -1e30, np.float32)
    for i, d in enumerate(dist):
        if d < 0 or d >= TX:
            continue
        onehot[bucket[d], i] = 1.0
        if d <= 127:
            mask[:8, i] = 0.0
        count = int(d <= 128) + int(d % 4 == 0) + int(d % 16 == 0)
        if count:
            mask[8:, i] = np.log(count)
    t["onehot"], t["mask"] = onehot, mask
    row = np.repeat(np.arange(TX // 64, dtype=np.float32), 64)
    col = np.tile(np.arange(64, dtype=np.float32), TX // 64)
    inv = (np.float32(10000.0) ** (-np.arange(0, 64, 2, dtype=np.float32) / np.float32(64))).astype(np.float32)
    ang = np.concatenate([row[:, None] * inv, col[:, None] * inv], axis=-1)
    cs = np.stack([np.repeat(np.cos(ang), 2, axis=1).T, np.repeat(np.sin(ang), 2, axis=1).T], axis=1)
    t["rope"] = np.ascontiguousarray(cs.astype(np.float32))
    rot = np.zeros((P, P), np.float32)
    for i in range(0, P, 2):
        rot[i + 1, i] = -1.0
        rot[i, i + 1] = 1.0
    t["rot"] = rot
    lin = np.linspace(0.0, 1.0, TX, dtype=np.float32)[:, None]
    w = np.float32(2.0 * np.pi / TX) * np.arange(TX, dtype=np.float32)[:, None]
    f = np.linspace(1e-4, 15, 16, dtype=np.float32)[None, :]
    t["zfeat"] = np.ascontiguousarray(np.concatenate([lin, np.cos(f * w), -np.sin(f * w)], axis=-1).T.astype(np.float32))
    lo_, hi_ = np.log(1e-2) / 1.5, np.log(1e-2) / 0.3
    deltas = np.abs(np.linspace(lo_, hi_, HW, dtype=np.float32))
    t["decay"] = np.exp(-lin * deltas).astype(np.float32)
    n, k = np.arange(TX)[:, None].astype(np.float64), np.arange(TX)[None, :].astype(np.float64)
    ph = 2 * np.pi * n * k / TB
    alt = (-1.0) ** n
    fwd = np.concatenate([np.cos(ph), alt, -np.sin(ph)[:, 1:]], axis=1)
    bwd = np.concatenate([np.cos(ph), alt, np.sin(ph)[:, 1:]], axis=1)
    bwd[0] = 0.0
    scale = np.full((TX, 1), 2.0 / TB)
    scale[0] = 1.0 / TB
    im = -np.sin(ph).T * (2.0 / TB)
    im[0] = alt[:, 0] / TB
    t["dft"] = np.stack([fwd, bwd]).astype(np.float32)
    t["idft"] = np.concatenate([np.cos(ph).T * scale, im], axis=0).astype(np.float32)
    return t



def param_rows():
    tiles = [
        [("ffn1_pre_g", 8), ("ffn1_post_g", 8), ("attn_pre_g", 8), ("attn_post_g", 8), ("ffn2_pre_g", 8),
         ("ffn2_post_g", 8), ("ple_pre_g", 8), ("ple_post_g", 8), ("b_out", 8), ("b_in", 18),
         ("norm_mix_2", 16), ("norm_final_2", 8), ("q_norm_2", 2), ("k_norm_2", 2)],
        [("b_mod_2", 96), ("norm_ffn_2", 16), ("hyena_bias_2", 8)],
        [("conv_w_2", 72), ("conv_b_2", 24), ("c_2", 8), ("c_ctx_2", 8)],
        [("filt_b1_2", 2), ("filt_b2_2", 2), ("filt_b3_2", 2), ("filt_freq_2", 6)],
    ]
    at, used = {}, []
    for g, names in enumerate(tiles):
        row = 0
        for name, rows in names:
            at[name] = (g, row, rows)
            row += rows
        used.append(row)
    return at, used


PAR_AT, PAR_USED = param_rows()


STAGES = [("ffn1_gu", FT), ("ffn1_dn", FT // 2), ("b1_in", 9), ("b1_out", 4),
          ("ffn2_gu", FT), ("ffn2_dn", FT // 2), ("ple_gate", 4), ("ple_proj", 1)]
for _l in range(2):
    STAGES += [(f"qkv{_l}", 6), (f"hy{_l}", 6), (f"oh{_l}", 2), (f"mix{_l}", 12), (f"out{_l}", 4),
               (f"gu{_l}", FT), (f"dn{_l}", FT // 2)]
FIRST, TOTAL = {}, 0
for _name, _n in STAGES:
    FIRST[_name] = TOTAL
    TOTAL += _n
CHUNKS = dict(STAGES)
STAT_BANK = [0, 4, 0, 0, 0, 4, 0, 4, 6, 6, 0, 6, 6]
MODC = 24


def lin(i, step, const):
    return const if i is None else i * step + const


def steps(eng, stage, body, tail=0):
    n, c0 = CHUNKS[stage], FIRST[stage]
    head = 3 + (n - 3 - tail) % 3
    turns = (n - head - tail) // 3
    if turns < 2:
        head, turns, tail = n, 0, 0
    for j in range(head):
        body(None, j, c0 + j)
    if turns:
        with eng.Fori(0, turns) as i:
            for u in range(3):
                body(i, head + u, c0 + head + u)
    for j in range(n - tail, n):
        body(None, j, c0 + j)


def two_blocks_kernel(nc, d):
    with ExitStack() as ctx:
        sems = {}

        def S(name):
            if name not in sems:
                sems[name] = ctx.enter_context(nc.semaphore(name))
            return sems[name]

        K = 1024
        slab = 207 * K + 768
        nc.alloc_sbuf_tensor("slab", [P, slab // 4], F32)
        base = nc.sbuf_base - slab

        def at(name, shape, off, dt=F32):
            assert off + 4 * int(np.prod(shape[1:])) <= slab, name
            return nc.alloc_sbuf_tensor_at(name, shape, dt, offset=base + off)

        X = at("X", [P, KT, TB], 0)
        RAW = at("RAW", [P, RING, CH], 16 * K)
        WHI = at("WHI", [P, RING, CH], 40 * K, F32R)
        WLO = at("WLO", [P, RING, CH], 64 * K, F32R)
        AHI1, ALO1 = at("AHI1", [P, KT, TX], 88 * K, F32R), at("ALO1", [P, KT, TX], 104 * K, F32R)
        AHI2, ALO2 = at("AHI2", [P, KT, TB], 88 * K, F32R), at("ALO2", [P, KT, TB], 104 * K, F32R)
        BIAS = [at("BIAS0", [P, 8, TX], 96 * K), at("BIAS1", [P, 8, TX], 112 * K)]
        SHI1, SLO1 = at("SHI1", [P, RING, 2, TX], 120 * K, F32R), at("SLO1", [P, RING, 2, TX], 132 * K, F32R)
        SHI2, SLO2 = at("SHI2", [P, RING, 2, TB], 120 * K, F32R), at("SLO2", [P, RING, 2, TB], 132 * K, F32R)
        REL, ONEHOT = at("REL", [NBKT, 16], 126 * K), at("ONEHOT", [NBKT, 384], 127 * K)
        MASK, EXT = at("MASK", [16, 384], 138 * K), at("EXT", [16, 384], 140 * K)
        PHI, PLO = at("PHI", [P, 2, TX], 130 * K, F32R), at("PLO", [P, 2, TX], 142 * K, F32R)
        DFT = at("DFT", [P, 2, 2, TB], 120 * K)
        IDFT = at("IDFT", [P, CTILES, TX], 128 * K)
        KR = at("KR", [P, 2, HW], 132 * K)
        KIZ = at("KIZ", [P, 2, HW], 136 * K)
        KRX = at("KRX", [P, HW], 140 * K)
        ROT = at("ROT", [P, P], 142 * K)
        HHI, HLO = at("HHI", [P, HT, TB], 120 * K, F32R), at("HLO", [P, HT, TB], 132 * K, F32R)
        A = 144 * K
        XS, CS, PST = at("XS", [P, 2, D], A), at("CS", [P, 2, D], A + 8 * K), at("PST", [P, 2, TX], A + 16 * K)
        GS = at("GS", [P, 4, P], A + 18 * K)
        HB1, HB2 = at("HB1", [P, FT, TX], A), at("HB2", [P, FT, TB], A)
        MRAW, MLO = at("MRAW", [P, RING, CH // 2], A + 24 * K), at("MLO", [P, RING, CH // 2], A + 24 * K, F32R)
        MHI = at("MHI", [P, RING, CH // 2], A + 36 * K, F32R)
        MROW = at("MROW", [4, 2 * P], 129 * K)
        SQ1, SQ2 = at("SQ1", [P, KT, TX], A), at("SQ2", [P, KT, TB], A)
        FB, TU = at("FB", [P, KT, TX], A + 8 * K), at("TU", [P, KT, TX], A + 16 * K)
        PG = at("PG", [P, KT, TX], A + 16 * K)
        Z = at("Z", [P, 18, TX], A)
        VT1 = at("VT1", [P, 10, P], A + 18 * K)
        KS = at("KS", [P, TX], A + 23 * K)
        SB1 = [at(f"SB1{i}", [P, 4, TX], A + (24 + 6 * i) * K) for i in range(2)]
        SB0 = [at(f"SB0{i}", [P, 4, P], A + (28 + 6 * i) * K) for i in range(2)]
        PT1 = [at(f"PT1{i}", [P, 4, 3 * P], A + (36 + 6 * i) * K) for i in range(2)]
        QKV = at("QKV", [P, 12, TB], A)
        VT2 = at("VT2", [P, 8, P], A + 24 * K)
        HSQ = at("HSQ", [P, 2, TB], 192 * K)
        PB = at("PB", [P, 2, 2, TB], A + 28 * K)
        PT2 = at("PT2", [P, 2, 4, TX], A + 36 * K)
        BR = at("BR", [P, 2, TX], 196 * K)
        ROPE = at("ROPE", [P, 2, TX], 198 * K)
        FW4, DEC = at("FW4", [FH, 2 * HW], A + 36 * K), at("DEC", [P, 2, HW], A + 32 * K)
        HF = at("HF", [P, 2, 2, HW], A + 40 * K)
        ZF = at("ZF", [FE, TX], 192 * K)
        FW = [at(f"FW{i}", [FE if i == 0 else FH, FH], 193 * K + 256 * i) for i in range(3)]
        FU = at("FU", [FH, 4, TX], A + 24 * K)
        HA = at("HA", [FH, 3, TX], A + 28 * K)
        HY = at("HY", [P, 12, TB], A + 24 * K)
        YS = at("YS", [P, CTILES, HW], A + 32 * K)
        VTT = at("VTT", [P, 2, HW], 124 * K)
        YT2 = at("YT2", [P, 2, HW], 196 * K)
        A2HI, A2LO = at("A2HI", [P, KT, TB], A + 16 * K, F32R), at("A2LO", [P, KT, TB], A + 32 * K, F32R)
        MG = at("MG", [P, KT, TB], A)
        YF, OUTS = at("YF", [P, KT, TX], A + 16 * K), at("OUTS", [P, 2, D], A + 24 * K)
        GU = at("GU", [P, RING, 2, TX], 192 * K)
        SIL = at("SIL", [P, RING, TB], 192 * K)
        SG = at("SG", [P, 2, 2, TB], 192 * K)
        YT1 = at("YT1", [P, 2, HW], 192 * K)
        P32 = at("P32", [P, 2, TX], 198 * K)
        RT = at("RT", [P, TB], 200 * K)
        PAR = at("PAR", [P, 4, P], 202 * K)
        IDENT, ONES = at("IDENT", [P, P], 204 * K), at("ONES", [P, P], 204 * K + 512)
        small = [205 * K]

        def sm(name, shape):
            t = at(name, shape, small[0])
            small[0] += (4 * int(np.prod(shape[1:])) + 31) // 32 * 32
            return t

        MOD = sm("MOD", [P, 2, 48, 2])
        GM = sm("GM", [P, 2, 2, 8, 2])
        HG = sm("HG", [P, 2, 8])
        SC = sm("SC", [P, 8, 2])
        SCR = at("SCR", [P, 8, 4], small[0], F32R)
        small[0] += 128
        MSUM = sm("MSUM", [P, 48, 4])
        STD, RC = sm("STD", [P, 40]), sm("RC", [P, 40])
        NM, SMX, RS = sm("NM", [P, 2, 8]), sm("SMX", [P, 2, 8]), sm("RS", [P, 2, 8])
        SINK, SE = sm("SINK", [P, 2, 8]), sm("SE", [P, 2, 8])
        EPSC = sm("EPSC", [P, 2])

        PS = ctx.enter_context(nc.psum_tensor("PS", [P, 8, 512], F32))
        bias_rows = nc.dram_tensor("bias_rows", (16, 384), F32).ap()

        def par(name, first=0, n=1):
            g, row, rows = PAR_AT[name]
            return PAR[:, g, row + first:row + first + n]

        def over_tokens(ap, n):
            return ap.unsqueeze(2).broadcast_to([P, ap.shape[1], n])

        def over_tiles(ap, n):
            return ap.unsqueeze(1).broadcast_to([P, n, ap.shape[1]])

        def ring1(j):
            return PS[:, 4 + j % 3, :].rearrange("p (t n) -> p t n", t=2)

        def ring2(j, n):
            s = 2 * (j % 3)
            return PS[:, s:s + 2, :] if n == TB else PS[:, s, :].rearrange("p (t n) -> p t n", t=2)

        def acc(m, n):
            return PS[:, m, :] if n == TB else PS[:, m // 2, m % 2 * TX:m % 2 * TX + TX]

        def stat_row(n_norm, t):
            return PS[:, STAT_BANK[n_norm], 0:P * t]

        block = ctx.enter_context(nc.Block())

        @block.sync
        def _(sp):
            def load(i, c, src, dst, half=lambda ap, t: ap[:, t * (ap.shape[1] // 2):(t + 1) * (ap.shape[1] // 2), :]):
                if c >= RING:
                    sp.wait_ge(S("lo_done"), lin(i, 3, c - RING + 1))
                for t in range(2):
                    sp.dma_start(half(dst(RAW[:, c % RING, :]), t), half(src, t)).then_inc(S(f"raw{c % RING}"), 16)

            def cols(w, n_first, k=KT, width=2 * P):
                return w.rearrange("(k p) n -> p k n", p=P)[:, :, bass.ds(n_first, width)]

            def by_k(k):
                return lambda r: r.rearrange("p (k n) -> p k n", k=k)

            def mod_load(layer, i, half):
                if half < 0:
                    return
                t = 2 * MODC * layer + half
                if t >= RING:
                    if half == 0:
                        sp.wait_ge(S("act_lo"), 3 * KT)
                    sp.wait_ge(S("mod_used"), lin(i, 6, t - RING + 1))
                k = 4 * (half % 2)
                src = cols(d["w_mod_2"][layer], lin(i, 3 * 2 * P, half // 2 * 2 * P))[:, k:k + 4, :]
                sp.dma_start(MRAW[:, t % RING, :].rearrange("p (k n) -> p k n", k=4), src)\
                  .then_inc(S(f"mod_raw{t % RING}"), 16)

            def gate_up(stage, w, layer=None):
                view = w.rearrange("(k p) (t n) -> p k t n", p=P, t=2)

                def body(i, j, c):
                    load(i, c, view[:, :, :, bass.ds(lin(i, 3 * P, j * P), P)],
                         lambda r: r.rearrange("p (k t n) -> p k t n", k=KT, t=2), lambda ap, t: ap[:, :, t, :])
                    if layer is not None:
                        mod_load(layer, i, 2 * j - 3)
                        mod_load(layer, i, 2 * j - 2)
                steps(sp, stage, body)

            def down(stage, w, layer=None):
                view = w.rearrange("(k p) n -> p k n", p=P)

                def body(i, j, c):
                    load(i, c, view[:, bass.ds(lin(i, 6, 2 * j), 2), :], by_k(2))
                    if layer is not None and i is None and j < 3:
                        for half in range(2 * (FT + j) - 3, 2 * (FT + j) - 1 if j < 2 else 2 * MODC):
                            mod_load(layer, None, half)
                steps(sp, stage, body, tail=2)

            def plain(stage, w, first=0):
                steps(sp, stage, lambda i, j, c: load(i, c, cols(w, lin(i, 6 * P, first + 2 * P * j)), by_k(KT)))

            sp.dma_start(IDENT[:, :], d["ident"]).then_inc(S("in_ident"), 16)
            sp.dma_start(XS[:, :, :], d["x"][0].rearrange("(t p) n -> p t n", p=P)).then_inc(S("in_x"), 16)
            gate_up("ffn1_gu", d["ffn1_w_gu"][0], 0)
            down("ffn1_dn", d["ffn1_w_down"][0], 0)
            plain("b1_in", d["w_in"][0])
            plain("b1_out", d["w_out"][0])
            gate_up("ffn2_gu", d["ffn2_w_gu"][0], 1)
            down("ffn2_dn", d["ffn2_w_down"][0], 1)
            plain("ple_gate", d["w_ple_gate"][0])
            load(None, FIRST["ple_proj"], d["w_ple_proj"][0].rearrange("(k p) n -> p k n", p=P), by_k(2))
            for layer in range(2):
                win = d["w_in_2"][layer]
                plain(f"qkv{layer}", win)
                plain(f"hy{layer}", win, 12 * P)
                woh = d["w_o_hyena_2"][layer].rearrange("(k p) n -> p k n", p=P)
                for j in range(2):
                    load(None, FIRST[f"oh{layer}"] + j, woh[:, :, 512 * j:512 * j + 512], by_k(HT))

                def mix(i, m):
                    c = FIRST[f"mix{layer}"] + 3 * m
                    n = lin(i, 2 * P, 2 * P * m)
                    load(i, c, cols(win, n + 32 * P), by_k(KT))
                    load(i, c + 1, cols(win, n + 24 * P), by_k(KT))
                    load(i, c + 2, cols(d["w_o_attn_2"][layer], n), by_k(KT))
                mix(None, 0)
                with sp.Fori(0, 3) as i:
                    mix(i, 1)
                plain(f"out{layer}", d["w_out_2"][layer])
                gate_up(f"gu{layer}", d["w_gate_up_2"][layer])
                down(f"dn{layer}", d["w_down_2"][layer])
            for t in range(2):
                sp.wait_ge(S("out_ev0"), t + 1)
                sp.wait_ge(S("out_ev1"), t + 1)
                sp.dma_start(d["out"][0, P * t:P * t + P, :], OUTS[:, t, :]).then_inc(S("out_dma"), 16)
            sp.wait_ge(S("out_dma"), 32)

        @block.gpsimd
        def _(pool):
            pool.wait_ge(S("ext_ev"), 1)
            pool.dma_start(bias_rows, EXT[:, :]).then_inc(S("bias_out"), 16)
            pool.wait_ge(S("bias_out"), 16)
            for b in range(2):
                src = bass.AP(tensor=bias_rows.tensor, offset=8 * b * 384, ap=[[1, P], [384, 8], [1, TX]])
                pool.dma_start(BIAS[b][:, :, :], src).then_inc(S("bias_in"), 16)

            def x_update(u):
                for k in range(KT):
                    pool.wait_ge(S("xt"), KT * u + k + 1)
                    pool.tensor_tensor(X[:, k, 0:TX], X[:, k, 0:TX], TU[:, k, :], ALU.add).then_inc(S("xu"), 1)

            x_update(0)
            pool.wait_ge(S("zt"), 18)
            for h in range(2):
                pool.dma_start(KS[64 - 64 * h:128 - 64 * h, :], Z[64 * h:64 * h + 64, 4, :]).then_inc(S("ks"), 16)
            x_update(1)
            x_update(2)
            x_update(3)
            for layer in range(2):
                if layer == 0:
                    pool.wait_ge(S("xu"), 4 * KT)
                else:
                    pool.wait_ge(S("xd"), 2 * KT)
                pool.wait_ge(S("pe_done"), FIRST[f"qkv{layer}"])
                loads = [(FW[0][:, :], d["filt_w1_2"][layer]), (ZF[:, :], d["zfeat"]),
                         (FW[1][:, :], d["filt_w2_2"][layer]), (FW[2][:, :], d["filt_w3_2"][layer]),
                         (FW4[:, :], d["filt_w4_2"][layer]), (DEC[:, :, :], d["decay"].rearrange("(t p) n -> p t n", p=P)),
                         (DFT[:, :, :, :], d["dft"].rearrange("r (t p) n -> p r t n", p=P)),
                         (IDFT[:, :, :], d["idft"].rearrange("(t p) n -> p t n", p=P)),
                         (ROPE[:, :, :], d["rope"]), (ROT[:, :], d["rot"])]
                for dst, src in loads:
                    pool.dma_start(dst, src).then_inc(S(f"tables{layer}"), 16)
                pool.wait_ge(S(f"tables{layer}"), 160)
                for r, j in enumerate((8, 0, 2, 4, 6)):
                    pool.wait_ge(S("h_rot"), 5 * layer + r + 1)
                    pool.tensor_tensor(QKV[:, j:j + 2, 0:TX], QKV[:, j:j + 2, 0:TX], over_tiles(ROPE[:, 0, :], 2), ALU.mult)\
                        .then_inc(S("h_cos"), 1)
                n = TB if layer == 0 else TX
                for m in range(HT):
                    pool.wait_ge(S("hy_taps"), 24 * layer + 16 + 2 * m + 2)
                    pool.tensor_tensor(HY[:, 8 + m, 0:n], HY[:, 8 + m, 0:n], HY[:, 4 + m, 0:n], ALU.mult).then_inc(S("hy_v"), 1)

        @block.scalar
        def _(act):
            def split_w(i, c):
                if c >= TOTAL:
                    return
                act.wait_ge(S(f"raw{c % RING}"), lin(i, 32, 32 * (c // RING + 1)))
                if c >= RING:
                    act.wait_ge(S("pe_done"), lin(i, 3, c - RING + 1))
                act.activation(WHI[:, c % RING, :], RAW[:, c % RING, :], ACT.Copy).then_inc(S("hi_done"), 1)

            def split_h(i, inst, stage, j, hb, shi, n):
                act.wait_ge(S("h"), lin(i, 6, FT * inst + 2 * j + 2))
                if j >= RING:
                    act.wait_ge(S("pe_done"), lin(i, 3, FIRST[stage] + j - RING + 1))
                act.activation(shi[:, j % RING, :, 0:n], hb[:, bass.ds(lin(i, 6, 2 * j), 2), 0:n], ACT.Copy)\
                   .then_inc(S("hs_hi"), 1)

            def mod_hi(layer, i, half):
                if half >= 2 * MODC:
                    return
                t = 2 * MODC * layer + half
                act.wait_ge(S(f"mod_raw{t % RING}"), lin(i, 32, 16 * (t // RING + 1)))
                act.activation(MHI[:, t % RING, :], MRAW[:, t % RING, :], ACT.Copy).then_inc(S("mod_hi"), 1)

            def mod_cols(layer, i, g):
                act.wait_ge(S("mod_tr"), lin(i, 3, MODC * layer + g + 1))
                act.activation(MSUM[:, bass.ds(lin(i, 6, 2 * g), 2), :], PS[:, 7, 0:8].rearrange("p (t v) -> p t v", t=2),
                               ACT.Copy).then_inc(S("mod_col"), 1)

            def mod_rows(layer, i, g):
                act.wait_ge(S("mod_used"), lin(i, 6, 2 * (MODC * layer + g) + 2))
                act.activation(MROW[:, :], PS[0:4, 7, TX:TB], ACT.Copy).then_inc(S("mod_row"), 1)

            def down(stage, inst, hb, shi, n):
                split_h(None, inst, stage, 0, hb, shi, n)
                split_h(None, inst, stage, 1, hb, shi, n)

                def body(i, j, c):
                    split_w(i, c + AHEAD)
                    if i is not None or j + AHEAD < FT // 2:
                        split_h(i, inst, stage, j + AHEAD, hb, shi, n)
                    if inst < 2 and i is None and j <= MODC - FT:
                        mod_cols(inst, None, FT + j - 1)
                    if inst < 2 and i is None and j < MODC - FT:
                        g = FT + j
                        mod_hi(inst, None, 2 * g + 1)
                        mod_hi(inst, None, 2 * g + 2)
                        mod_rows(inst, None, g)
                steps(act, stage, body, tail=2)

            def norm_std(n_norm, t):
                act.wait_ge(S("n_ss"), n_norm + 1)
                act.activation(RT[:, 0:P * t], stat_row(n_norm, t), ACT.Sqrt, scale=1.0 / D, bias=EPSC[:, 0:1])\
                   .then_inc(S("n_std"), 1)

            def squares(src, dst, n_before, ready):
                for k in range(KT):
                    ready(k)
                    act.activation(dst(k), src(k), ACT.Square).then_inc(S("n_sq"), 1)

            def gained(name, ready):
                for k in range(KT):
                    ready(k)
                    act.activation(AHI1[:, k, :], X[:, k, 0:TX], ACT.Identity, scale=par(name, k)).then_inc(S("act_hi"), 1)
                    act.activation(SQ1[:, k, :], X[:, k, 0:TX], ACT.Square).then_inc(S("n_sq"), 1)

            def silus1(stage, inst):
                mod_hi(inst, None, 0)

                def body(i, j, c):
                    split_w(i, c + AHEAD)
                    if j:
                        mod_cols(inst, i, j - 1)
                    mod_hi(inst, i, 2 * j + 1)
                    mod_hi(inst, i, 2 * j + 2)
                    act.wait_ge(S("gu"), lin(i, 3, FT * inst + j + 1))
                    act.activation(GU[:, j % RING, 0, :], GU[:, j % RING, 0, :], ACT.Silu).then_inc(S("sil"), 1)
                    mod_rows(inst, i, j)
                steps(act, stage, body)

            for g, names in enumerate([[n for n in PAR_AT if PAR_AT[n][0] == g] for g in range(4)]):
                for name in names:
                    _, row, rows = PAR_AT[name]
                    width = FH if g == 3 else P
                    src = d[name]
                    dims = " ".join("abc"[:len(src.shape)])
                    flat = src.rearrange(f"{dims} -> ({dims})") if len(src.shape) > 1 else src
                    if g == 3:
                        act.wait_ge(S("gs_clear"), 1)
                    act.dma_start(GS[row:row + rows, g, 0:width], flat.rearrange("(r n) -> r n", n=width))\
                       .then_inc(S("in_par"), 16)
            act.dma_start(PST[:, :, :], d["p"][0, 0].rearrange("(t p) n -> p t n", p=P)).then_inc(S("in_p"), 16)
            for dst, src in ((REL[:, :], d["rel_bias"]), (ONEHOT[:, :], d["onehot"]), (MASK[:, :], d["mask"])):
                act.dma_start(dst, src).then_inc(S("in_bias"), 16)
            act.dma_start(SINK[:, 0, :], d["sinks"].broadcast_to([P, 8])).then_inc(S("in_sink"), 16)
            act.dma_start(CS[:, :, :], d["ctx_2"][0].rearrange("(t p) n -> p t n", p=P)).then_inc(S("in_ctx"), 16)

            for b in range(4):
                act.wait_ge(S("tr_x"), b + 1)
                act.activation(X[:, 2 * b:2 * b + 2, 0:TX], PS[:, b, :].rearrange("p (t n) -> p t n", t=2), ACT.Copy)\
                   .then_inc(S("x_ev"), 1)
            split_w(None, 0)
            act.wait_ge(S("par_ev"), 4)
            gained("ffn1_pre_g", lambda k: act.wait_ge(S("x_ev"), k // 2 + 1))
            for v, name in enumerate(("c_2", "c_ctx_2")):
                act.activation(SC[:, :, v], par(name, 0, 8), ACT.Silu).then_inc(S("sc"), 1)
            act.wait_ge(S("sc"), 2)
            act.activation(SCR[:, :, 0:2], SC[:, :, :], ACT.Copy).then_inc(S("sc_hi"), 1)
            split_w(None, 1)
            act.wait_ge(S("p_ev"), 1)
            act.activation(PHI[:, :, :], P32[:, :, :], ACT.Copy).then_inc(S("p_hi"), 1)

            for inst, (pre, post) in enumerate(((0, 1), (4, 5))):
                f = f"ffn{inst + 1}"
                norm_std(pre, 2)
                silus1(f + "_gu", inst)
                down(f + "_dn", inst, HB1, SHI1, TX)
                act.wait_ge(S("pe_done"), FIRST[f + "_dn"] + FT // 2)
                squares(lambda k: acc(k, TX), lambda k: SQ1[:, k, :], 0, lambda k: None)
                norm_std(post, 2)
                if inst == 1:
                    break
                gained("attn_pre_g", lambda k: act.wait_ge(S("xu"), k + 1))
                norm_std(2, 2)
                steps(act, "b1_in", lambda i, j, c: split_w(i, c + AHEAD))

                def keys_out(g):
                    act.wait_ge(S("a_tr"), g + 1)
                    act.activation(PT1[g % 2][:, :, :], PS[:, 3:7, 0:3 * P], ACT.Copy).then_inc(S("a_pt"), 1)

                def mixed_hi(g):
                    act.wait_ge(S("a_pv"), g + 1)
                    act.activation(AHI1[:, 2 * g:2 * g + 2, :], PS[:, 7, :].rearrange("p (t n) -> p t n", t=2), ACT.Copy)\
                       .then_inc(S("act_hi"), 2)
                for g in range(4):
                    s = g % 2
                    act.wait_ge(S("a_nm"), g + 1)
                    for b in range(8):
                        src = SB1[s][:, b, :] if b < 4 else SB0[s][:, b - 4, :]
                        act.activation(src, src, ACT.Exp, bias=NM[:, s, b:b + 1], accum_out=SMX[:, s, b:b + 1])\
                           .then_inc(S("a_ex"), 1)
                    if g < 2:
                        act.wait_ge(S("a_se0"), g + 1)
                        act.activation(SE[:, g, :], SE[:, g, :], ACT.Exp).then_inc(S("a_sink"), 1)
                    if g >= 1:
                        keys_out(g - 1)
                        mixed_hi(g - 1)
                keys_out(3)
                mixed_hi(3)
                for j in range(4):
                    split_w(None, FIRST["b1_out"] + j + AHEAD)
                squares(lambda k: FB[:, k, :], lambda k: SQ1[:, k, :], 0, lambda k: act.wait_ge(S("f_ev"), k // 2 + 1))
                norm_std(3, 2)
                gained("ffn2_pre_g", lambda k: act.wait_ge(S("xu"), KT + k + 1))

            gained("ple_pre_g", lambda k: act.wait_ge(S("xu"), 2 * KT + k + 1))
            norm_std(6, 2)
            for j in range(4):
                split_w(None, FIRST["ple_gate"] + j + AHEAD)
                act.wait_ge(S("pg"), j + 1)
                act.activation(PG[:, 2 * j:2 * j + 2, :], GU[:, j % RING, :, :], ACT.Sigmoid).then_inc(S("pg_sig"), 1)
            split_w(None, FIRST["ple_proj"] + AHEAD)
            squares(lambda k: FB[:, k, :], lambda k: SQ1[:, k, :], 0, lambda k: act.wait_ge(S("f_ev"), 5))
            norm_std(7, 2)

            def mod_tile(first, k, v):
                return MOD[:, layer, first + k, v:v + 1]

            def modulated(n_norm, inst, which, shift, t, ready):
                n = P * t
                squares(lambda k: X[:, k, 0:n], lambda k: SQ2[:, k, 0:n], 0, ready)
                norm_std(n_norm, t)
                for k in range(KT):
                    if t == 4:
                        act.wait_ge(S("xr"), KT * inst + k + 1)
                        act.activation(SQ2[:, k, TX:TB], SQ2[:, k, TX:TB], ACT.Identity,
                                       scale=GM[:, layer, which, k, 1:2], bias=mod_tile(shift, k, 1)).then_inc(S("xm_ctx"), 1)
                        act.wait_ge(S("xm_ctx"), KT * inst + k + 1)
                    act.wait_ge(S("xm"), KT * inst + k + 1)
                    act.activation(AHI2[:, k, 0:n], SQ2[:, k, 0:n], ACT.Copy).then_inc(S("act_hi"), 1)

            for layer in range(2):
                nt = TB if layer == 0 else TX
                y_done = 8 * (2 if layer == 0 else 3)
                if layer == 0:
                    modulated(8, 0, 0, 0, 4, lambda k: (act.wait_ge(S("xu"), 4 * KT), act.wait_ge(S("c_ev"), 4)))
                else:
                    modulated(10, 2, 0, 0, 4, lambda k: act.wait_ge(S("xd"), 2 * (k + 1)))
                for q in range(6):
                    n = TB if layer == 0 or q >= 4 else TX
                    c = FIRST[f"qkv{layer}"] + q
                    split_w(None, c + AHEAD)
                    act.wait_ge(S("pe_done"), c + 1)
                    act.activation(QKV[:, 2 * q:2 * q + 2, 0:n], ring2(q, n), ACT.Copy).then_inc(S("qkv_ev"), 1)
                    if q < 3:
                        act.wait_ge(S("f_arg"), 6 * (3 * layer + q + 1))
                        act.activation(HA[:, q, :], FU[:, 1, :], ACT.Sin).then_inc(S("f_h"), 1)
                act.wait_ge(S("f_k"), 2 * layer + 1)
                act.activation(KR[:, :, :], PS[:, 6:8, :], ACT.Copy).then_inc(S("f_kc"), 1)
                act.activation(KRX[:, :], PS[:, 6, :], ACT.Copy).then_inc(S("f_kc"), 1)

                def query_pair(pair):
                    if pair == 0:
                        act.wait_ge(S("h_kn"), 2 * layer + 2)
                    act.wait_ge(S("h_ss"), 5 * layer + pair + 1)
                    q2 = QKV[:, 2 * pair:2 * pair + 2, 0:nt]
                    act.activation(HSQ[:, :, 0:nt], q2, ACT.Square).then_inc(S("h_sq"), 1)
                    act.activation(q2, q2, ACT.Identity, scale=par("q_norm_2", layer)).then_inc(S("h_gain"), 1)

                for q in range(6):
                    c = FIRST[f"hy{layer}"] + q
                    if q == 1:
                        act.wait_ge(S("qkv_ev"), 6 * layer + 6)
                        act.activation(HSQ[:, :, :], QKV[:, 8:10, :], ACT.Square).then_inc(S("h_sq"), 1)
                    if q >= 3:
                        query_pair(q - 3)
                    split_w(None, c + AHEAD)
                    act.wait_ge(S("pe_done"), c + 1)
                    for t in range(2):
                        m = 2 * q + t
                        act.activation(HY[:, m, 0:nt], ring2(q, nt)[:, t, :], ACT.Identity,
                                       scale=par("conv_w_2", 36 * layer + 12 + m), bias=par("conv_b_2", 12 * layer + m))\
                           .then_inc(S("hy_mid"), 1)
                    if q == 0:
                        act.wait_ge(S("f_k"), 2 * layer + 2)
                        act.activation(KIZ[:, :, :], PS[:, 6:8, :], ACT.Copy).then_inc(S("f_kc"), 1)
                    if q == 1:
                        act.wait_ge(S("h_ss"), 5 * layer + 1)
                        act.activation(HSQ[:, :, :], PS[:, 6:8, :], ACT.Sqrt, scale=1.0 / DH2, bias=EPSC[:, 0:1])\
                           .then_inc(S("h_std"), 1)
                query_pair(3)
                tq = nt // P
                act.wait_ge(S("h_ss"), 5 * layer + 5)
                act.activation(STD[:, 0:8 * tq], PS[:, 6, 0:8 * tq], ACT.Sqrt, bias=EPSC[:, 1:2]).then_inc(S("h_std"), 1)
                for grp in range(nt // TX):
                    y = 2 * layer + grp
                    act.wait_ge(S("y_tr"), y + 1)
                    if grp:
                        act.wait_ge(S("y_fwd"), y)
                    act.activation(VTT[:, :, :], PS[:, 0:2, :], ACT.Copy).then_inc(S("y_vt"), 1)
                act.wait_ge(S("y_h"), y_done)
                for m in range(HT):
                    act.activation(HHI[:, m, 0:nt], HY[:, 8 + m, 0:nt], ACT.Copy).then_inc(S("hh_hi"), 1)
                act.wait_ge(S("hh_lo"), HT * (layer + 1))
                act.wait_ge(S("v_tr"), layer + 1)
                act.activation(VT2[:, :, :], PS[:, 4:6, :].rearrange("p a (b n) -> p (a b) n", n=P), ACT.Copy)\
                   .then_inc(S("v_ev"), 1)

                units = [(0, h) for h in range(NH2)] + ([(1, h) for h in range(NH2)] if layer == 0 else [])
                u0 = 2 * NH2 * layer

                def exps(u):
                    grp, h = units[u]
                    s = u % 2
                    act.wait_ge(S("b_nm"), 2 * (u0 + u) + 2)
                    for t in range(2):
                        src = PS[:, 2 * s + t, :] if grp == 0 else PS[:, 2 * s, TX * t:TX * t + TX]
                        n = TB if grp == 0 else TX
                        col = h * tq + 2 * grp + t
                        act.activation(PB[:, s, t, 0:n], src, ACT.Exp, scale=RC[:, col:col + 1],
                                       bias=NM[:, s, t:t + 1], accum_out=SMX[:, s, t:t + 1]).then_inc(S("b_ex"), 1)

                exps(0)
                for u, (grp, h) in enumerate(units):
                    if u + 1 < len(units):
                        exps(u + 1)
                    kts = 4 if grp == 0 else 2
                    act.wait_ge(S("b_tr"), u0 + u + 1)
                    act.activation(PT2[:, u % 2, 0:kts, :],
                                   PS[:, 4:4 + kts // 2, :].rearrange("p a (b n) -> p (a b) n", n=TX), ACT.Copy)\
                       .then_inc(S("b_pt"), 1)

                act.wait_ge(S("b_o"), u0 + len(units))
                for k in range(KT):
                    act.activation(A2HI[:, k, 0:nt], QKV[:, k, 0:nt], ACT.Copy).then_inc(S("a2_hi"), 1)
                for j in range(2):
                    c = FIRST[f"oh{layer}"] + j
                    split_w(None, c + AHEAD)
                    act.wait_ge(S("pe_done"), c + 1)
                    act.wait_ge(S("a2_lo"), KT * (layer + 1))
                    src = PS[:, 4 * j:4 * j + 4, 0:nt]
                    act.activation(MG[:, 4 * j:4 * j + 4, 0:nt], src, ACT.Copy).then_inc(S("oh_ev"), 1)

                def mix(i, m):
                    c = FIRST[f"mix{layer}"] + 3 * m
                    for g in range(2):
                        split_w(i, c + g + AHEAD)
                        act.wait_ge(S("pe_done"), lin(i, 3, c + g + 1))
                        if layer + m:
                            act.wait_ge(S("merge"), lin(i, 3, 12 * layer + 3 * (m - 1) + (1 if g == 0 else 3)))
                        act.activation(SG[:, g, :, 0:nt], ring2(g, nt), ACT.Sigmoid).then_inc(S("gate"), 1)
                    split_w(i, c + 2 + AHEAD)
                mix(None, 0)
                with act.Fori(0, 3) as i:
                    mix(i, 1)
                act.wait_ge(S("pe_done"), FIRST[f"out{layer}"])
                act.wait_ge(S("merge"), 12 * (layer + 1))
                for k in range(KT):
                    act.activation(AHI2[:, k, 0:nt], MG[:, k, 0:nt], ACT.Copy).then_inc(S("mg_hi"), 1)
                for j in range(4):
                    split_w(None, FIRST[f"out{layer}"] + j + AHEAD)

                t = nt // P
                per = nt // TX
                xo0 = 2 * KT * layer
                modulated(9 + 2 * layer, 1 + 2 * layer, 1, 24, t, lambda k: act.wait_ge(S("xo"), xo0 + per * (k + 1)))
                inst = 2 + layer

                def silus2(i, j, c):
                    split_w(i, c + AHEAD)
                    act.wait_ge(S("pe_done"), lin(i, 3, c + 1))
                    if j >= RING:
                        act.wait_ge(S("h"), lin(i, 3, FT * inst + j - RING + 1))
                    act.activation(SIL[:, j % RING, 0:nt], ring2(j, nt)[:, 0, :], ACT.Silu).then_inc(S("sil"), 1)
                steps(act, f"gu{layer}", silus2)
                down(f"dn{layer}", inst, HB2, SHI2, nt)

            squares(lambda k: X[:, k, 0:TX], lambda k: SQ1[:, k, :], 0, lambda k: act.wait_ge(S("xd"), 2 * KT + k + 1))
            norm_std(12, 2)
            for t in range(2):
                act.wait_ge(S("out_tr"), 2 * t + 2)
                act.activation(OUTS[:, t, 512:], PS[:, 2 * t + 1, :], ACT.Copy).then_inc(S("out_ev1"), 1)

        @block.vector
        def _(dve):
            def split_w(i, c):
                if c >= TOTAL:
                    return
                dve.wait_ge(S("hi_done"), lin(i, 3, c + 1))
                dve.tensor_tensor(WLO[:, c % RING, :], RAW[:, c % RING, :], WHI[:, c % RING, :].bitcast(F32), ALU.subtract)\
                   .then_inc(S("lo_done"), 1)

            def split_h(i, inst, j, hb, shi, slo, n):
                dve.wait_ge(S("hs_hi"), lin(i, 3, FT // 2 * inst + j + 1))
                dve.tensor_tensor(slo[:, j % RING, :, 0:n], hb[:, bass.ds(lin(i, 6, 2 * j), 2), 0:n],
                                  shi[:, j % RING, :, 0:n].bitcast(F32), ALU.subtract).then_inc(S("hs_lo"), 1)

            def mod_lo(layer, i, half):
                if half >= 2 * MODC:
                    return
                t = 2 * MODC * layer + half
                dve.wait_ge(S("mod_hi"), lin(i, 6, t + 1))
                dve.tensor_tensor(MLO[:, t % RING, :], MRAW[:, t % RING, :], MHI[:, t % RING, :].bitcast(F32), ALU.subtract)\
                   .then_inc(S("mod_lo"), 1)

            def down(stage, inst, hb, shi, slo, n):
                split_h(None, inst, 0, hb, shi, slo, n)
                split_h(None, inst, 1, hb, shi, slo, n)

                def body(i, j, c):
                    split_w(i, c + AHEAD)
                    if i is not None or j + AHEAD < FT // 2:
                        split_h(i, inst, j + AHEAD, hb, shi, slo, n)
                    if inst < 2 and i is None and j < MODC - FT:
                        mod_lo(inst, None, 2 * (FT + j) + 1)
                        mod_lo(inst, None, 2 * (FT + j) + 2)
                steps(dve, stage, body, tail=2)

            def norm_row(n_norm, t):
                dve.wait_ge(S("n_std"), n_norm + 1)
                dve.reciprocal(RT[:, 0:P * t], RT[:, 0:P * t]).then_inc(S("n_rt"), 1)
                dve.wait_ge(S("n_rt"), n_norm + 1)

            def gained_lo(inst, name):
                for k in range(KT):
                    dve.wait_ge(S("act_hi"), KT * inst + k + 1)
                    dve.scalar_tensor_tensor(out=ALO1[:, k, :], in0=X[:, k, 0:TX], scalar=par(name, k),
                                             in1=AHI1[:, k, :].bitcast(F32), op0=ALU.mult, op1=ALU.subtract)\
                       .then_inc(S("act_lo"), 1)

            def branch(src, gain):
                for k in range(KT):
                    dve.scalar_tensor_tensor(out=TU[:, k, :], in0=src(k), scalar=gain(k), in1=RT[:, 0:TX],
                                             op0=ALU.mult, op1=ALU.mult).then_inc(S("xt"), 1)

            dve.memset(GS[:, 3, :], 0.0).then_inc(S("gs_clear"), 1)
            dve.memset(ONES[:, :], 1.0).then_inc(S("const"), 1)
            dve.memset(EPSC[:, 0:1], EPS).then_inc(S("const"), 1)
            dve.memset(EPSC[:, 1:2], EPS * DH2).then_inc(S("const"), 1)
            dve.wait_ge(S("tr_par"), 1)
            for g in range(4):
                dve.tensor_copy(PAR[:, g, 0:PAR_USED[g]], PS[:, 4, g * P:g * P + PAR_USED[g]]).then_inc(S("par_ev"), 1)
            split_w(None, 0)
            gained_lo(0, "ffn1_pre_g")
            dve.wait_ge(S("sc_hi"), 1)
            dve.tensor_tensor(SCR[:, :, 2:4], SC[:, :, :], SCR[:, :, 0:2].bitcast(F32), ALU.subtract).then_inc(S("sc_lo"), 1)
            split_w(None, 1)
            dve.wait_ge(S("tr_p"), 1)
            dve.tensor_copy(P32[:, :, :], PS[:, 5, :].rearrange("p (t n) -> p t n", t=2)).then_inc(S("p_ev"), 1)
            dve.wait_ge(S("in_bias"), 48)
            dve.wait_ge(S("mm_ext"), 1)
            dve.tensor_tensor(EXT[:, :], PS[0:16, 6, 0:384], MASK[:, :], ALU.add).then_inc(S("ext_ev"), 1)
            dve.wait_ge(S("p_hi"), 1)
            dve.tensor_tensor(PLO[:, :, :], P32[:, :, :], PHI[:, :, :].bitcast(F32), ALU.subtract).then_inc(S("p_lo"), 1)
            dve.wait_ge(S("par_ev"), 4)
            dve.tensor_scalar(HG[:, 0, :], par("ffn1_post_g", 0, 8), 0.5, None, ALU.mult).then_inc(S("hg"), 1)
            dve.tensor_scalar(HG[:, 1, :], par("ffn2_post_g", 0, 8), 0.5, None, ALU.mult).then_inc(S("hg"), 1)
            dve.wait_ge(S("in_sink"), 16)
            dve.tensor_scalar(SINK[:, 1, :], SINK[:, 0, :], -1.0, None, ALU.mult).then_inc(S("nsink"), 1)
            for b in range(4):
                dve.wait_ge(S("tr_c"), b + 1)
                dve.tensor_copy(X[:, 2 * b:2 * b + 2, TX:TB], PS[:, b, :].rearrange("p (t n) -> p t n", t=2))\
                   .then_inc(S("c_ev"), 1)

            for inst, (pre, post) in enumerate(((0, 1), (4, 5))):
                f = f"ffn{inst + 1}"

                def hidden1(i, j, c):
                    split_w(i, c + AHEAD)
                    if i is None and j == 0:
                        norm_row(pre, 2)
                        mod_lo(inst, None, 0)
                    mod_lo(inst, i, 2 * j + 1)
                    mod_lo(inst, i, 2 * j + 2)
                    dve.wait_ge(S("pe_done"), lin(i, 3, c + 1))
                    dve.tensor_tensor(GU[:, j % RING, :, :], ring1(j), over_tiles(RT[:, 0:TX], 2), ALU.mult)\
                       .then_inc(S("gu"), 1)
                    dve.wait_ge(S("sil"), lin(i, 3, FT * inst + j + 1))
                    dve.tensor_tensor(HB1[:, bass.ds(lin(i, 3, j), 1), :], GU[:, j % RING, 0:1, :], GU[:, j % RING, 1:2, :],
                                      ALU.mult).then_inc(S("h"), 1)
                steps(dve, f + "_gu", hidden1)
                down(f + "_dn", inst, HB1, SHI1, SLO1, TX)
                dve.wait_ge(S("mod_col"), MODC * (inst + 1))
                bias = over_tokens(par("b_mod_2", 48 * inst, 48), 2)
                dve.tensor_tensor(MOD[:, inst, :, :], MSUM[:, :, 2:4], bias, ALU.add).then_inc(S("mod_ev"), 1)
                dve.wait_ge(S("mod_ev"), 4 * inst + 1)
                dve.tensor_tensor(MOD[:, inst, :, :], MOD[:, inst, :, :], MSUM[:, :, 0:2], ALU.add).then_inc(S("mod_ev"), 1)
                dve.wait_ge(S("mod_ev"), 4 * inst + 2)
                for w, (first, name) in enumerate(((8, "norm_mix_2"), (32, "norm_ffn_2"))):
                    dve.scalar_tensor_tensor(out=GM[:, inst, w, :, :], in0=MOD[:, inst, first:first + 8, :], scalar=1.0,
                                             in1=over_tokens(par(name, 8 * inst, 8), 2), op0=ALU.add, op1=ALU.mult)\
                       .then_inc(S("mod_ev"), 1)
                norm_row(post, 2)
                dve.wait_ge(S("hg"), 2)
                branch(lambda k: acc(k, TX), lambda k: HG[:, inst, k:k + 1])
                if inst == 1:
                    break
                gained_lo(1, "attn_pre_g")

                def z_tiles(i, j, c):
                    split_w(i, c + AHEAD)
                    if i is None and j == 0:
                        norm_row(2, 2)
                    dve.wait_ge(S("pe_done"), lin(i, 3, c + 1))
                    dve.tensor_tensor(GU[:, j % RING, :, :], ring1(j), over_tiles(RT[:, 0:TX], 2), ALU.mult)\
                       .then_inc(S("zt"), 1)
                    dve.wait_ge(S("zt"), lin(i, 6, 2 * j + 1))
                    g, row, _ = PAR_AT["b_in"]
                    bias = PAR[:, g, bass.ds(lin(i, 6, row + 2 * j), 2)]
                    dve.tensor_tensor(Z[:, bass.ds(lin(i, 6, 2 * j), 2), :], GU[:, j % RING, :, :], over_tokens(bias, TX),
                                      ALU.add).then_inc(S("zt"), 1)
                steps(dve, "b1_in", z_tiles)

                for b in range(3):
                    dve.wait_ge(S("vt_tr"), b + 1)
                    n = 4 if b < 2 else 2
                    dve.tensor_copy(VT1[:, 4 * b:4 * b + n, :], PS[:, b, 0:n * P].rearrange("p (a n) -> p a n", n=P))\
                       .then_inc(S("vt_ev"), 1)

                def scores_in(g):
                    s = g % 2
                    dve.wait_ge(S("a_s"), g + 1)
                    heads = BIAS[g // 2][:, 4 * (g % 2):4 * (g % 2) + 4, ::-1]
                    for a in range(2):
                        dve.scalar_tensor_tensor(out=SB1[s][:, a::2, :], in0=PS[:, a, :].rearrange("p (b n) -> p b n", n=TX),
                                                 scalar=DH1 ** -0.5, in1=heads[:, a::2, :], op0=ALU.mult, op1=ALU.add)\
                           .then_inc(S("a_sb"), 1)
                    dve.scalar_tensor_tensor(out=SB0[s][:, :, :], in0=PS[:, 2, :].rearrange("p (b n) -> p b n", n=P),
                                             scalar=DH1 ** -0.5, in1=heads[:, :, P:TX], op0=ALU.mult, op1=ALU.add)\
                       .then_inc(S("a_sb"), 1)
                    dve.wait_ge(S("a_sb"), 3 * g + 3)
                    dve.tensor_reduce(SE[:, s, 0:4] if g < 2 else NM[:, s, 0:4], SB1[s][:, :, :], AX.X, ALU.max, negate=True)\
                       .then_inc(S("a_mx"), 1)
                    last = dve.tensor_reduce(SE[:, s, 4:8] if g < 2 else NM[:, s, 4:8], SB0[s][:, :, :], AX.X, ALU.max,
                                             negate=True)
                    if g >= 2:
                        last.then_inc(S("a_nm"), 1)
                        return
                    last.then_inc(S("a_mx"), 1)
                    dve.wait_ge(S("a_mx"), 2 * g + 2)
                    dve.wait_ge(S("nsink"), 1)
                    sinks = over_tiles(SINK[:, 1, 4 * g:4 * g + 4], 2)
                    dve.tensor_tensor(NM[:, s, :].rearrange("p (t h) -> p t h", t=2), SE[:, s, :].rearrange("p (t h) -> p t h", t=2),
                                      sinks, ALU.min).then_inc(S("a_nm"), 1)
                    dve.wait_ge(S("a_nm"), g + 1)
                    dve.tensor_tensor(SE[:, s, :].rearrange("p (t h) -> p t h", t=2), NM[:, s, :].rearrange("p (t h) -> p t h", t=2),
                                      sinks, ALU.subtract).then_inc(S("a_se0"), 1)

                def normalise(g):
                    s = g % 2
                    dve.wait_ge(S("a_ex"), 8 * g + 8)
                    if g < 2:
                        dve.wait_ge(S("a_sink"), g + 1)
                        dve.tensor_tensor(SMX[:, s, :], SMX[:, s, :], SE[:, s, :], ALU.add).then_inc(S("a_tot"), 1)
                        dve.wait_ge(S("a_tot"), g + 1)
                    dve.reciprocal(RS[:, s, :], SMX[:, s, :]).then_inc(S("a_rs"), 1)
                    dve.wait_ge(S("a_rs"), g + 1)
                    dve.tensor_tensor(SB1[s][:, :, :], SB1[s][:, :, :], over_tokens(RS[:, s, 0:4], TX), ALU.mult)\
                       .then_inc(S("a_p"), 1)
                    dve.tensor_tensor(SB0[s][:, :, :], SB0[s][:, :, :], over_tokens(RS[:, s, 4:8], P), ALU.mult)\
                       .then_inc(S("a_p"), 1)

                def mixed_lo(g):
                    dve.wait_ge(S("act_hi"), 2 * KT + 2 * g + 2)
                    dve.tensor_tensor(ALO1[:, 2 * g:2 * g + 2, :], PS[:, 7, :].rearrange("p (t n) -> p t n", t=2),
                                      AHI1[:, 2 * g:2 * g + 2, :].bitcast(F32), ALU.subtract).then_inc(S("act_lo"), 2)

                dve.wait_ge(S("bias_in"), 32)
                scores_in(0)
                for g in range(4):
                    normalise(g)
                    if g < 3:
                        scores_in(g + 1)
                    if g >= 1:
                        mixed_lo(g - 1)
                mixed_lo(3)
                for j in range(4):
                    c = FIRST["b1_out"] + j
                    split_w(None, c + AHEAD)
                    dve.wait_ge(S("pe_done"), c + 1)
                    dve.tensor_tensor(FB[:, 2 * j:2 * j + 2, :], ring1(j), over_tokens(par("b_out", 2 * j, 2), TX), ALU.add)\
                       .then_inc(S("f_ev"), 1)
                norm_row(3, 2)
                dve.wait_ge(S("f_ev"), 4)
                branch(lambda k: FB[:, k, :], lambda k: par("attn_post_g", k))
                gained_lo(3, "ffn2_pre_g")

            gained_lo(4, "ple_pre_g")
            for j in range(4):
                c = FIRST["ple_gate"] + j
                split_w(None, c + AHEAD)
                if j == 0:
                    norm_row(6, 2)
                dve.wait_ge(S("pe_done"), c + 1)
                if j >= RING:
                    dve.wait_ge(S("pg_sig"), j - RING + 1)
                dve.tensor_tensor(GU[:, j % RING, :, :], ring1(j), over_tiles(RT[:, 0:TX], 2), ALU.mult).then_inc(S("pg"), 1)
            split_w(None, FIRST["ple_proj"] + AHEAD)
            dve.wait_ge(S("pe_done"), FIRST["ple_proj"] + 1)
            dve.wait_ge(S("pg_sig"), 4)
            dve.tensor_tensor(FB[:, :, :], PG[:, :, :], PS[:, 0:4, :].rearrange("p a (b n) -> p (a b) n", n=TX), ALU.mult)\
               .then_inc(S("f_ev"), 1)
            norm_row(7, 2)
            dve.wait_ge(S("f_ev"), 5)
            branch(lambda k: FB[:, k, :], lambda k: par("ple_post_g", k))

            def modulated(n_norm, inst, a_inst, which, shift, t):
                n = P * t
                norm_row(n_norm, t)

                def low(k):
                    dve.wait_ge(S("act_hi"), KT * a_inst + k + 1)
                    dve.tensor_tensor(ALO2[:, k, 0:n], SQ2[:, k, 0:n], AHI2[:, k, 0:n].bitcast(F32), ALU.subtract)\
                       .then_inc(S("act_lo"), 1)
                for k in range(KT):
                    dve.tensor_tensor(SQ2[:, k, 0:n], X[:, k, 0:n], RT[:, 0:n], ALU.mult).then_inc(S("xr"), 1)
                    dve.wait_ge(S("xr"), KT * inst + k + 1)
                    dve.tensor_scalar(SQ2[:, k, 0:TX], SQ2[:, k, 0:TX], GM[:, layer, which, k, 0:1],
                                      MOD[:, layer, shift + k, 0:1], ALU.mult, ALU.add).then_inc(S("xm"), 1)
                    if k:
                        low(k - 1)
                low(KT - 1)

            for layer in range(2):
                nt = TB if layer == 0 else TX
                y_done = 8 * (2 if layer == 0 else 3)
                modulated(8 + 2 * layer, 2 * layer, 5 + 2 * layer, 0, 0, 4)

                def network(l):
                    a0 = 6 * (3 * layer + l)
                    dve.wait_ge(S("f_mm"), 3 * layer + l + 1)
                    row = PAR_AT[f"filt_b{l + 1}_2"][1] + layer
                    fr = PAR_AT["filt_freq_2"][1] + 3 * layer + l
                    dve.tensor_scalar(FU[:, 0, :], PS[0:FH, 7, 0:TX], PAR[0:FH, 3, row:row + 1], PAR[0:FH, 3, fr:fr + 1],
                                      ALU.add, ALU.mult).then_inc(S("f_arg"), 1)
                    dve.wait_ge(S("f_arg"), a0 + 1)
                    dve.tensor_scalar(FU[:, 1, :], FU[:, 0, :], 1.0 / (2.0 * np.pi), MAGIC, ALU.mult, ALU.add)\
                       .then_inc(S("f_arg"), 1)
                    dve.wait_ge(S("f_arg"), a0 + 2)
                    dve.tensor_scalar(FU[:, 2, :], FU[:, 1, :], -MAGIC, None, ALU.add).then_inc(S("f_arg"), 1)
                    dve.wait_ge(S("f_arg"), a0 + 3)
                    dve.scalar_tensor_tensor(out=FU[:, 3, :], in0=FU[:, 2, :], scalar=-TWO_PI_HI, in1=FU[:, 0, :],
                                             op0=ALU.mult, op1=ALU.add).then_inc(S("f_arg"), 1)
                    dve.wait_ge(S("f_arg"), a0 + 4)
                    dve.scalar_tensor_tensor(out=FU[:, 0, :], in0=FU[:, 2, :], scalar=-TWO_PI_LO, in1=FU[:, 3, :],
                                             op0=ALU.mult, op1=ALU.add).then_inc(S("f_arg"), 1)
                    dve.wait_ge(S("f_arg"), a0 + 5)
                    dve.tensor_scalar(FU[:, 1, :], FU[:, 0, :], PI_IN, -PI_IN, ALU.min, ALU.max).then_inc(S("f_arg"), 1)

                def decay(t):
                    dve.wait_ge(S("f_taps"), 2 * layer + t + 1)
                    for r in range(2):
                        dve.tensor_tensor(HF[:, t, r, :], PS[:, 6 + r, :], DEC[:, t, :], ALU.mult).then_inc(S("f_dec"), 1)

                beside = [lambda: network(0), lambda: network(1), lambda: network(2), lambda: decay(0), lambda: decay(1),
                          lambda: None]
                for q in range(6):
                    split_w(None, FIRST[f"qkv{layer}"] + q + AHEAD)
                    beside[q]()

                def keys():
                    dve.wait_ge(S("h_std"), 2 * layer + 1)
                    for kv in range(2):
                        dve.reciprocal(HSQ[:, kv, :], HSQ[:, kv, :]).then_inc(S("h_kr"), 1)
                    for kv in range(2):
                        dve.wait_ge(S("h_kr"), 2 * layer + kv + 1)
                        dve.scalar_tensor_tensor(out=QKV[:, 8 + kv, :], in0=QKV[:, 8 + kv, :], scalar=par("k_norm_2", layer),
                                                 in1=HSQ[:, kv, :], op0=ALU.mult, op1=ALU.mult).then_inc(S("h_kn"), 1)

                def rotated(r, tile):
                    if r:
                        dve.wait_ge(S("h_sum"), 5 * layer + r)
                    dve.wait_ge(S("h_rot"), 5 * layer + r + 1)
                    dve.tensor_tensor(BR[:, :, :], PS[:, 7, :].rearrange("p (t n) -> p t n", t=2), over_tiles(ROPE[:, 1, :], 2),
                                      ALU.mult).then_inc(S("h_sin"), 1)
                    dve.wait_ge(S("h_sin"), 5 * layer + r + 1)
                    dve.wait_ge(S("h_cos"), 5 * layer + r + 1)
                    dve.tensor_tensor(QKV[:, tile:tile + 2, 0:TX], QKV[:, tile:tile + 2, 0:TX], BR[:, :, :], ALU.add)\
                       .then_inc(S("h_sum"), 1)

                for q in range(6):
                    c = FIRST[f"hy{layer}"] + q
                    split_w(None, c + AHEAD)
                    if q == 2:
                        keys()
                    if q >= 3:
                        rotated(q - 3, (8, 0, 2)[q - 3])
                    for t in range(2):
                        m = 2 * q + t
                        dve.wait_ge(S("hy_mid"), 12 * layer + 2 * q + 2)
                        u3 = ring2(q, nt)[:, t, :].rearrange("p (g n) -> p g n", n=TX)
                        y3 = HY[:, m, 0:nt].rearrange("p (g n) -> p g n", n=TX)
                        dve.scalar_tensor_tensor(out=y3[:, :, 1:TX], in0=u3[:, :, 0:TX - 1], scalar=par("conv_w_2", 36 * layer + m),
                                                 in1=y3[:, :, 1:TX], op0=ALU.mult, op1=ALU.add).then_inc(S("hy_taps"), 1)
                        dve.wait_ge(S("hy_taps"), 24 * layer + 2 * m + 1)
                        dve.scalar_tensor_tensor(out=y3[:, :, 0:TX - 1], in0=u3[:, :, 1:TX],
                                                 scalar=par("conv_w_2", 36 * layer + 24 + m), in1=y3[:, :, 0:TX - 1],
                                                 op0=ALU.mult, op1=ALU.add).then_inc(S("hy_taps"), 1)
                    if q == 0:
                        dve.wait_ge(S("f_kc"), 3 * layer + 3)
                        dve.tensor_copy(KRX[0:1, :], PS[0:1, 6, :]).then_inc(S("f_fix"), 1)
                        dve.memset(KIZ[0:1, 0, :], 0.0).then_inc(S("f_fix"), 1)
                rotated(3, 4)
                rotated(4, 6)
                tq = nt // P
                dve.wait_ge(S("h_std"), 2 * layer + 2)
                dve.reciprocal(RC[:, 0:8 * tq], STD[:, 0:8 * tq]).then_inc(S("h_rc"), 1)
                dve.wait_ge(S("h_sum"), 5 * (layer + 1))
                dve.wait_ge(S("f_fix"), 2 * layer + 2)
                for grp in range(nt // TX):
                    y = 2 * layer + grp
                    re, im = PS[:, 2:4, :], PS[:, 4:6, :]
                    if y:
                        dve.wait_ge(S("y_h"), 8 * y)
                    dve.wait_ge(S("y_fwd"), y + 1)
                    dve.tensor_tensor(YT1[:, :, :], re, KR[:, :, :], ALU.mult).then_inc(S("y_mul"), 1)
                    dve.tensor_tensor(YT2[:, :, :], im, KIZ[:, :, :], ALU.mult).then_inc(S("y_mul"), 1)
                    dve.wait_ge(S("y_mul"), 7 * y + 2)
                    dve.tensor_tensor(YS[:, 0:2, :], YT1[:, :, :], YT2[:, :, :], ALU.subtract).then_inc(S("y_mul"), 1)
                    dve.wait_ge(S("y_mul"), 7 * y + 3)
                    dve.tensor_tensor(YT1[:, :, :], re, KIZ[:, :, :], ALU.mult).then_inc(S("y_mul"), 1)
                    dve.tensor_tensor(YT2[:, 0, :], im[:, 0, :], KRX[:, :], ALU.mult).then_inc(S("y_mul"), 1)
                    dve.tensor_tensor(YT2[:, 1, :], im[:, 1, :], KR[:, 1, :], ALU.mult).then_inc(S("y_mul"), 1)
                    dve.wait_ge(S("y_mul"), 7 * y + 6)
                    dve.tensor_tensor(YS[:, 2:4, :], YT1[:, :, :], YT2[:, :, :], ALU.add).then_inc(S("y_mul"), 1)
                    dve.wait_ge(S("y_mul"), 7 * y + 7)
                    dve.wait_ge(S("y_inv"), y + 1)
                    g = slice(TX * grp, TX * grp + TX)
                    for m in range(HT):
                        tmp = YT1[:, m // 2, m % 2 * TX:m % 2 * TX + TX]
                        out = PS[:, 6 + m // 2, m % 2 * TX:m % 2 * TX + TX]
                        dve.scalar_tensor_tensor(out=tmp, in0=HY[:, 8 + m, g], scalar=par("hyena_bias_2", 4 * layer + m), in1=out,
                                                 op0=ALU.mult, op1=ALU.add).then_inc(S("y_h"), 1)
                        dve.wait_ge(S("y_h"), 8 * y + 2 * m + 1)
                        dve.tensor_tensor(HY[:, 8 + m, g], tmp, HY[:, m, g], ALU.mult).then_inc(S("y_h"), 1)
                for m in range(HT):
                    dve.wait_ge(S("hh_hi"), HT * layer + m + 1)
                    dve.tensor_tensor(HLO[:, m, 0:nt], HY[:, 8 + m, 0:nt], HHI[:, m, 0:nt].bitcast(F32), ALU.subtract)\
                       .then_inc(S("hh_lo"), 1)
                units = [(0, h) for h in range(NH2)] + ([(1, h) for h in range(NH2)] if layer == 0 else [])
                u0 = 2 * NH2 * layer

                def maxima(u):
                    grp, h = units[u]
                    s = u % 2
                    dve.wait_ge(S("b_s"), u0 + u + 1)
                    src = PS[:, 2 * s:2 * s + 2, :] if grp == 0 else PS[:, 2 * s, :].rearrange("p (t n) -> p t n", t=2)
                    dve.tensor_reduce(NM[:, s, 2:4], src, AX.X, ALU.max, negate=True).then_inc(S("b_nm"), 1)
                    dve.wait_ge(S("b_nm"), 2 * (u0 + u) + 1)
                    col = h * tq + 2 * grp
                    dve.tensor_tensor(NM[:, s, 0:2], NM[:, s, 2:4], RC[:, col:col + 2], ALU.mult).then_inc(S("b_nm"), 1)

                def normalise2(u):
                    s = u % 2
                    n = TB if units[u][0] == 0 else TX
                    dve.wait_ge(S("b_ex"), 2 * (u0 + u) + 2)
                    dve.reciprocal(RS[:, s, 0:2], SMX[:, s, 0:2]).then_inc(S("b_rs"), 1)
                    dve.wait_ge(S("b_rs"), u0 + u + 1)
                    for t in range(2):
                        dve.tensor_scalar(PB[:, s, t, 0:n], PB[:, s, t, 0:n], RS[:, s, t:t + 1], None, ALU.mult)\
                           .then_inc(S("b_p"), 1)

                def attended(u):
                    grp, h = units[u]
                    dve.wait_ge(S("b_pv"), u0 + u + 1)
                    dve.tensor_copy(QKV[:, h, TX * grp:TX * grp + TX], PS[:, 6 + u % 2, 0:TX]).then_inc(S("b_o"), 1)

                dve.wait_ge(S("h_rc"), layer + 1)
                maxima(0)
                for u in range(len(units)):
                    if u + 1 < len(units):
                        maxima(u + 1)
                    normalise2(u)
                    if u:
                        attended(u - 1)
                attended(len(units) - 1)

                dve.wait_ge(S("hh_lo"), HT * (layer + 1))
                for k in range(KT):
                    dve.wait_ge(S("a2_hi"), KT * layer + k + 1)
                    dve.tensor_tensor(A2LO[:, k, 0:nt], QKV[:, k, 0:nt], A2HI[:, k, 0:nt].bitcast(F32), ALU.subtract)\
                       .then_inc(S("a2_lo"), 1)
                for j in range(2):
                    split_w(None, FIRST[f"oh{layer}"] + j + AHEAD)

                def mix(i, m):
                    c = FIRST[f"mix{layer}"] + 3 * m
                    b = 12 * layer + 3 * m
                    mg = MG[:, bass.ds(lin(i, 2, 2 * m), 2), 0:nt]
                    split_w(i, c + AHEAD)
                    dve.wait_ge(S("gate"), lin(i, 2, 8 * layer + 2 * m + 1))
                    dve.tensor_tensor(mg, mg, SG[:, 0, :, 0:nt], ALU.mult).then_inc(S("merge"), 1)
                    split_w(i, c + 1 + AHEAD)
                    split_w(i, c + 2 + AHEAD)
                    dve.wait_ge(S("gate"), lin(i, 2, 8 * layer + 2 * m + 2))
                    dve.wait_ge(S("pe_done"), lin(i, 3, c + 3))
                    dve.tensor_tensor(SG[:, 1, :, 0:nt], SG[:, 1, :, 0:nt], ring2(2, nt), ALU.mult).then_inc(S("merge"), 1)
                    dve.wait_ge(S("merge"), lin(i, 3, b + 2))
                    dve.tensor_tensor(mg, mg, SG[:, 1, :, 0:nt], ALU.add).then_inc(S("merge"), 1)
                mix(None, 0)
                with dve.Fori(0, 3) as i:
                    mix(i, 1)
                for k in range(KT):
                    dve.wait_ge(S("mg_hi"), KT * layer + k + 1)
                    dve.tensor_tensor(ALO2[:, k, 0:nt], MG[:, k, 0:nt], AHI2[:, k, 0:nt].bitcast(F32), ALU.subtract)\
                       .then_inc(S("mg_lo"), 1)

                def gated_update(src, m, gate, sem):
                    for v in range(nt // TX):
                        g = slice(TX * v, TX * v + TX)
                        dve.scalar_tensor_tensor(out=X[:, m, g], in0=src[:, g], scalar=MOD[:, layer, gate + m, v:v + 1],
                                                 in1=X[:, m, g], op0=ALU.mult, op1=ALU.add).then_inc(S(sem), 1)
                for j in range(4):
                    c = FIRST[f"out{layer}"] + j
                    split_w(None, c + AHEAD)
                    dve.wait_ge(S("pe_done"), c + 1)
                    for t in range(2):
                        gated_update(ring2(j, nt)[:, t, :], 2 * j + t, 16, "xo")
                xo_now = 2 * KT if layer == 0 else 3 * KT
                dve.wait_ge(S("xo"), xo_now)
                modulated(9 + 2 * layer, 1 + 2 * layer, 6 + 2 * layer, 1, 24, nt // P)
                inst = 2 + layer

                def hidden2(i, j, c):
                    split_w(i, c + AHEAD)
                    dve.wait_ge(S("sil"), lin(i, 3, FT * inst + j + 1))
                    dve.tensor_tensor(HB2[:, bass.ds(lin(i, 3, j), 1), 0:nt], SIL[:, j % RING:j % RING + 1, 0:nt],
                                      ring2(j, nt)[:, 1:2, :], ALU.mult).then_inc(S("h"), 1)
                steps(dve, f"gu{layer}", hidden2)
                down(f"dn{layer}", inst, HB2, SHI2, SLO2, nt)
                dve.wait_ge(S("pe_done"), FIRST[f"dn{layer}"] + FT // 2)
                for m in range(KT):
                    gated_update(acc(m, nt), m, 40, "xd")

            dve.wait_ge(S("xd"), 3 * KT)
            norm_row(12, 2)
            for k in range(KT):
                dve.scalar_tensor_tensor(out=YF[:, k, :], in0=X[:, k, 0:TX], scalar=par("norm_final_2", k), in1=RT[:, 0:TX],
                                         op0=ALU.mult, op1=ALU.mult).then_inc(S("yf"), 1)
            for t in range(2):
                dve.wait_ge(S("out_tr"), 2 * t + 1)
                dve.tensor_copy(OUTS[:, t, 0:512], PS[:, 2 * t, :]).then_inc(S("out_ev0"), 1)

        @block.tensor
        def _(pe):
            def product(out, whi, wlo, xhi, xlo, first, last, shared=False):
                pe.matmul(out, whi, xhi, start=first, stop=False, skip_group_check=shared)
                pe.matmul(out, whi, xlo, start=False, stop=False, skip_group_check=shared)
                return pe.matmul(out, wlo, xhi, start=False, stop=last, skip_group_check=shared)

            def weights(c, t, k, width):
                a = k * width + t * P
                return WHI[:, c % RING, a:a + P], WLO[:, c % RING, a:a + P]

            def chunk_ready(i, c):
                pe.wait_ge(S("lo_done"), lin(i, 3, c + 1))

            def by_columns(i, c, outs, hi, lo, n, k_tiles=KT, width=2 * P, ready=None, turn=None):
                chunk_ready(i, c)
                for t, out in enumerate(outs):
                    if turn and t:
                        mod_row_ready(*turn)
                    for k in range(k_tiles):
                        if turn and t and k == 1:
                            mod_turn()
                        if ready and t == 0:
                            ready(k)
                        last = product(out, *weights(c, t, k, width), hi[:, k, 0:n], lo[:, k, 0:n], k == 0, k == k_tiles - 1)
                last.then_inc(S("pe_done"), 1)

            def down(stage, inst, shi, slo, n):
                def body(i, j, c):
                    chunk_ready(i, c)
                    pe.wait_ge(S("hs_lo"), lin(i, 3, FT // 2 * inst + j + 1))
                    end = i is None and j == FT // 2 - 1
                    for m in range(KT):
                        if m == KT // 2 and inst < 2 and i is None and j <= MODC - FT:
                            mod_row_ready(inst, None, FT + j - 1)
                            mod_turn()
                        for kk in range(2):
                            start = i is None and j == 0 and kk == 0 and (n == TB or m % 2 == 0)
                            last = product(acc(m, n), *weights(c, m, kk, D), shi[:, j % RING, kk, 0:n],
                                           slo[:, j % RING, kk, 0:n], start, end and kk == 1, shared=True)
                    last.then_inc(S("pe_done"), 1)
                    if stage in ("ffn1_dn", "ffn2_dn") and i is None and j < MODC - FT:
                        modulation(inst, None, FT + j)
                steps(pe, stage, body, tail=2)

            def mod_row_ready(layer, i, g):
                pe.wait_ge(S("mod_row"), lin(i, 3, MODC * layer + g + 1))

            def mod_turn():
                for t in range(2):
                    last = pe.transpose(PS[:, 7, 4 * t:4 * t + 4], MROW[:, t * P:t * P + P], IDENT[0:4, 0:4])
                last.then_inc(S("mod_tr"), 1)

            def modulation(layer, i, g):
                if g:
                    pe.wait_ge(S("mod_col"), lin(i, 3, MODC * layer + g))
                for hh in range(2):
                    t = 2 * (MODC * layer + g) + hh
                    pe.wait_ge(S("mod_lo"), lin(i, 6, t + 1))
                    for kk in range(4):
                        k = 4 * hh + kk
                        for w in (MHI, MLO):
                            last = pe.matmul(PS[0:4, 7, TX:TB], SCR[:, k, :], w[:, t % RING, kk * 2 * P:kk * 2 * P + 2 * P],
                                             start=k == 0 and w is MHI, stop=k == KT - 1 and w is MLO)
                    last.then_inc(S("mod_used"), 1)

            def norm_sums(n_norm, t, src):
                for k in range(KT):
                    pe.wait_ge(S("n_sq"), KT * n_norm + k + 1)
                    last = pe.matmul(stat_row(n_norm, t), ONES[:, :], src[:, k, 0:P * t], start=k == 0, stop=k == KT - 1)
                last.then_inc(S("n_ss"), 1)

            def wait_k(sem, before):
                return lambda k: pe.wait_ge(S(sem), before + k + 1)

            pe.wait_ge(S("in_ident"), 16)
            pe.wait_ge(S("in_x"), 16)
            for b in range(4):
                for k in (2 * b, 2 * b + 1):
                    for t in range(2):
                        last = pe.transpose(PS[:, b, k % 2 * TX + t * P:k % 2 * TX + t * P + P], XS[:, t, k * P:k * P + P], IDENT[:, :])
                last.then_inc(S("tr_x"), 1)
            pe.wait_ge(S("gs_clear"), 1)
            pe.wait_ge(S("in_par"), 16 * len(PAR_AT))
            for g in range(4):
                n = PAR_USED[g]
                last = pe.transpose(PS[:, 4, g * P:g * P + n], GS[0:n, g, :], IDENT[0:n, 0:n])
            last.then_inc(S("tr_par"), 1)
            pe.wait_ge(S("in_p"), 16)
            for k in range(2):
                for t in range(2):
                    last = pe.transpose(PS[:, 5, k * TX + t * P:k * TX + t * P + P], PST[:, t, k * P:k * P + P], IDENT[:, :])
            last.then_inc(S("tr_p"), 1)
            pe.wait_ge(S("in_bias"), 48)
            pe.matmul(PS[0:16, 6, 0:384], REL[:, :], ONEHOT[:, :], start=True, stop=True).then_inc(S("mm_ext"), 1)
            pe.wait_ge(S("in_ctx"), 16)
            for b in range(4):
                pe.wait_ge(S("x_ev"), b + 1)
                for k in (2 * b, 2 * b + 1):
                    for t in range(2):
                        last = pe.transpose(PS[:, b, k % 2 * TX + t * P:k % 2 * TX + t * P + P], CS[:, t, k * P:k * P + P], IDENT[:, :])
                last.then_inc(S("tr_c"), 1)
            pe.wait_ge(S("const"), 3)

            for inst, (pre, post) in enumerate(((0, 1), (4, 5))):
                f = f"ffn{inst + 1}"

                def gate_up(i, j, c):
                    first = i is None and j == 0
                    if first and inst == 0:
                        pe.wait_ge(S("par_ev"), 4)
                        pe.wait_ge(S("p_ev"), 1)
                        pe.wait_ge(S("ext_ev"), 1)
                    if j >= RING:
                        pe.wait_ge(S("gu"), lin(i, 3, FT * inst + j - RING + 1))
                    out = ring1(j)
                    by_columns(i, c, [out[:, 0, :], out[:, 1, :]], AHI1, ALO1, TX,
                               ready=wait_k("act_lo", 3 * KT * inst) if first else None,
                               turn=(inst, i, j - 1) if j else None)
                    if i is None and j == 0:
                        pe.wait_ge(S("c_ev"), 4)
                        norm_sums(pre, 2, SQ1)
                        if inst == 0:
                            pe.wait_ge(S("sc_lo"), 1)
                    modulation(inst, i, j)
                steps(pe, f + "_gu", gate_up)
                down(f + "_dn", inst, SHI1, SLO1, TX)
                norm_sums(post, 2, SQ1)
                if inst == 1:
                    break

                def project(i, j, c):
                    if j >= RING:
                        pe.wait_ge(S("zt"), lin(i, 6, 2 * (j - RING) + 1))
                    out = ring1(j)
                    by_columns(i, c, [out[:, 0, :], out[:, 1, :]], AHI1, ALO1, TX,
                               ready=wait_k("act_lo", KT) if i is None and j == 0 else None)
                    if i is None and j == 0:
                        norm_sums(2, 2, SQ1)
                steps(pe, "b1_in", project)

                pe.wait_ge(S("zt"), 18)
                for b in range(3):
                    for a in range(4 * b, min(4 * b + 4, 10)):
                        tile = 5 if a < 2 else 13 + a // 2
                        last = pe.transpose(PS[:, b, a % 4 * P:a % 4 * P + P], Z[:, tile, a % 2 * P:a % 2 * P + P], IDENT[:, :])
                    last.then_inc(S("vt_tr"), 1)

                def scores(g):
                    if g:
                        pe.wait_ge(S("a_sb"), 3 * g)
                    else:
                        pe.wait_ge(S("vt_ev"), 3)
                    for hl in (0, 2, 1, 3):
                        h = 4 * g + hl
                        p0 = 64 * (h % 2)
                        if hl == 1:
                            pe.wait_ge(S("a_even"), g + 1)
                        if h < 8:
                            q = Z[p0:p0 + 64, h // 2, :]
                            k = Z[p0:p0 + 64, 4, :] if h // 4 == h % 2 else KS[p0:p0 + 64, :]
                        else:
                            q, k = Z[p0:p0 + 64, 6 + (h - 8) // 2, :], Z[p0:p0 + 64, 10 + (h - 8) // 2, :]
                        pe.matmul(PS[:, hl % 2, hl // 2 * TX:hl // 2 * TX + TX], q[:, P:TX], k[:, :], start=True, stop=True)
                        last = pe.matmul(PS[:, 2, hl * P:hl * P + P], q[:, 0:P], k[:, 0:P], start=True, stop=True)
                        if hl == 2:
                            last.then_inc(S("a_even"), 1)
                    last.then_inc(S("a_s"), 1)

                pe.wait_ge(S("ks"), 32)
                scores(0)
                for g in range(4):
                    s = g % 2
                    if g < 3:
                        scores(g + 1)
                    pe.wait_ge(S("a_p"), 2 * g + 2)
                    if g:
                        pe.wait_ge(S("a_pt"), g)
                    for hl in range(4):
                        for src, col in ((SB0[s][:, hl, :], 0), (SB1[s][:, hl, 0:P], P), (SB1[s][:, hl, P:TX], 2 * P)):
                            last = pe.transpose(PS[:, 3 + hl, col:col + P], src, IDENT[:, :])
                    last.then_inc(S("a_tr"), 1)
                    pe.wait_ge(S("a_pt"), g + 1)
                    if g:
                        pe.wait_ge(S("act_lo"), 2 * KT + 2 * g)
                    for hl in range(4):
                        h = 4 * g + hl
                        p0 = 64 * (h % 2)
                        v, c0 = (0, 64 * g) if h < 8 else (2 + 2 * ((h - 8) // 2), p0)
                        out = PS[p0:p0 + 64, 7, hl // 2 * TX:hl // 2 * TX + TX]
                        pe.matmul(out, VT1[:, v, c0:c0 + 64], PT1[s][:, hl, 0:TX], start=True, stop=False)
                        last = pe.matmul(out[:, P:TX], VT1[:, v + 1, c0:c0 + 64], PT1[s][:, hl, TX:3 * P], start=False, stop=True)
                    last.then_inc(S("a_pv"), 1)

                for j in range(4):
                    if j >= RING:
                        pe.wait_ge(S("f_ev"), j - RING + 1)
                    out = ring1(j)
                    by_columns(None, FIRST["b1_out"] + j, [out[:, 0, :], out[:, 1, :]], AHI1, ALO1, TX,
                               ready=wait_k("act_lo", 2 * KT) if j == 0 else None)
                norm_sums(3, 2, SQ1)

            for j in range(4):
                if j >= RING:
                    pe.wait_ge(S("pg"), j - RING + 1)
                out = ring1(j)
                by_columns(None, FIRST["ple_gate"] + j, [out[:, 0, :], out[:, 1, :]], AHI1, ALO1, TX,
                           ready=wait_k("act_lo", 4 * KT) if j == 0 else None)
                if j == 0:
                    norm_sums(6, 2, SQ1)
            pe.wait_ge(S("p_lo"), 1)
            by_columns(None, FIRST["ple_proj"], [acc(m, TX) for m in range(KT)], PHI, PLO, TX, k_tiles=2, width=D)
            norm_sums(7, 2, SQ1)

            for layer in range(2):
                nt = TB if layer == 0 else TX
                def network(l):
                    if l == 0:
                        pe.wait_ge(S(f"tables{layer}"), 160)
                    else:
                        pe.wait_ge(S("f_h"), 3 * layer + l)
                    pe.matmul(PS[0:FH, 7, 0:TX], FW[l][:, :], ZF[:, :] if l == 0 else HA[:, l - 1, :], start=True, stop=True)\
                      .then_inc(S("f_mm"), 1)

                def taps(t):
                    if t == 0:
                        pe.wait_ge(S("f_h"), 3 * layer + 3)
                        pe.wait_ge(S("n_std"), 9 + 2 * layer)
                    else:
                        pe.wait_ge(S("f_dec"), 4 * layer + 2)
                    for r in range(2):
                        last = pe.matmul(PS[:, 6 + r, :], HA[:, 2, t * P:t * P + P], FW4[:, r * HW:r * HW + HW],
                                         start=True, stop=True)
                    last.then_inc(S("f_taps"), 1)

                def spectrum(half):
                    if half == 0:
                        pe.wait_ge(S("f_dec"), 4 * layer + 4)
                    else:
                        pe.wait_ge(S("f_kc"), 3 * layer + 2)
                    for ct in (2 * half, 2 * half + 1):
                        for r in range(2):
                            for t in range(2):
                                last = pe.matmul(PS[:, 6 + ct % 2, :], DFT[:, r, t, ct * P:ct * P + P], HF[:, t, r, :],
                                                 start=r + t == 0, stop=r + t == 2)
                    last.then_inc(S("f_k"), 1)

                norm_sums(8 + 2 * layer, 4, SQ2)
                beside = [lambda: network(0), lambda: network(1), lambda: network(2), lambda: taps(0), lambda: taps(1),
                          lambda: spectrum(0)]
                for q in range(6):
                    n = TB if layer == 0 or q >= 4 else TX
                    if q >= RING:
                        pe.wait_ge(S("qkv_ev"), 6 * layer + q - RING + 1)
                    out = ring2(q, n)
                    by_columns(None, FIRST[f"qkv{layer}"] + q, [out[:, 0, :], out[:, 1, :]], AHI2, ALO2, n,
                               ready=wait_k("act_lo", KT * (5 + 2 * layer)) if q == 0 else None)
                    beside[q]()

                tq = nt // P

                def key_sums():
                    pe.wait_ge(S("h_sq"), 5 * layer + 1)
                    pe.wait_ge(S("f_fix"), 2 * layer + 2)
                    for kv in range(2):
                        last = pe.matmul(PS[:, 6 + kv, :], ONES[:, :], HSQ[:, kv, :], start=True, stop=True)
                    last.then_inc(S("h_ss"), 1)

                def query_sums(pair):
                    pe.wait_ge(S("h_sq"), 5 * layer + pair + 2)
                    for h in (2 * pair, 2 * pair + 1):
                        for t in range(tq):
                            last = pe.matmul(PS[:, 6, h * tq + t:h * tq + t + 1], HSQ[:, h % 2, t * P:t * P + P], ONES[:, 0:1],
                                             start=True, stop=True)
                    last.then_inc(S("h_ss"), 1)

                def rotate(r, tile):
                    if r == 0:
                        pe.wait_ge(S("h_kn"), 2 * layer + 2)
                    else:
                        pe.wait_ge(S("h_gain"), 4 * layer + r)
                        pe.wait_ge(S("h_sin"), 5 * layer + r)
                    for j in range(2):
                        last = pe.matmul(PS[:, 7, j * TX:j * TX + TX], ROT[:, :], QKV[:, tile + j, 0:TX], start=True, stop=True)
                    last.then_inc(S("h_rot"), 1)

                for q in range(6):
                    if q < RING:
                        pe.wait_ge(S("qkv_ev"), 6 * layer + q + RING + 1)
                    else:
                        pe.wait_ge(S("hy_taps"), 24 * layer + 4 * (q - RING + 1))
                    out = ring2(q, nt)
                    by_columns(None, FIRST[f"hy{layer}"] + q, [out[:, 0, :], out[:, 1, :]], AHI2, ALO2, nt)
                    if q == 0:
                        spectrum(1)
                    elif q == 1:
                        key_sums()
                    elif q == 2:
                        rotate(0, 8)
                    else:
                        query_sums(q - 3)
                        rotate(q - 2, 2 * (q - 3))
                query_sums(3)
                rotate(4, 6)

                groups = nt // TX

                def turned(grp):
                    pe.wait_ge(S("hy_v"), HT * (layer + 1))
                    pe.wait_ge(S("hy_taps"), 24 * (layer + 1))
                    if grp:
                        pe.wait_ge(S("y_vt"), 2 * layer + grp)
                    for t in range(2):
                        for m in range(HT):
                            last = pe.transpose(PS[:, t, m * P:m * P + P], HY[:, 8 + m, TX * grp + t * P:TX * grp + t * P + P],
                                                IDENT[:, :])
                    last.then_inc(S("y_tr"), 1)

                def forward(grp):
                    y = 2 * layer + grp
                    pe.wait_ge(S("y_vt"), y + 1)
                    if grp:
                        pe.wait_ge(S("y_mul"), 7 * y)
                    for ct in range(CTILES):
                        for t in range(2):
                            last = pe.matmul(PS[:, 2 + ct, :], DFT[:, 0, t, ct * P:ct * P + P], VTT[:, t, :], start=t == 0, stop=t == 1)
                    last.then_inc(S("y_fwd"), 1)

                def inverse(grp):
                    y = 2 * layer + grp
                    pe.wait_ge(S("y_mul"), 7 * y + 7)
                    if grp:
                        pe.wait_ge(S("y_h"), 8 * y)
                    for m in range(HT):
                        for ct in range(CTILES):
                            last = pe.matmul(PS[:, 6 + m // 2, m % 2 * TX:m % 2 * TX + TX], YS[:, ct, m * P:m * P + P], IDFT[:, ct, :],
                                             start=ct == 0, stop=ct == CTILES - 1)
                    last.then_inc(S("y_inv"), 1)

                turned(0)
                forward(0)
                if groups == 2:
                    turned(1)
                inverse(0)
                if groups == 2:
                    forward(1)
                    inverse(1)

                units = [(0, h) for h in range(NH2)] + ([(1, h) for h in range(NH2)] if layer == 0 else [])
                u0 = 2 * NH2 * layer

                def scores2(u):
                    grp, h = units[u]
                    if u >= 2:
                        pe.wait_ge(S("b_ex"), 2 * (u0 + u - 1))
                    for t in range(2):
                        q = QKV[:, h, TX * grp + t * P:TX * grp + t * P + P]
                        if grp == 0:
                            last = pe.matmul(PS[:, 2 * (u % 2) + t, :], q, QKV[:, 8 + h // 4, :], start=True, stop=True)
                        else:
                            last = pe.matmul(PS[:, 2 * (u % 2), TX * t:TX * t + TX], q, QKV[:, 8 + h // 4, TX:TB], start=True, stop=True)
                    last.then_inc(S("b_s"), 1)

                def values(u):
                    grp, h = units[u]
                    pe.wait_ge(S("b_pt"), u0 + u + 1)
                    if u >= 2:
                        pe.wait_ge(S("b_o"), u0 + u - 1)
                    kts = range(4) if grp == 0 else range(2, 4)
                    for a, kt in enumerate(kts):
                        last = pe.matmul(PS[:, 6 + u % 2, 0:TX], VT2[:, 2 * kt + h // 4, :], PT2[:, u % 2, a, :],
                                         start=a == 0, stop=a == len(kts) - 1)
                    last.then_inc(S("b_pv"), 1)

                y_done = 8 * (2 if layer == 0 else 3)
                pe.wait_ge(S("y_h"), y_done)
                pe.wait_ge(S("h_sum"), 5 * (layer + 1))
                scores2(0)
                for a in range(8):
                    last = pe.transpose(PS[:, 4 + a // 4, a % 4 * P:a % 4 * P + P], QKV[:, 10 + a % 2, a // 2 * P:a // 2 * P + P],
                                        IDENT[:, :])
                last.then_inc(S("v_tr"), 1)
                for u, (grp, h) in enumerate(units):
                    if u + 1 < len(units):
                        scores2(u + 1)
                    if u:
                        values(u - 1)
                    if u == 0:
                        pe.wait_ge(S("v_ev"), layer + 1)
                    pe.wait_ge(S("b_p"), 2 * (u0 + u) + 2)
                    for a in range(4 if grp == 0 else 2):
                        for t in range(2):
                            last = pe.transpose(PS[:, 4 + a // 2, a % 2 * TX + t * P:a % 2 * TX + t * P + P],
                                                PB[:, u % 2, t, a * P:a * P + P], IDENT[:, :])
                    last.then_inc(S("b_tr"), 1)
                values(len(units) - 1)

                for j in range(2):
                    if j == 0:
                        pe.wait_ge(S("b_o"), u0 + len(units))
                    outs = [PS[:, 4 * j + t, 0:nt] for t in range(4)]
                    by_columns(None, FIRST[f"oh{layer}"] + j, outs, HHI, HLO, nt, k_tiles=HT, width=4 * P,
                               ready=wait_k("hh_lo", HT * layer) if j == 0 else None)

                def mix(i, m):
                    c = FIRST[f"mix{layer}"] + 3 * m
                    for g, (hi, lo) in enumerate(((AHI2, ALO2), (AHI2, ALO2), (A2HI, A2LO))):
                        if m == 0:
                            if g == 0:
                                pe.wait_ge(S("oh_ev"), 2 * (layer + 1))
                            if g == 2:
                                pe.wait_ge(S("a2_lo"), KT * (layer + 1))
                        elif g < 2:
                            pe.wait_ge(S("gate"), lin(i, 2, 8 * layer + 2 * (m - 1) + g + 1))
                        else:
                            pe.wait_ge(S("merge"), lin(i, 3, 12 * layer + 3 * (m - 1) + 2))
                        out = ring2(g, nt)
                        by_columns(i, c + g, [out[:, 0, :], out[:, 1, :]], hi, lo, nt)
                mix(None, 0)
                with pe.Fori(0, 3) as i:
                    mix(i, 1)
                pe.wait_ge(S("merge"), 12 * (layer + 1))
                for j in range(4):
                    if j >= RING:
                        pe.wait_ge(S("xo"), 2 * KT * layer + 2 * (nt // TX))
                    out = ring2(j, nt)
                    by_columns(None, FIRST[f"out{layer}"] + j, [out[:, 0, :], out[:, 1, :]], AHI2, ALO2, nt,
                               ready=wait_k("mg_lo", KT * layer) if j == 0 else None)
                norm_sums(9 + 2 * layer, nt // P, SQ2)
                inst = 2 + layer

                def gate_up2(i, j, c):
                    if j >= RING:
                        pe.wait_ge(S("h"), lin(i, 3, FT * inst + j - RING + 1))
                    out = ring2(j, nt)
                    by_columns(i, c, [out[:, 0, :], out[:, 1, :]], AHI2, ALO2, nt,
                               ready=wait_k("act_lo", KT * (6 + 2 * layer)) if i is None and j == 0 else None)
                steps(pe, f"gu{layer}", gate_up2)
                pe.wait_ge(S("h"), FT * (inst + 1))
                down(f"dn{layer}", inst, SHI2, SLO2, nt)

            pe.wait_ge(S("xd"), 3 * KT)
            norm_sums(12, 2, SQ1)
            for t in range(2):
                for a in range(2):
                    for k in range(4 * a, 4 * a + 4):
                        pe.wait_ge(S("yf"), k + 1)
                        last = pe.transpose(PS[:, 2 * t + a, k % 4 * P:k % 4 * P + P], YF[:, k, t * P:t * P + P], IDENT[:, :])
                    last.then_inc(S("out_tr"), 1)


_NAMES = ["x", "p", "rel_bias", "ffn1_pre_g", "ffn1_w_gu", "ffn1_w_down", "ffn1_post_g", "attn_pre_g", "w_in", "b_in",
          "sinks", "w_out", "b_out", "attn_post_g", "ffn2_pre_g", "ffn2_w_gu", "ffn2_w_down", "ffn2_post_g",
          "ple_pre_g", "w_ple_gate", "w_ple_proj", "ple_post_g", "c_2", "ctx_2", "c_ctx_2", "w_mod_2", "b_mod_2",
          "norm_mix_2", "w_in_2", "q_norm_2", "k_norm_2", "conv_w_2", "conv_b_2", "filt_w1_2", "filt_b1_2",
          "filt_w2_2", "filt_b2_2", "filt_w3_2", "filt_b3_2", "filt_w4_2", "filt_freq_2", "hyena_bias_2",
          "w_o_attn_2", "w_o_hyena_2", "w_out_2", "norm_ffn_2", "w_gate_up_2", "w_down_2", "norm_final_2"]


def kernel(**inputs):
    import concourse.bacc as bacc
    from concourse.bass_utils import run_bass_kernel_spmd

    nc = bacc.Bacc("TRN2", target_bir_lowering=False, num_devices=1)
    tensors = {n: np.ascontiguousarray(inputs[n]) for n in _NAMES}
    tensors.update({f"{n}": a for n, a in shape_tables().items()})
    arrays, aps = {}, {}
    for name, a in tensors.items():
        arrays[f"in_{name}_dram"] = a
        aps[name] = nc.dram_tensor(f"in_{name}_dram", a.shape, mybir.dt.from_np(a.dtype), kind="ExternalInput").ap()
    aps["out"] = nc.dram_tensor("out_0_dram", (1, TX, D), F32, kind="ExternalOutput").ap()
    two_blocks_kernel(nc, aps)
    r = run_bass_kernel_spmd(nc, [arrays], core_ids=[0])
    return r.results[0]["out_0_dram"]
```

```python
from contextlib import ExitStack

import numpy as np

import concourse.bass as bass
from concourse import mybir

F32 = mybir.dt.float32
F32R = mybir.dt.float32r
ALU = mybir.AluOpType
ACT = mybir.ActivationFunctionType
AX = mybir.AxisListType

P = 128
D = 1024
KT = D // P
TX = 256
TB = 2 * TX
DFF = 2816
FT = DFF // P
EPS = 1e-6
CH = 2048
RING = 3
AHEAD = 2
DH1 = 64
NBKT = 32
DH2 = 128
NH2 = 8
HW = 512
HT = HW // P
FH = 64
FE = 33
CTILES = TB // P
MAGIC = 12582912.0
TWO_PI_HI = 6.28125
TWO_PI_LO = 2.0 * np.pi - 6.28125
PI_IN = 3.1415925



def t5_buckets(n):
    d = np.arange(n)
    nf = np.maximum(d, 1).astype(np.float32)
    exact = NBKT // 2
    large = exact + (np.log(nf / np.float32(exact)) / np.float32(np.log(2048 / exact)) * np.float32(NBKT - exact)).astype(np.int32)
    return np.where(d < exact, d, np.minimum(large, NBKT - 1))


def shape_tables():
    t = {}
    t["ident"] = np.eye(P, dtype=np.float32)
    dist = np.arange(384) - 127
    bucket = t5_buckets(TX)
    onehot = np.zeros((NBKT, 384), np.float32)
    mask = np.full((16, 384), -1e30, np.float32)
    for i, d in enumerate(dist):
        if d < 0 or d >= TX:
            continue
        onehot[bucket[d], i] = 1.0
        if d <= 127:
            mask[:8, i] = 0.0
        count = int(d <= 128) + int(d % 4 == 0) + int(d % 16 == 0)
        if count:
            mask[8:, i] = np.log(count)
    t["onehot"], t["mask"] = onehot, mask
    row = np.repeat(np.arange(TX // 64, dtype=np.float32), 64)
    col = np.tile(np.arange(64, dtype=np.float32), TX // 64)
    inv = (np.float32(10000.0) ** (-np.arange(0, 64, 2, dtype=np.float32) / np.float32(64))).astype(np.float32)
    ang = np.concatenate([row[:, None] * inv, col[:, None] * inv], axis=-1)
    cs = np.stack([np.repeat(np.cos(ang), 2, axis=1).T, np.repeat(np.sin(ang), 2, axis=1).T], axis=1)
    t["rope"] = np.ascontiguousarray(cs.astype(np.float32))
    rot = np.zeros((P, P), np.float32)
    for i in range(0, P, 2):
        rot[i + 1, i] = -1.0
        rot[i, i + 1] = 1.0
    t["rot"] = rot
    lin = np.linspace(0.0, 1.0, TX, dtype=np.float32)[:, None]
    w = np.float32(2.0 * np.pi / TX) * np.arange(TX, dtype=np.float32)[:, None]
    f = np.linspace(1e-4, 15, 16, dtype=np.float32)[None, :]
    t["zfeat"] = np.ascontiguousarray(np.concatenate([lin, np.cos(f * w), -np.sin(f * w)], axis=-1).T.astype(np.float32))
    lo_, hi_ = np.log(1e-2) / 1.5, np.log(1e-2) / 0.3
    deltas = np.abs(np.linspace(lo_, hi_, HW, dtype=np.float32))
    t["decay"] = np.exp(-lin * deltas).astype(np.float32)
    n, k = np.arange(TX)[:, None].astype(np.float64), np.arange(TX)[None, :].astype(np.float64)
    ph = 2 * np.pi * n * k / TB
    alt = (-1.0) ** n
    fwd = np.concatenate([np.cos(ph), alt, -np.sin(ph)[:, 1:]], axis=1)
    bwd = np.concatenate([np.cos(ph), alt, np.sin(ph)[:, 1:]], axis=1)
    bwd[0] = 0.0
    scale = np.full((TX, 1), 2.0 / TB)
    scale[0] = 1.0 / TB
    im = -np.sin(ph).T * (2.0 / TB)
    im[0] = alt[:, 0] / TB
    t["dft"] = np.stack([fwd, bwd]).astype(np.float32)
    t["idft"] = np.concatenate([np.cos(ph).T * scale, im], axis=0).astype(np.float32)
    return t



def param_rows():
    tiles = [
        [("ffn1_pre_g", 8), ("ffn1_post_g", 8), ("attn_pre_g", 8), ("attn_post_g", 8), ("ffn2_pre_g", 8),
         ("ffn2_post_g", 8), ("ple_pre_g", 8), ("ple_post_g", 8), ("b_out", 8), ("b_in", 18),
         ("norm_mix_2", 16), ("norm_final_2", 8), ("q_norm_2", 2), ("k_norm_2", 2)],
        [("b_mod_2", 96), ("norm_ffn_2", 16), ("hyena_bias_2", 8)],
        [("conv_w_2", 72), ("conv_b_2", 24), ("c_2", 8), ("c_ctx_2", 8)],
        [("filt_b1_2", 2), ("filt_b2_2", 2), ("filt_b3_2", 2), ("filt_freq_2", 6)],
    ]
    at, used = {}, []
    for g, names in enumerate(tiles):
        row = 0
        for name, rows in names:
            at[name] = (g, row, rows)
            row += rows
        used.append(row)
    return at, used


PAR_AT, PAR_USED = param_rows()


STAGES = [("ffn1_gu", FT), ("ffn1_dn", FT // 2), ("b1_in", 9), ("b1_out", 4),
          ("ffn2_gu", FT), ("ffn2_dn", FT // 2), ("ple_proj", 1), ("ple_gate", 4)]
for _l in range(2):
    STAGES += [(f"qkv{_l}", 6), (f"hy{_l}", 6), (f"oh{_l}", 2), (f"mix{_l}", 12), (f"out{_l}", 4),
               (f"gu{_l}", FT), (f"dn{_l}", FT // 2)]
FIRST, TOTAL = {}, 0
for _name, _n in STAGES:
    FIRST[_name] = TOTAL
    TOTAL += _n
CHUNKS = dict(STAGES)
STAT_BANK = [0, 4, 0, 0, 0, 4, 3, 3, 6, 6, 0, 6, 6]
MODC = 24


def lin(i, step, const):
    return const if i is None else i * step + const


def steps(eng, stage, body, tail=0):
    n, c0 = CHUNKS[stage], FIRST[stage]
    head = 3 + (n - 3 - tail) % 3
    turns = (n - head - tail) // 3
    if turns < 2:
        head, turns, tail = n, 0, 0
    for j in range(head):
        body(None, j, c0 + j)
    if turns:
        with eng.Fori(0, turns) as i:
            for u in range(3):
                body(i, head + u, c0 + head + u)
    for j in range(n - tail, n):
        body(None, j, c0 + j)


def two_blocks_kernel(nc, d):
    with ExitStack() as ctx:
        sems = {}

        def S(name):
            if name not in sems:
                sems[name] = ctx.enter_context(nc.semaphore(name))
            return sems[name]

        K = 1024
        slab = 207 * K + 768
        nc.alloc_sbuf_tensor("slab", [P, slab // 4], F32)
        base = nc.sbuf_base - slab

        def at(name, shape, off, dt=F32):
            assert off + 4 * int(np.prod(shape[1:])) <= slab, name
            return nc.alloc_sbuf_tensor_at(name, shape, dt, offset=base + off)

        X = at("X", [P, KT, TB], 0)
        RAW = at("RAW", [P, RING, CH], 16 * K)
        WHI = at("WHI", [P, RING, CH], 40 * K, F32R)
        WLO = at("WLO", [P, RING, CH], 64 * K, F32R)
        AHI1, ALO1 = at("AHI1", [P, KT, TX], 88 * K, F32R), at("ALO1", [P, KT, TX], 104 * K, F32R)
        AHI2, ALO2 = at("AHI2", [P, KT, TB], 88 * K, F32R), at("ALO2", [P, KT, TB], 104 * K, F32R)
        BIAS = [at("BIAS0", [P, 8, TX], 96 * K), at("BIAS1", [P, 8, TX], 112 * K)]
        SHI1, SLO1 = at("SHI1", [P, RING, 2, TX], 120 * K, F32R), at("SLO1", [P, RING, 2, TX], 132 * K, F32R)
        SHI2, SLO2 = at("SHI2", [P, RING, 2, TB], 120 * K, F32R), at("SLO2", [P, RING, 2, TB], 132 * K, F32R)
        REL, ONEHOT = at("REL", [NBKT, 16], 126 * K), at("ONEHOT", [NBKT, 384], 127 * K)
        MASK, EXT = at("MASK", [16, 384], 138 * K), at("EXT", [16, 384], 140 * K)
        PHI, PLO = at("PHI", [P, 2, TX], 130 * K, F32R), at("PLO", [P, 2, TX], 142 * K, F32R)
        DFT = at("DFT", [P, 2, 2, TB], 120 * K)
        IDFT = at("IDFT", [P, CTILES, TX], 128 * K)
        KR = at("KR", [P, 2, 2, TX], 132 * K)
        KIZ = at("KIZ", [P, 2, 2, TX], 136 * K)
        KRX = at("KRX", [P, 2, TX], 140 * K)
        ROT = at("ROT", [P, P], 142 * K)
        HHI, HLO = at("HHI", [P, HT, TB], 120 * K, F32R), at("HLO", [P, HT, TB], 132 * K, F32R)
        A = 144 * K
        XS, CS, PST = at("XS", [P, 2, D], A), at("CS", [P, 2, D], A + 8 * K), at("PST", [P, 2, TX], A + 16 * K)
        GS = at("GS", [P, 4, P], A + 18 * K)
        HB1, HB2 = at("HB1", [P, FT, TX], A), at("HB2", [P, FT, TB], A)
        MRAW, MLO = at("MRAW", [P, RING, CH // 2], A + 24 * K), at("MLO", [P, RING, CH // 2], A + 24 * K, F32R)
        MHI = at("MHI", [P, RING, CH // 2], A + 36 * K, F32R)
        MROW = at("MROW", [4, 2 * P], 129 * K)
        SQ1, SQ2 = at("SQ1", [P, KT, TX], A), at("SQ2", [P, KT, TB], A)
        FB, TU = at("FB", [P, KT, TX], A + 8 * K), at("TU", [P, KT, TX], A + 16 * K)
        PG = at("PG", [P, KT, TX], A + 16 * K)
        Z = at("Z", [P, 18, TX], A)
        VT1 = at("VT1", [P, 10, P], A + 18 * K)
        KS = at("KS", [P, TX], A + 23 * K)
        SB1 = [at(f"SB1{i}", [P, 4, TX], A + (24 + 6 * i) * K) for i in range(2)]
        SB0 = [at(f"SB0{i}", [P, 4, P], A + (28 + 6 * i) * K) for i in range(2)]
        PT1 = [at(f"PT1{i}", [P, 4, 3 * P], A + (36 + 6 * i) * K) for i in range(2)]
        QKV = at("QKV", [P, 12, TB], A)
        VT2 = at("VT2", [P, 8, P], A + 24 * K)
        HSQ = at("HSQ", [P, 2, TB], 192 * K)
        PB = at("PB", [P, 2, 2, TB], A + 32 * K)
        PT2 = at("PT2", [P, 2, 4, TX], A + 40 * K)
        BR = at("BR", [P, 2, TX], 196 * K)
        ROPE = at("ROPE", [P, 2, TX], 198 * K)
        FW4, DEC = at("FW4", [FH, 2 * HW], A + 36 * K), at("DEC", [P, 2, HW], A + 32 * K)
        HF = at("HF", [P, 2, 2, HW], A + 40 * K)
        ZF = at("ZF", [FE, TX], 192 * K)
        FW = [at(f"FW{i}", [FE if i == 0 else FH, FH], 193 * K + 256 * i) for i in range(3)]
        FU = at("FU", [FH, 4, TX], A + 24 * K)
        HA = at("HA", [FH, 3, TX], A + 28 * K)
        HY = at("HY", [P, 12, TB], A + 24 * K)
        YS = at("YS", [P, 2, CTILES, TX], A + 32 * K)
        VTT = at("VTT", [P, 2, HW], 124 * K)
        A2HI, A2LO = at("A2HI", [P, KT, TB], A + 16 * K, F32R), at("A2LO", [P, KT, TB], A + 32 * K, F32R)
        MG = at("MG", [P, KT, TB], A)
        YF, OUTS = at("YF", [P, KT, TX], A + 16 * K), at("OUTS", [P, 2, D], A + 24 * K)
        GU = at("GU", [P, RING, 2, TX], 192 * K)
        SIL = at("SIL", [P, RING, TB], 192 * K)
        SG = at("SG", [P, 2, 2, TB], 192 * K)
        YT1, YT2 = at("YT1", [P, 2, 2, TX], 192 * K), at("YT2", [P, 2, 2, TX], 196 * K)
        P32 = at("P32", [P, 2, TX], 198 * K)
        RT = at("RT", [P, TB], 200 * K)
        PAR = at("PAR", [P, 4, P], 202 * K)
        IDENT, ONES = at("IDENT", [P, P], 204 * K), at("ONES", [P, P], 204 * K + 512)
        small = [205 * K]

        def sm(name, shape):
            t = at(name, shape, small[0])
            small[0] += (4 * int(np.prod(shape[1:])) + 31) // 32 * 32
            return t

        MOD = sm("MOD", [P, 2, 48, 2])
        GM = sm("GM", [P, 2, 2, 8, 2])
        HG = sm("HG", [P, 2, 8])
        SC = sm("SC", [P, 8, 2])
        SCR = at("SCR", [P, 8, 4], small[0], F32R)
        small[0] += 128
        MSUM = sm("MSUM", [P, 48, 4])
        STD, RC = sm("STD", [P, 40]), sm("RC", [P, 40])
        NM, SMX, RS = sm("NM", [P, 2, 8]), sm("SMX", [P, 2, 8]), sm("RS", [P, 2, 8])
        SINK, SE = sm("SINK", [P, 2, 8]), sm("SE", [P, 2, 8])
        EPSC = sm("EPSC", [P, 2])

        PS = ctx.enter_context(nc.psum_tensor("PS", [P, 8, 512], F32))
        bias_rows = nc.dram_tensor("bias_rows", (16, 384), F32).ap()

        def par(name, first=0, n=1):
            g, row, rows = PAR_AT[name]
            return PAR[:, g, row + first:row + first + n]

        def over_tokens(ap, n):
            return ap.unsqueeze(2).broadcast_to([P, ap.shape[1], n])

        def over_tiles(ap, n):
            return ap.unsqueeze(1).broadcast_to([P, n, ap.shape[1]])

        def ring1(j):
            return PS[:, 4 + j % 3, :].rearrange("p (t n) -> p t n", t=2)

        def projected(b):
            return PS[:, (5, 6, 7, 4)[b], :].rearrange("p (t n) -> p t n", t=2)

        def ringp(j):
            return PS[:, j % 3, :].rearrange("p (t n) -> p t n", t=2)

        def ring2(j, n):
            s = 2 * (j % 3)
            return PS[:, s:s + 2, :] if n == TB else PS[:, s, :].rearrange("p (t n) -> p t n", t=2)

        def acc(m, n):
            return PS[:, m, :] if n == TB else PS[:, m // 2, m % 2 * TX:m % 2 * TX + TX]

        def stat_row(n_norm, t):
            return PS[:, STAT_BANK[n_norm], 0:P * t]

        def load_rows(eng, name):
            g, row, rows = PAR_AT[name]
            src = d[name]
            dims = " ".join("abc"[:len(src.shape)])
            flat = src.rearrange(f"{dims} -> ({dims})") if len(src.shape) > 1 else src
            width = FH if g == 3 else P
            eng.dma_start(GS[row:row + rows, g, 0:width], flat.rearrange("(r n) -> r n", n=width)).then_inc(S(f"in_par{g}"), 16)

        block = ctx.enter_context(nc.Block())

        @block.sync
        def _(sp):
            def load(i, c, src, dst, half=lambda ap, t: ap[:, t * (ap.shape[1] // 2):(t + 1) * (ap.shape[1] // 2), :]):
                if c >= RING:
                    sp.wait_ge(S("lo_done"), lin(i, 3, c - RING + 1))
                for t in range(2):
                    sp.dma_start(half(dst(RAW[:, c % RING, :]), t), half(src, t)).then_inc(S(f"raw{c % RING}"), 16)

            def cols(w, n_first, k=KT, width=2 * P):
                return w.rearrange("(k p) n -> p k n", p=P)[:, :, bass.ds(n_first, width)]

            def by_k(k):
                return lambda r: r.rearrange("p (k n) -> p k n", k=k)

            def mod_load(layer, i, half):
                if half < 0:
                    return
                t = 2 * MODC * layer + half
                if t >= RING:
                    if half == 0:
                        sp.wait_ge(S("act_lo"), 3 * KT)
                    sp.wait_ge(S("mod_used"), lin(i, 6, t - RING + 1))
                k = 4 * (half % 2)
                src = cols(d["w_mod_2"][layer], lin(i, 3 * 2 * P, half // 2 * 2 * P))[:, k:k + 4, :]
                sp.dma_start(MRAW[:, t % RING, :].rearrange("p (k n) -> p k n", k=4), src)\
                  .then_inc(S(f"mod_raw{t % RING}"), 16)

            def gate_up(stage, w, layer=None):
                view = w.rearrange("(k p) (t n) -> p k t n", p=P, t=2)

                def body(i, j, c):
                    if c == 1:
                        sp.wait_ge(S("in_par0"), 16 * sum(at[0] == 0 for at in PAR_AT.values()))
                    load(i, c, view[:, :, :, bass.ds(lin(i, 3 * P, j * P), P)],
                         lambda r: r.rearrange("p (k t n) -> p k t n", k=KT, t=2), lambda ap, t: ap[:, :, t, :])
                    if layer == 0 and i is None and j == 1:
                        sp.dma_start(PST[:, :, :], d["p"][0, 0].rearrange("(t p) n -> p t n", p=P)).then_inc(S("in_p"), 16)
                        sp.dma_start(CS[:, :, :], d["ctx_2"][0].rearrange("(t p) n -> p t n", p=P)).then_inc(S("in_ctx"), 16)
                    if layer is not None:
                        mod_load(layer, i, 2 * j - 3)
                        mod_load(layer, i, 2 * j - 2)
                steps(sp, stage, body)

            def down(stage, w, layer=None):
                view = w.rearrange("(k p) n -> p k n", p=P)

                def body(i, j, c):
                    load(i, c, view[:, bass.ds(lin(i, 6, 2 * j), 2), :], by_k(2))
                    if layer is not None and i is None and j < 3:
                        for half in range(2 * (FT + j) - 3, 2 * (FT + j) - 1 if j < 2 else 2 * MODC):
                            mod_load(layer, None, half)
                steps(sp, stage, body, tail=2)

            def plain(stage, w, first=0):
                steps(sp, stage, lambda i, j, c: load(i, c, cols(w, lin(i, 6 * P, first + 2 * P * j)), by_k(KT)))

            def tables(layer):
                if layer == 0:
                    sp.wait_ge(S("xu"), 4 * KT)
                else:
                    sp.wait_ge(S("xd"), 2 * KT)
                sp.wait_ge(S("pe_done"), FIRST[f"qkv{layer}"])
                for dst, src in ((FW[0][:, :], d["filt_w1_2"][layer]), (ZF[:, :], d["zfeat"]),
                                 (FW[1][:, :], d["filt_w2_2"][layer]), (FW[2][:, :], d["filt_w3_2"][layer]),
                                 (FW4[:, :], d["filt_w4_2"][layer]), (DEC[:, :, :], d["decay"].rearrange("(t p) n -> p t n", p=P)),
                                 (DFT[:, :, :, :], d["dft"].rearrange("r (t p) n -> p r t n", p=P)),
                                 (IDFT[:, :, :], d["idft"].rearrange("(t p) n -> p t n", p=P)),
                                 (ROPE[:, :, :], d["rope"]), (ROT[:, :], d["rot"])):
                    sp.dma_start(dst, src).then_inc(S(f"tables{layer}"), 16)

            sp.dma_start(IDENT[:, :], d["ident"]).then_inc(S("in_ident"), 16)
            sp.dma_start(XS[:, :, :], d["x"][0].rearrange("(t p) n -> p t n", p=P)).then_inc(S("in_x"), 16)
            gate_up("ffn1_gu", d["ffn1_w_gu"][0], 0)
            down("ffn1_dn", d["ffn1_w_down"][0], 0)
            plain("b1_in", d["w_in"][0])
            plain("b1_out", d["w_out"][0])
            gate_up("ffn2_gu", d["ffn2_w_gu"][0], 1)
            down("ffn2_dn", d["ffn2_w_down"][0], 1)
            load(None, FIRST["ple_proj"], d["w_ple_proj"][0].rearrange("(k p) n -> p k n", p=P), by_k(2))
            plain("ple_gate", d["w_ple_gate"][0])
            for layer in range(2):
                win = d["w_in_2"][layer]
                for j in range(6):
                    load(None, FIRST[f"qkv{layer}"] + j, cols(win, 2 * P * j), by_k(KT))
                    if j == 2:
                        tables(layer)
                plain(f"hy{layer}", win, 12 * P)
                woh = d["w_o_hyena_2"][layer].rearrange("(k p) n -> p k n", p=P)
                for j in range(2):
                    load(None, FIRST[f"oh{layer}"] + j, woh[:, :, 512 * j:512 * j + 512], by_k(HT))

                def mix(i, m):
                    c = FIRST[f"mix{layer}"] + 3 * m
                    n = lin(i, 2 * P, 2 * P * m)
                    load(i, c, cols(win, n + 32 * P), by_k(KT))
                    load(i, c + 1, cols(win, n + 24 * P), by_k(KT))
                    load(i, c + 2, cols(d["w_o_attn_2"][layer], n), by_k(KT))
                mix(None, 0)
                with sp.Fori(0, 3) as i:
                    mix(i, 1)
                plain(f"out{layer}", d["w_out_2"][layer])
                gate_up(f"gu{layer}", d["w_gate_up_2"][layer])
                down(f"dn{layer}", d["w_down_2"][layer])
            for t in range(2):
                sp.wait_ge(S("out_ev0"), t + 1)
                sp.wait_ge(S("out_ev1"), t + 1)
                sp.dma_start(d["out"][0, P * t:P * t + P, :], OUTS[:, t, :]).then_inc(S("out_dma"), 16)
            sp.wait_ge(S("out_dma"), 32)

        @block.gpsimd
        def _(pool):
            def small_load(g):
                for name in PAR_AT:
                    if PAR_AT[name][0] == g:
                        load_rows(pool, name)
            small_load(2)
            small_load(1)
            pool.wait_ge(S("gs_clear"), 1)
            small_load(3)
            for dst, src in ((REL[:, :], d["rel_bias"]), (ONEHOT[:, :], d["onehot"]), (MASK[:, :], d["mask"])):
                pool.dma_start(dst, src).then_inc(S("in_bias"), 16)
            pool.dma_start(SINK[:, 0, :], d["sinks"].broadcast_to([P, 8])).then_inc(S("in_sink"), 16)

            def add_squares(count, n_norm):
                pool.wait_ge(S("n_sq"), KT * (n_norm + 1))
                for r, w in enumerate((4, 2, 1)):
                    if r:
                        pool.wait_ge(S("n_pre"), 3 * count + r)
                    pool.tensor_tensor(SQ1[:, 0:w, :], SQ1[:, 0:w, :], SQ1[:, w:2 * w, :], ALU.add).then_inc(S("n_pre"), 1)

            add_squares(0, 0)
            pool.wait_ge(S("ext_ev"), 1)
            pool.dma_start(bias_rows, EXT[:, :]).then_inc(S("bias_out"), 16)
            pool.wait_ge(S("bias_out"), 16)
            for b in range(2):
                src = bass.AP(tensor=bias_rows.tensor, offset=8 * b * 384, ap=[[1, P], [384, 8], [1, TX]])
                pool.dma_start(BIAS[b][:, :, :], src).then_inc(S("bias_in"), 16)

            def x_update(u):
                for k in range(KT):
                    pool.wait_ge(S("xt"), KT * u + k + 1)
                    pool.tensor_tensor(X[:, k, 0:TX], X[:, k, 0:TX], TU[:, k, :], ALU.add).then_inc(S("xu"), 1)

            def ctx_over_rms(inst):
                pool.wait_ge(S("n_rtc"), inst + 1)
                for k in range(KT):
                    pool.tensor_tensor(SQ2[:, k, TX:TB], X[:, k, TX:TB], RT[:, TX:TB], ALU.mult).then_inc(S("xrc"), 1)

            x_update(0)
            add_squares(1, 2)
            pool.wait_ge(S("zt"), 6)
            for h in range(2):
                pool.dma_start(KS[64 - 64 * h:128 - 64 * h, :], Z[64 * h:64 * h + 64, 4, :]).then_inc(S("ks"), 16)
            for g in range(4):
                pool.wait_ge(S("a_rs"), g + 1)
                s = g % 2
                pool.tensor_tensor(SB0[s][:, :, :], SB0[s][:, :, :], over_tokens(RS[:, s, 4:8], P), ALU.mult).then_inc(S("a_p0"), 1)
            x_update(1)
            add_squares(2, 4)
            x_update(2)
            add_squares(3, 6)
            x_update(3)
            for layer in range(2):
                ctx_over_rms(2 * layer)
                pool.wait_ge(S(f"tables{layer}"), 160)
                for r, j in enumerate((8, 0, 2, 4, 6)):
                    pool.wait_ge(S("h_rot"), 5 * layer + r + 1)
                    pool.tensor_tensor(QKV[:, j:j + 2, 0:TX], QKV[:, j:j + 2, 0:TX], over_tiles(ROPE[:, 0, :], 2), ALU.mult)\
                        .then_inc(S("h_cos"), 1)
                if layer == 0:
                    ctx_over_rms(1)

        @block.scalar
        def _(act):
            def split_w(i, c):
                if c >= TOTAL:
                    return
                act.wait_ge(S(f"raw{c % RING}"), lin(i, 32, 32 * (c // RING + 1)))
                if c >= RING:
                    act.wait_ge(S("pe_done"), lin(i, 3, c - RING + 1))
                act.activation(WHI[:, c % RING, :], RAW[:, c % RING, :], ACT.Copy).then_inc(S("hi_done"), 1)

            def split_h(i, inst, stage, j, hb, shi, n):
                act.wait_ge(S("h"), lin(i, 6, FT * inst + 2 * j + 2))
                if j >= RING:
                    act.wait_ge(S("pe_done"), lin(i, 3, FIRST[stage] + j - RING + 1))
                act.activation(shi[:, j % RING, :, 0:n], hb[:, bass.ds(lin(i, 6, 2 * j), 2), 0:n], ACT.Copy)\
                   .then_inc(S("hs_hi"), 1)

            def first_hidden(inst, hb, shi, n):
                for j in range(AHEAD):
                    split_h(None, inst, None, j, hb, shi, n)

            def mod_hi(layer, i, half):
                if half >= 2 * MODC:
                    return
                t = 2 * MODC * layer + half
                act.wait_ge(S(f"mod_raw{t % RING}"), lin(i, 32, 16 * (t // RING + 1)))
                act.activation(MHI[:, t % RING, :], MRAW[:, t % RING, :], ACT.Copy).then_inc(S("mod_hi"), 1)

            def mod_cols(layer, i, g):
                act.wait_ge(S("mod_tr"), lin(i, 3, MODC * layer + g + 1))
                act.activation(MSUM[:, bass.ds(lin(i, 6, 2 * g), 2), :], PS[:, 7, 0:8].rearrange("p (t v) -> p t v", t=2),
                               ACT.Copy).then_inc(S("mod_col"), 1)

            def mod_rows(layer, i, g):
                act.wait_ge(S("mod_used"), lin(i, 6, 2 * (MODC * layer + g) + 2))
                act.activation(MROW[:, :], PS[0:4, 7, TX:TB], ACT.Copy).then_inc(S("mod_row"), 1)

            def down(stage, inst, hb, shi, n):
                def body(i, j, c):
                    mods = inst < 2 and i is None
                    if mods and j < MODC - FT:
                        mod_hi(inst, None, 2 * (FT + j) + 1)
                    split_w(i, c + AHEAD)
                    if mods and j <= MODC - FT:
                        mod_cols(inst, None, FT + j - 1)
                    if i is not None or j + AHEAD < FT // 2:
                        split_h(i, inst, stage, j + AHEAD, hb, shi, n)
                    if mods and j < MODC - FT:
                        mod_hi(inst, None, 2 * (FT + j) + 2)
                        mod_rows(inst, None, FT + j)
                steps(act, stage, body, tail=2)

            def norm_std(n_norm, t):
                act.wait_ge(S("n_ss"), n_norm + 1)
                act.activation(RT[:, 0:P * t], stat_row(n_norm, t), ACT.Sqrt, scale=1.0 / D, bias=EPSC[:, 0:1])\
                   .then_inc(S("n_std"), 1)

            def squares(src, dst, ready):
                for k in range(KT):
                    ready(k)
                    act.activation(dst(k), src(k), ACT.Square).then_inc(S("n_sq"), 1)

            def gained(name, ready):
                for k in range(KT):
                    ready(k)
                    act.activation(AHI1[:, k, :], X[:, k, 0:TX], ACT.Identity, scale=par(name, k)).then_inc(S("act_hi"), 1)
                for k in range(0, KT, 4):
                    act.activation(SQ1[:, k:k + 4, :], X[:, k:k + 4, 0:TX], ACT.Square).then_inc(S("n_sq"), 4)

            def silus1(stage, inst, pre):
                if inst == 0:
                    mod_hi(0, None, 0)

                def body(i, j, c):
                    if i is None and j == FT - 1:
                        first_hidden(inst, HB1, SHI1, TX)
                    if j == 0:
                        mod_hi(inst, i, 1)
                        split_w(i, c + AHEAD)
                    else:
                        split_w(i, c + AHEAD)
                        mod_cols(inst, i, j - 1)
                        mod_hi(inst, i, 2 * j + 1)
                    mod_hi(inst, i, 2 * j + 2)
                    if i is None and j == 0:
                        norm_std(pre, 2)
                    act.wait_ge(S("gu"), lin(i, 3, FT * inst + j + 1))
                    act.activation(GU[:, j % RING, 0, :], GU[:, j % RING, 0, :], ACT.Silu).then_inc(S("sil"), 1)
                    mod_rows(inst, i, j)
                    if inst == 0 and i is None and j == 0:
                        act.wait_ge(S("p_ev"), 1)
                        act.activation(PHI[:, :, :], P32[:, :, :], ACT.Copy).then_inc(S("p_hi"), 1)
                steps(act, stage, body, tail=1)

            for name in PAR_AT:
                if PAR_AT[name][0] == 0:
                    load_rows(act, name)

            for b in range(4):
                act.wait_ge(S("tr_x"), b + 1)
                act.activation(X[:, 2 * b:2 * b + 2, 0:TX], PS[:, b, :].rearrange("p (t n) -> p t n", t=2), ACT.Copy)\
                   .then_inc(S("x_ev"), 1)
            split_w(None, 0)
            act.wait_ge(S("par_ev"), 1)
            gained("ffn1_pre_g", lambda k: act.wait_ge(S("x_ev"), k // 2 + 1))
            act.wait_ge(S("par_ev"), 2)
            for v, name in enumerate(("c_2", "c_ctx_2")):
                act.activation(SC[:, :, v], par(name, 0, 8), ACT.Silu).then_inc(S("sc"), 1)
            act.wait_ge(S("sc"), 2)
            act.activation(SCR[:, :, 0:2], SC[:, :, :], ACT.Copy).then_inc(S("sc_hi"), 1)
            split_w(None, 1)

            for inst, (pre, post) in enumerate(((0, 1), (4, 5))):
                f = f"ffn{inst + 1}"
                silus1(f + "_gu", inst, pre)
                down(f + "_dn", inst, HB1, SHI1, TX)
                act.wait_ge(S("pe_done"), FIRST[f + "_dn"] + FT // 2)
                squares(lambda k: acc(k, TX), lambda k: SQ1[:, k, :], lambda k: None)
                norm_std(post, 2)
                if inst == 1:
                    break
                gained("attn_pre_g", lambda k: act.wait_ge(S("xu"), k + 1))

                def project(i, j, c):
                    split_w(i, c + AHEAD)
                    if i is None and j == 0:
                        norm_std(2, 2)
                steps(act, "b1_in", project)

                def keys_out(g):
                    act.wait_ge(S("a_tr"), g + 1)
                    act.activation(PT1[g % 2][:, :, :], PS[:, 3:7, 0:3 * P], ACT.Copy).then_inc(S("a_pt"), 1)

                def mixed_hi(g):
                    act.wait_ge(S("a_pv"), g + 1)
                    act.activation(AHI1[:, 2 * g:2 * g + 2, :], PS[:, 7, :].rearrange("p (t n) -> p t n", t=2), ACT.Copy)\
                       .then_inc(S("act_hi"), 2)
                for g in range(4):
                    s = g % 2
                    act.wait_ge(S("a_nm"), g + 1)
                    for b in range(8):
                        src = SB1[s][:, b, :] if b < 4 else SB0[s][:, b - 4, :]
                        act.activation(src, src, ACT.Exp, bias=NM[:, s, b:b + 1], accum_out=SMX[:, s, b:b + 1])\
                           .then_inc(S("a_ex"), 1)
                    if g < 2:
                        act.wait_ge(S("a_se0"), g + 1)
                        act.activation(SE[:, g, :], SE[:, g, :], ACT.Exp).then_inc(S("a_sink"), 1)
                    if g >= 2:
                        mixed_hi(g - 2)
                    if g >= 1:
                        keys_out(g - 1)
                mixed_hi(2)
                keys_out(3)
                mixed_hi(3)
                for j in range(4):
                    split_w(None, FIRST["b1_out"] + j + AHEAD)
                mod_hi(1, None, 0)
                squares(lambda k: FB[:, k, :], lambda k: SQ1[:, k, :], lambda k: act.wait_ge(S("f_ev"), k // 2 + 1))
                norm_std(3, 2)
                gained("ffn2_pre_g", lambda k: act.wait_ge(S("xu"), KT + k + 1))

            gained("ple_pre_g", lambda k: act.wait_ge(S("xu"), 2 * KT + k + 1))
            split_w(None, FIRST["ple_proj"] + AHEAD)

            def embedded_squares(j):
                act.wait_ge(S("f_ev"), 4 + j + 1)
                act.activation(SQ1[:, 2 * j:2 * j + 2, :], FB[:, 2 * j:2 * j + 2, :], ACT.Square).then_inc(S("n_sq"), 2)
            for j in range(4):
                if j < 3:
                    split_w(None, FIRST["ple_gate"] + j + AHEAD)
                if j == 0:
                    norm_std(6, 2)
                act.wait_ge(S("pg"), j + 1)
                act.activation(PG[:, 2 * j:2 * j + 2, :], GU[:, j % RING, :, :], ACT.Sigmoid).then_inc(S("pg_sig"), 1)
                if j:
                    embedded_squares(j - 1)
            embedded_squares(3)
            norm_std(7, 2)
            split_w(None, FIRST["ple_gate"] + 3 + AHEAD)

            def mod_tile(first, k, v):
                return MOD[:, layer, first + k, v:v + 1]

            def modulated(n_norm, inst, which, shift, t, ready):
                n = P * t
                squares(lambda k: X[:, k, 0:n], lambda k: SQ2[:, k, 0:n], ready)
                if t == 4:
                    act.wait_ge(S("n_ss"), n_norm + 1)
                    for g, sem in ((0, "n_stdx"), (TX, "n_std")):
                        act.activation(RT[:, g:g + TX], stat_row(n_norm, t)[:, g:g + TX], ACT.Sqrt, scale=1.0 / D,
                                       bias=EPSC[:, 0:1]).then_inc(S(sem), 1)
                else:
                    norm_std(n_norm, t)
                for k in range(KT):
                    act.wait_ge(S("xm"), KT * inst + k + 1)
                    act.activation(AHI2[:, k, 0:TX], SQ2[:, k, 0:TX], ACT.Identity, bias=mod_tile(shift, k, 0))\
                       .then_inc(S("act_hi"), 1)
                if t == 4 and layer == 0:
                    ctx_modulated(inst, which, shift)

            def ctx_modulated(inst, which, shift, ks=range(KT)):
                for k in ks:
                    act.wait_ge(S("xrc"), KT * inst + k + 1)
                    act.activation(SQ2[:, k, TX:TB], SQ2[:, k, TX:TB], ACT.Identity,
                                   scale=GM[:, layer, which, k, 1:2], bias=mod_tile(shift, k, 1)).then_inc(S("xmc"), 1)
                    if k > ks[0]:
                        ctx_hi(inst, k - 1)
                ctx_hi(inst, ks[-1])

            def ctx_hi(inst, k):
                act.wait_ge(S("xmc"), KT * inst + k + 1)
                act.activation(AHI2[:, k, TX:TB], SQ2[:, k, TX:TB], ACT.Copy).then_inc(S("ctx_hi"), 1)

            for layer in range(2):
                nt = TB if layer == 0 else TX
                y_done = 4 * (4 if layer == 0 else 6)
                if layer == 0:
                    modulated(8, 0, 0, 0, 4, lambda k: (act.wait_ge(S("xu"), 3 * KT + k + 1), act.wait_ge(S("c_ev"), 4)))
                else:
                    modulated(10, 2, 0, 0, 4, lambda k: act.wait_ge(S("xd"), 2 * (k + 1)))
                for q in range(6):
                    n = TB if layer == 0 or q >= 4 else TX
                    c = FIRST[f"qkv{layer}"] + q
                    split_w(None, c + AHEAD)
                    act.wait_ge(S("pe_done"), c + 1)
                    act.activation(QKV[:, 2 * q:2 * q + 2, 0:n], ring2(q, n), ACT.Copy).then_inc(S("qkv_ev"), 1)
                    if q < 3:
                        act.wait_ge(S("f_arg"), 6 * (3 * layer + q + 1))
                        act.activation(HA[:, q, :], FU[:, 1, :], ACT.Sin).then_inc(S("f_h"), 1)
                    if q in (1, 2) and layer == 1:
                        ctx_modulated(2, 0, 0, range(4 * q - 4, 4 * q))
                act.wait_ge(S("f_k"), 2 * layer + 1)
                for h in range(2):
                    act.activation(KR[:, h, :, :], PS[:, 6:8, TX * h:TX * h + TX], ACT.Copy).then_inc(S("f_kc"), 1)
                act.activation(KRX[:, :, :], PS[:, 6, :].rearrange("p (h n) -> p h n", h=2), ACT.Copy).then_inc(S("f_kc"), 1)

                def query_pair(pair):
                    if pair == 0:
                        act.wait_ge(S("h_kn"), 2 * layer + 2)
                    act.wait_ge(S("h_ss"), 5 * layer + pair + 1)
                    q2 = QKV[:, 2 * pair:2 * pair + 2, 0:nt]
                    act.activation(HSQ[:, :, 0:nt], q2, ACT.Square).then_inc(S("h_sq"), 1)
                    act.activation(q2, q2, ACT.Identity, scale=par("q_norm_2", layer)).then_inc(S("h_gain"), 1)

                for q in range(6):
                    c = FIRST[f"hy{layer}"] + q
                    if q == 1:
                        act.wait_ge(S("qkv_ev"), 6 * layer + 6)
                        act.activation(HSQ[:, :, :], QKV[:, 8:10, :], ACT.Square).then_inc(S("h_sq"), 1)
                    if q >= 3:
                        query_pair(q - 3)
                    split_w(None, c + AHEAD)
                    act.wait_ge(S("pe_done"), c + 1)
                    for t in range(2):
                        m = 2 * q + t
                        act.activation(HY[:, m, 0:nt], ring2(q, nt)[:, t, :], ACT.Identity,
                                       scale=par("conv_w_2", 36 * layer + 12 + m), bias=par("conv_b_2", 12 * layer + m))\
                           .then_inc(S("hy_mid"), 1)
                    if q == 0:
                        act.wait_ge(S("f_k"), 2 * layer + 2)
                        for h in range(2):
                            act.activation(KIZ[:, h, :, :], PS[:, 6:8, TX * h:TX * h + TX], ACT.Copy).then_inc(S("f_kc"), 1)
                    if q == 1:
                        act.wait_ge(S("h_ss"), 5 * layer + 1)
                        act.activation(HSQ[:, :, :], PS[:, 6:8, :], ACT.Sqrt, scale=1.0 / DH2, bias=EPSC[:, 0:1])\
                           .then_inc(S("h_std"), 1)
                query_pair(3)
                tq = nt // P
                act.wait_ge(S("h_ss"), 5 * layer + 5)
                act.activation(STD[:, 0:8 * tq], PS[:, 6, 0:8 * tq], ACT.Sqrt, bias=EPSC[:, 1:2]).then_inc(S("h_std"), 1)
                for grp in range(nt // TX):
                    y = 2 * layer + grp
                    act.wait_ge(S("y_tr"), y + 1)
                    if grp:
                        act.wait_ge(S("y_fwd"), 4 * layer + 2)
                    act.activation(VTT[:, :, :], PS[:, 0:2, :], ACT.Copy).then_inc(S("y_vt"), 1)
                units = [(0, h) for h in range(NH2)] + ([(1, h) for h in range(NH2)] if layer == 0 else [])
                u0 = 2 * NH2 * layer

                def exps(u):
                    grp, h = units[u]
                    s = u % 2
                    act.wait_ge(S("b_nm"), 2 * (u0 + u) + 2)
                    for t in range(2):
                        src = PS[:, 2 * s + t, :] if grp == 0 else PS[:, 2 * s, TX * t:TX * t + TX]
                        n = TB if grp == 0 else TX
                        col = h * tq + 2 * grp + t
                        act.activation(PB[:, s, t, 0:n], src, ACT.Exp, scale=RC[:, col:col + 1],
                                       bias=NM[:, s, t:t + 1], accum_out=SMX[:, s, t:t + 1]).then_inc(S("b_ex"), 1)

                act.wait_ge(S("y_inv"), y_done // 4)
                exps(0)
                act.wait_ge(S("y_h"), y_done)
                for m in range(HT):
                    act.activation(HHI[:, m, 0:nt], HY[:, 8 + m, 0:nt], ACT.Copy).then_inc(S("hh_hi"), 1)
                act.wait_ge(S("hh_lo"), HT * (layer + 1))
                act.wait_ge(S("v_tr"), layer + 1)
                act.activation(VT2[:, :, :], PS[:, 4:6, :].rearrange("p a (b n) -> p (a b) n", n=P), ACT.Copy)\
                   .then_inc(S("v_ev"), 1)

                for u, (grp, h) in enumerate(units):
                    if u + 1 < len(units):
                        exps(u + 1)
                    kts = 4 if grp == 0 else 2
                    act.wait_ge(S("b_tr"), u0 + u + 1)
                    act.activation(PT2[:, u % 2, 0:kts, :],
                                   PS[:, 4:4 + kts // 2, :].rearrange("p a (b n) -> p (a b) n", n=TX), ACT.Copy)\
                       .then_inc(S("b_pt"), 1)

                act.wait_ge(S("b_o"), u0 + len(units))
                for k in range(KT):
                    act.activation(A2HI[:, k, 0:nt], QKV[:, k, 0:nt], ACT.Copy).then_inc(S("a2_hi"), 1)
                for j in range(2):
                    c = FIRST[f"oh{layer}"] + j
                    split_w(None, c + AHEAD)
                    act.wait_ge(S("pe_done"), c + 1)
                    act.wait_ge(S("a2_lo"), KT * (layer + 1))
                    src = PS[:, 4 * j:4 * j + 4, 0:nt]
                    act.activation(MG[:, 4 * j:4 * j + 4, 0:nt], src, ACT.Copy).then_inc(S("oh_ev"), 1)

                def mix(i, m):
                    c = FIRST[f"mix{layer}"] + 3 * m
                    for g in range(2):
                        split_w(i, c + g + AHEAD)
                        act.wait_ge(S("pe_done"), lin(i, 3, c + g + 1))
                        if layer + m:
                            act.wait_ge(S("merge"), lin(i, 3, 12 * layer + 3 * (m - 1) + (1 if g == 0 else 3)))
                        act.activation(SG[:, g, :, 0:nt], ring2(g, nt), ACT.Sigmoid).then_inc(S("gate"), 1)
                    split_w(i, c + 2 + AHEAD)
                mix(None, 0)
                with act.Fori(0, 3) as i:
                    mix(i, 1)
                act.wait_ge(S("pe_done"), FIRST[f"out{layer}"])
                act.wait_ge(S("merge"), 12 * (layer + 1))
                for k in range(KT):
                    act.activation(AHI2[:, k, 0:nt], MG[:, k, 0:nt], ACT.Copy).then_inc(S("mg_hi"), 1)
                for j in range(4):
                    split_w(None, FIRST[f"out{layer}"] + j + AHEAD)

                t = nt // P
                per = nt // TX
                xo0 = 2 * KT * layer
                modulated(9 + 2 * layer, 1 + 2 * layer, 1, 24, t, lambda k: act.wait_ge(S("xo"), xo0 + per * (k + 1)))
                inst = 2 + layer

                def silus2(i, j, c):
                    if i is None and j == FT - 1:
                        first_hidden(inst, HB2, SHI2, nt)
                    split_w(i, c + AHEAD)
                    act.wait_ge(S("pe_done"), lin(i, 3, c + 1))
                    if j >= RING:
                        act.wait_ge(S("h"), lin(i, 3, FT * inst + j - RING + 1))
                    act.activation(SIL[:, j % RING, 0:nt], ring2(j, nt)[:, 0, :], ACT.Silu).then_inc(S("sil"), 1)
                steps(act, f"gu{layer}", silus2, tail=1)
                down(f"dn{layer}", inst, HB2, SHI2, nt)

            squares(lambda k: X[:, k, 0:TX], lambda k: SQ1[:, k, :], lambda k: act.wait_ge(S("xd"), 2 * KT + k + 1))
            norm_std(12, 2)
            for t in range(2):
                act.wait_ge(S("out_tr"), 2 * t + 2)
                act.activation(OUTS[:, t, 512:], PS[:, 2 * t + 1, :], ACT.Copy).then_inc(S("out_ev1"), 1)

        @block.vector
        def _(dve):
            def split_w(i, c):
                if c >= TOTAL:
                    return
                dve.wait_ge(S("hi_done"), lin(i, 3, c + 1))
                dve.tensor_tensor(WLO[:, c % RING, :], RAW[:, c % RING, :], WHI[:, c % RING, :].bitcast(F32), ALU.subtract)\
                   .then_inc(S("lo_done"), 1)

            def split_h(i, inst, j, hb, shi, slo, n):
                dve.wait_ge(S("hs_hi"), lin(i, 3, FT // 2 * inst + j + 1))
                dve.tensor_tensor(slo[:, j % RING, :, 0:n], hb[:, bass.ds(lin(i, 6, 2 * j), 2), 0:n],
                                  shi[:, j % RING, :, 0:n].bitcast(F32), ALU.subtract).then_inc(S("hs_lo"), 1)

            def first_hidden(inst, hb, shi, slo, n):
                for j in range(AHEAD):
                    split_h(None, inst, j, hb, shi, slo, n)

            def mod_lo(layer, i, half):
                if half >= 2 * MODC:
                    return
                t = 2 * MODC * layer + half
                dve.wait_ge(S("mod_hi"), lin(i, 6, t + 1))
                dve.tensor_tensor(MLO[:, t % RING, :], MRAW[:, t % RING, :], MHI[:, t % RING, :].bitcast(F32), ALU.subtract)\
                   .then_inc(S("mod_lo"), 1)

            def down(stage, inst, hb, shi, slo, n):
                def body(i, j, c):
                    mods = inst < 2 and i is None and j < MODC - FT
                    if mods:
                        mod_lo(inst, None, 2 * (FT + j) + 1)
                    split_w(i, c + AHEAD)
                    if i is not None or j + AHEAD < FT // 2:
                        split_h(i, inst, j + AHEAD, hb, shi, slo, n)
                    if mods:
                        mod_lo(inst, None, 2 * (FT + j) + 2)
                steps(dve, stage, body, tail=2)

            def norm_row(n_norm, t):
                dve.wait_ge(S("n_std"), n_norm + 1)
                dve.reciprocal(RT[:, 0:P * t], RT[:, 0:P * t]).then_inc(S("n_rt"), 1)
                dve.wait_ge(S("n_rt"), n_norm + 1)

            def gained_lo(inst, name, ks=range(KT)):
                for k in ks:
                    dve.wait_ge(S("act_hi"), KT * inst + k + 1)
                    dve.scalar_tensor_tensor(out=ALO1[:, k, :], in0=X[:, k, 0:TX], scalar=par(name, k),
                                             in1=AHI1[:, k, :].bitcast(F32), op0=ALU.mult, op1=ALU.subtract)\
                       .then_inc(S("act_lo"), 1)

            def branch(src, gain, inst=None, name=None):
                for k in range(KT):
                    dve.scalar_tensor_tensor(out=TU[:, k, :], in0=src(k), scalar=gain(k), in1=RT[:, 0:TX],
                                             op0=ALU.mult, op1=ALU.mult).then_inc(S("xt"), 1)
                    if name and k >= 3:
                        gained_lo(inst, name, [k - 3])
                if name:
                    gained_lo(inst, name, range(KT - 3, KT))

            dve.memset(GS[:, 3, :], 0.0).then_inc(S("gs_clear"), 1)
            dve.memset(ONES[:, :], 1.0).then_inc(S("const"), 1)
            dve.memset(EPSC[:, 0:1], EPS).then_inc(S("const"), 1)
            dve.memset(EPSC[:, 1:2], EPS * DH2).then_inc(S("const"), 1)
            for n, g in enumerate((0, 2)):
                dve.wait_ge(S("tr_par"), n + 1)
                dve.tensor_copy(PAR[:, g, 0:PAR_USED[g]], PS[:, 4 + n, 0:PAR_USED[g]]).then_inc(S("par_ev"), 1)
            split_w(None, 0)
            gained_lo(0, "ffn1_pre_g")
            dve.wait_ge(S("sc_hi"), 1)
            dve.tensor_tensor(SCR[:, :, 2:4], SC[:, :, :], SCR[:, :, 0:2].bitcast(F32), ALU.subtract).then_inc(S("sc_lo"), 1)
            split_w(None, 1)

            def later_parameters():
                dve.wait_ge(S("tr_par"), 3)
                for n, g in enumerate((1, 3)):
                    dve.tensor_copy(PAR[:, g, 0:PAR_USED[g]], PS[:, 1, n * P:n * P + PAR_USED[g]]).then_inc(S("par_ev"), 1)
                dve.wait_ge(S("tr_p"), 1)
                dve.tensor_copy(P32[:, :, :], PS[:, 2, :].rearrange("p (t n) -> p t n", t=2)).then_inc(S("p_ev"), 1)
                dve.wait_ge(S("in_bias"), 48)
                dve.wait_ge(S("mm_ext"), 1)
                dve.tensor_tensor(EXT[:, :], PS[0:16, 3, 0:384], MASK[:, :], ALU.add).then_inc(S("ext_ev"), 1)
                dve.wait_ge(S("p_hi"), 1)
                dve.tensor_tensor(PLO[:, :, :], P32[:, :, :], PHI[:, :, :].bitcast(F32), ALU.subtract).then_inc(S("p_lo"), 1)
                dve.wait_ge(S("par_ev"), 4)
                dve.tensor_scalar(HG[:, 0, :], par("ffn1_post_g", 0, 8), 0.5, None, ALU.mult).then_inc(S("hg"), 1)
                dve.tensor_scalar(HG[:, 1, :], par("ffn2_post_g", 0, 8), 0.5, None, ALU.mult).then_inc(S("hg"), 1)
                dve.wait_ge(S("in_sink"), 16)
                dve.tensor_scalar(SINK[:, 1, :], SINK[:, 0, :], -1.0, None, ALU.mult).then_inc(S("nsink"), 1)

            def context():
                for b in range(4):
                    dve.wait_ge(S("tr_c"), b + 1)
                    dve.tensor_copy(X[:, 2 * b:2 * b + 2, TX:TB], PS[:, b, :].rearrange("p (t n) -> p t n", t=2))\
                       .then_inc(S("c_ev"), 1)

            for inst, (pre, post) in enumerate(((0, 1), (4, 5))):
                f = f"ffn{inst + 1}"

                def hidden1(i, j, c):
                    if i is None and j == FT - 1:
                        first_hidden(inst, HB1, SHI1, SLO1, TX)
                    if i is None and j == 0:
                        if inst == 0:
                            mod_lo(0, None, 0)
                        mod_lo(inst, None, 1)
                        split_w(i, c + AHEAD)
                    else:
                        split_w(i, c + AHEAD)
                        mod_lo(inst, i, 2 * j + 1)
                    if i is None and j == 0:
                        norm_row(pre, 2)
                    dve.wait_ge(S("pe_done"), lin(i, 3, c + 1))
                    dve.tensor_tensor(GU[:, j % RING, :, :], ring1(j), over_tiles(RT[:, 0:TX], 2), ALU.mult)\
                       .then_inc(S("gu"), 1)
                    mod_lo(inst, i, 2 * j + 2)
                    dve.wait_ge(S("sil"), lin(i, 3, FT * inst + j + 1))
                    dve.tensor_tensor(HB1[:, bass.ds(lin(i, 3, j), 1), :], GU[:, j % RING, 0:1, :], GU[:, j % RING, 1:2, :],
                                      ALU.mult).then_inc(S("h"), 1)
                    if inst == 0 and i is None:
                        if j == 0:
                            later_parameters()
                        elif j == 1:
                            context()
                steps(dve, f + "_gu", hidden1, tail=1)
                down(f + "_dn", inst, HB1, SHI1, SLO1, TX)
                dve.wait_ge(S("mod_col"), MODC * (inst + 1))
                bias = over_tokens(par("b_mod_2", 48 * inst, 48), 2)
                dve.tensor_tensor(MOD[:, inst, :, :], MSUM[:, :, 2:4], bias, ALU.add).then_inc(S("mod_ev"), 1)
                dve.wait_ge(S("mod_ev"), 4 * inst + 1)
                dve.tensor_tensor(MOD[:, inst, :, :], MOD[:, inst, :, :], MSUM[:, :, 0:2], ALU.add).then_inc(S("mod_ev"), 1)
                dve.wait_ge(S("mod_ev"), 4 * inst + 2)
                for w, (first, name) in enumerate(((8, "norm_mix_2"), (32, "norm_ffn_2"))):
                    dve.scalar_tensor_tensor(out=GM[:, inst, w, :, :], in0=MOD[:, inst, first:first + 8, :], scalar=1.0,
                                             in1=over_tokens(par(name, 8 * inst, 8), 2), op0=ALU.add, op1=ALU.mult)\
                       .then_inc(S("mod_ev"), 1)
                norm_row(post, 2)
                dve.wait_ge(S("hg"), 2)
                branch(lambda k: acc(k, TX), lambda k: HG[:, inst, k:k + 1], *((1, "attn_pre_g"), (4, "ple_pre_g"))[inst])
                if inst == 1:
                    break

                def z_tiles(i, j, c):
                    split_w(i, c + AHEAD)
                    if i is None and j == 0:
                        norm_row(2, 2)
                    dve.wait_ge(S("pe_done"), lin(i, 3, c + 1))
                    dve.tensor_tensor(GU[:, j % RING, :, :], ring1(j), over_tiles(RT[:, 0:TX], 2), ALU.mult)\
                       .then_inc(S("zt"), 1)
                    dve.wait_ge(S("zt"), lin(i, 6, 2 * j + 1))
                    g, row, _ = PAR_AT["b_in"]
                    bias = PAR[:, g, bass.ds(lin(i, 6, row + 2 * j), 2)]
                    dve.tensor_tensor(Z[:, bass.ds(lin(i, 6, 2 * j), 2), :], GU[:, j % RING, :, :], over_tokens(bias, TX),
                                      ALU.add).then_inc(S("zt"), 1)
                steps(dve, "b1_in", z_tiles)

                def scores_in(g):
                    s = g % 2
                    dve.wait_ge(S("a_s"), g + 1)
                    heads = BIAS[g // 2][:, 4 * (g % 2):4 * (g % 2) + 4, ::-1]
                    for a in range(2):
                        dve.scalar_tensor_tensor(out=SB1[s][:, a::2, :], in0=PS[:, a, :].rearrange("p (b n) -> p b n", n=TX),
                                                 scalar=DH1 ** -0.5, in1=heads[:, a::2, :], op0=ALU.mult, op1=ALU.add)\
                           .then_inc(S("a_sb"), 1)
                    dve.scalar_tensor_tensor(out=SB0[s][:, :, :], in0=PS[:, 2, :].rearrange("p (b n) -> p b n", n=P),
                                             scalar=DH1 ** -0.5, in1=heads[:, :, P:TX], op0=ALU.mult, op1=ALU.add)\
                       .then_inc(S("a_sb"), 1)

                def score_maxima(g):
                    s = g % 2
                    dve.wait_ge(S("a_sb"), 3 * g + 3)
                    dve.tensor_reduce(SE[:, s, 0:4] if g < 2 else NM[:, s, 0:4], SB1[s][:, :, :], AX.X, ALU.max, negate=True)\
                       .then_inc(S("a_mx"), 1)
                    last = dve.tensor_reduce(SE[:, s, 4:8] if g < 2 else NM[:, s, 4:8], SB0[s][:, :, :], AX.X, ALU.max,
                                             negate=True)
                    if g >= 2:
                        last.then_inc(S("a_nm"), 1)
                        return
                    last.then_inc(S("a_mx"), 1)
                    dve.wait_ge(S("a_mx"), 2 * g + 2)
                    dve.wait_ge(S("nsink"), 1)
                    sinks = over_tiles(SINK[:, 1, 4 * g:4 * g + 4], 2)
                    dve.tensor_tensor(NM[:, s, :].rearrange("p (t h) -> p t h", t=2), SE[:, s, :].rearrange("p (t h) -> p t h", t=2),
                                      sinks, ALU.min).then_inc(S("a_nm"), 1)
                    dve.wait_ge(S("a_nm"), g + 1)
                    dve.tensor_tensor(SE[:, s, :].rearrange("p (t h) -> p t h", t=2), NM[:, s, :].rearrange("p (t h) -> p t h", t=2),
                                      sinks, ALU.subtract).then_inc(S("a_se0"), 1)

                def normalise(g):
                    s = g % 2
                    dve.wait_ge(S("a_ex"), 8 * g + 8)
                    if g < 2:
                        dve.wait_ge(S("a_sink"), g + 1)
                        dve.tensor_tensor(SMX[:, s, :], SMX[:, s, :], SE[:, s, :], ALU.add).then_inc(S("a_tot"), 1)
                        dve.wait_ge(S("a_tot"), g + 1)
                    dve.reciprocal(RS[:, s, :], SMX[:, s, :]).then_inc(S("a_rs"), 1)
                    dve.wait_ge(S("a_rs"), g + 1)
                    dve.tensor_tensor(SB1[s][:, :, :], SB1[s][:, :, :], over_tokens(RS[:, s, 0:4], TX), ALU.mult)\
                       .then_inc(S("a_p"), 1)

                def mixed_lo(g):
                    dve.wait_ge(S("act_hi"), 2 * KT + 2 * g + 2)
                    dve.tensor_tensor(ALO1[:, 2 * g:2 * g + 2, :], PS[:, 7, :].rearrange("p (t n) -> p t n", t=2),
                                      AHI1[:, 2 * g:2 * g + 2, :].bitcast(F32), ALU.subtract).then_inc(S("act_lo"), 2)

                dve.wait_ge(S("bias_in"), 32)
                scores_in(0)
                score_maxima(0)
                for b in range(3):
                    dve.wait_ge(S("vt_tr"), b + 1)
                    n = 4 if b < 2 else 2
                    dve.tensor_copy(VT1[:, 4 * b:4 * b + n, :], PS[:, 3 + b, 0:n * P].rearrange("p (a n) -> p a n", n=P))\
                       .then_inc(S("vt_ev"), 1)
                for g in range(4):
                    if g < 3:
                        scores_in(g + 1)
                    normalise(g)
                    if g < 3:
                        score_maxima(g + 1)
                    if g >= 2:
                        mixed_lo(g - 2)
                mixed_lo(2)
                mixed_lo(3)
                for j in range(4):
                    c = FIRST["b1_out"] + j
                    split_w(None, c + AHEAD)
                    dve.wait_ge(S("pe_done"), c + 1)
                    dve.tensor_tensor(FB[:, 2 * j:2 * j + 2, :], ring1(j), over_tokens(par("b_out", 2 * j, 2), TX), ALU.add)\
                       .then_inc(S("f_ev"), 1)
                mod_lo(1, None, 0)
                norm_row(3, 2)
                dve.wait_ge(S("f_ev"), 4)
                branch(lambda k: FB[:, k, :], lambda k: par("attn_post_g", k), 3, "ffn2_pre_g")

            split_w(None, FIRST["ple_proj"] + AHEAD)

            def embedded(j):
                dve.wait_ge(S("pg_sig"), j + 1)
                dve.tensor_tensor(FB[:, 2 * j:2 * j + 2, :], PG[:, 2 * j:2 * j + 2, :], projected(j), ALU.mult).then_inc(S("f_ev"), 1)
            dve.wait_ge(S("pe_done"), FIRST["ple_proj"] + 1)
            for j in range(4):
                c = FIRST["ple_gate"] + j
                if j < 3:
                    split_w(None, c + AHEAD)
                if j == 0:
                    norm_row(6, 2)
                dve.wait_ge(S("pe_done"), c + 1)
                if j >= RING:
                    dve.wait_ge(S("pg_sig"), j - RING + 1)
                dve.tensor_tensor(GU[:, j % RING, :, :], ringp(j), over_tiles(RT[:, 0:TX], 2), ALU.mult).then_inc(S("pg"), 1)
                if j:
                    embedded(j - 1)
            embedded(3)
            norm_row(7, 2)
            dve.wait_ge(S("f_ev"), 8)
            branch(lambda k: FB[:, k, :], lambda k: par("ple_post_g", k))
            split_w(None, FIRST["ple_gate"] + 3 + AHEAD)

            def modulated(n_norm, inst, a_inst, which, shift, t):
                halves = t // 2
                if halves == 1:
                    norm_row(n_norm, t)
                else:
                    dve.wait_ge(S("n_stdx"), inst + 1)
                    dve.reciprocal(RT[:, 0:TX], RT[:, 0:TX]).then_inc(S("n_rt"), 1)
                    dve.wait_ge(S("n_rt"), n_norm + 1)

                def low(k):
                    dve.wait_ge(S("act_hi"), KT * a_inst + k + 1)
                    dve.scalar_tensor_tensor(out=ALO2[:, k, 0:TX], in0=SQ2[:, k, 0:TX], scalar=MOD[:, layer, shift + k, 0:1],
                                             in1=AHI2[:, k, 0:TX].bitcast(F32), op0=ALU.add, op1=ALU.subtract)\
                       .then_inc(S("act_lo"), 1)
                for k in range(KT):
                    dve.scalar_tensor_tensor(out=SQ2[:, k, 0:TX], in0=X[:, k, 0:TX], scalar=GM[:, layer, which, k, 0:1],
                                             in1=RT[:, 0:TX], op0=ALU.mult, op1=ALU.mult).then_inc(S("xm"), 1)
                    if k == 6 and halves == 2:
                        dve.wait_ge(S("n_std"), n_norm + 1)
                        dve.reciprocal(RT[:, TX:TB], RT[:, TX:TB]).then_inc(S("n_rtc"), 1)
                    if k >= 2:
                        low(k - 2)
                low(KT - 2)
                low(KT - 1)
                if halves == 2 and layer == 0:
                    ctx_low(inst)

            def ctx_low(inst, ks=range(KT)):
                for k in ks:
                    dve.wait_ge(S("ctx_hi"), KT * inst + k + 1)
                    dve.tensor_tensor(ALO2[:, k, TX:TB], SQ2[:, k, TX:TB], AHI2[:, k, TX:TB].bitcast(F32), ALU.subtract)\
                       .then_inc(S("ctx_lo"), 1)

            for layer in range(2):
                nt = TB if layer == 0 else TX
                modulated(8 + 2 * layer, 2 * layer, 5 + 2 * layer, 0, 0, 4)

                def network(l):
                    a0 = 6 * (3 * layer + l)
                    dve.wait_ge(S("f_mm"), 3 * layer + l + 1)
                    row = PAR_AT[f"filt_b{l + 1}_2"][1] + layer
                    fr = PAR_AT["filt_freq_2"][1] + 3 * layer + l
                    dve.tensor_scalar(FU[:, 0, :], PS[0:FH, 7, 0:TX], PAR[0:FH, 3, row:row + 1], PAR[0:FH, 3, fr:fr + 1],
                                      ALU.add, ALU.mult).then_inc(S("f_arg"), 1)
                    dve.wait_ge(S("f_arg"), a0 + 1)
                    dve.tensor_scalar(FU[:, 1, :], FU[:, 0, :], 1.0 / (2.0 * np.pi), MAGIC, ALU.mult, ALU.add)\
                       .then_inc(S("f_arg"), 1)
                    dve.wait_ge(S("f_arg"), a0 + 2)
                    dve.tensor_scalar(FU[:, 2, :], FU[:, 1, :], -MAGIC, None, ALU.add).then_inc(S("f_arg"), 1)
                    dve.wait_ge(S("f_arg"), a0 + 3)
                    dve.scalar_tensor_tensor(out=FU[:, 3, :], in0=FU[:, 2, :], scalar=-TWO_PI_HI, in1=FU[:, 0, :],
                                             op0=ALU.mult, op1=ALU.add).then_inc(S("f_arg"), 1)
                    dve.wait_ge(S("f_arg"), a0 + 4)
                    dve.scalar_tensor_tensor(out=FU[:, 0, :], in0=FU[:, 2, :], scalar=-TWO_PI_LO, in1=FU[:, 3, :],
                                             op0=ALU.mult, op1=ALU.add).then_inc(S("f_arg"), 1)
                    dve.wait_ge(S("f_arg"), a0 + 5)
                    dve.tensor_scalar(FU[:, 1, :], FU[:, 0, :], PI_IN, -PI_IN, ALU.min, ALU.max).then_inc(S("f_arg"), 1)

                def decay(t):
                    dve.wait_ge(S("f_taps"), 2 * layer + t + 1)
                    for r in range(2):
                        dve.tensor_tensor(HF[:, t, r, :], PS[:, 6 + r, :], DEC[:, t, :], ALU.mult).then_inc(S("f_dec"), 1)

                beside = [lambda: network(0), lambda: network(1), lambda: network(2), lambda: decay(0), lambda: decay(1),
                          lambda: None]
                for q in range(6):
                    split_w(None, FIRST[f"qkv{layer}"] + q + AHEAD)
                    beside[q]()
                    if q in (1, 2) and layer == 1:
                        ctx_low(2, range(4 * q - 4, 4 * q))

                def keys():
                    dve.wait_ge(S("h_std"), 2 * layer + 1)
                    for kv in range(2):
                        dve.reciprocal(HSQ[:, kv, :], HSQ[:, kv, :]).then_inc(S("h_kr"), 1)
                    for kv in range(2):
                        dve.wait_ge(S("h_kr"), 2 * layer + kv + 1)
                        dve.scalar_tensor_tensor(out=QKV[:, 8 + kv, :], in0=QKV[:, 8 + kv, :], scalar=par("k_norm_2", layer),
                                                 in1=HSQ[:, kv, :], op0=ALU.mult, op1=ALU.mult).then_inc(S("h_kn"), 1)

                def rotated(r, tile):
                    if r:
                        dve.wait_ge(S("h_sum"), 5 * layer + r)
                    dve.wait_ge(S("h_rot"), 5 * layer + r + 1)
                    dve.tensor_tensor(BR[:, :, :], PS[:, 7, :].rearrange("p (t n) -> p t n", t=2), over_tiles(ROPE[:, 1, :], 2),
                                      ALU.mult).then_inc(S("h_sin"), 1)
                    dve.wait_ge(S("h_sin"), 5 * layer + r + 1)
                    dve.wait_ge(S("h_cos"), 5 * layer + r + 1)
                    dve.tensor_tensor(QKV[:, tile:tile + 2, 0:TX], QKV[:, tile:tile + 2, 0:TX], BR[:, :, :], ALU.add)\
                       .then_inc(S("h_sum"), 1)

                for q in range(6):
                    c = FIRST[f"hy{layer}"] + q
                    split_w(None, c + AHEAD)
                    if q == 2:
                        keys()
                    if q >= 4:
                        rotated(q - 4, (8, 0)[q - 4])
                    for t in range(2):
                        m = 2 * q + t
                        dve.wait_ge(S("hy_mid"), 12 * layer + 2 * q + 2)
                        u3 = ring2(q, nt)[:, t, :].rearrange("p (g n) -> p g n", n=TX)
                        y3 = HY[:, m, 0:nt].rearrange("p (g n) -> p g n", n=TX)
                        dve.scalar_tensor_tensor(out=y3[:, :, 1:TX], in0=u3[:, :, 0:TX - 1], scalar=par("conv_w_2", 36 * layer + m),
                                                 in1=y3[:, :, 1:TX], op0=ALU.mult, op1=ALU.add).then_inc(S("hy_taps"), 1)
                        dve.wait_ge(S("hy_taps"), 24 * layer + 2 * m + 1)
                        dve.scalar_tensor_tensor(out=y3[:, :, 0:TX - 1], in0=u3[:, :, 1:TX],
                                                 scalar=par("conv_w_2", 36 * layer + 24 + m), in1=y3[:, :, 0:TX - 1],
                                                 op0=ALU.mult, op1=ALU.add).then_inc(S("hy_taps"), 1)
                        if m >= 8:
                            dve.wait_ge(S("hy_taps"), 24 * layer + 2 * m + 2)
                            dve.tensor_tensor(HY[:, m, 0:nt], HY[:, m, 0:nt], HY[:, m - 4, 0:nt], ALU.mult).then_inc(S("hy_v"), 1)
                    if q == 0:
                        dve.wait_ge(S("f_kc"), 5 * layer + 5)
                        dve.tensor_copy(KRX[0:1, :, :], PS[0:1, 6, :].rearrange("p (h n) -> p h n", h=2)).then_inc(S("f_fix"), 1)
                        dve.memset(KIZ[0:1, :, 0, :], 0.0).then_inc(S("f_fix"), 1)
                rotated(2, 2)
                rotated(3, 4)
                rotated(4, 6)
                tq = nt // P
                dve.wait_ge(S("h_std"), 2 * layer + 2)
                dve.reciprocal(RC[:, 0:8 * tq], STD[:, 0:8 * tq]).then_inc(S("h_rc"), 1)
                dve.wait_ge(S("h_sum"), 5 * (layer + 1))
                units = [(0, h) for h in range(NH2)] + ([(1, h) for h in range(NH2)] if layer == 0 else [])
                u0 = 2 * NH2 * layer

                def maxima(u):
                    grp, h = units[u]
                    s = u % 2
                    dve.wait_ge(S("b_s"), u0 + u + 1)
                    src = PS[:, 2 * s:2 * s + 2, :] if grp == 0 else PS[:, 2 * s, :].rearrange("p (t n) -> p t n", t=2)
                    dve.tensor_reduce(NM[:, s, 2:4], src, AX.X, ALU.max, negate=True).then_inc(S("b_nm"), 1)
                    dve.wait_ge(S("b_nm"), 2 * (u0 + u) + 1)
                    col = h * tq + 2 * grp
                    dve.tensor_tensor(NM[:, s, 0:2], NM[:, s, 2:4], RC[:, col:col + 2], ALU.mult).then_inc(S("b_nm"), 1)

                def normalise2(u):
                    s = u % 2
                    n = TB if units[u][0] == 0 else TX
                    dve.wait_ge(S("b_ex"), 2 * (u0 + u) + 2)
                    dve.reciprocal(RS[:, s, 0:2], SMX[:, s, 0:2]).then_inc(S("b_rs"), 1)
                    dve.wait_ge(S("b_rs"), u0 + u + 1)
                    for t in range(2):
                        dve.tensor_scalar(PB[:, s, t, 0:n], PB[:, s, t, 0:n], RS[:, s, t:t + 1], None, ALU.mult)\
                           .then_inc(S("b_p"), 1)

                def attended(u):
                    grp, h = units[u]
                    dve.wait_ge(S("b_pv"), u0 + u + 1)
                    dve.tensor_copy(QKV[:, h, TX * grp:TX * grp + TX], PS[:, 6 + u % 2, 0:TX]).then_inc(S("b_o"), 1)

                dve.wait_ge(S("f_fix"), 2 * layer + 2)

                def spectra(y):
                    h = y % 2
                    y += 4 * layer
                    re, im = (PS[:, 2 + 2 * h + b, :].rearrange("p (c n) -> p c n", c=2) for b in range(2))
                    t1, t2 = YT1[:, h, :, :], YT2[:, h, :, :]
                    if y >= 2:
                        dve.wait_ge(S("y_inv"), y - 1)
                        dve.wait_ge(S("y_h"), 4 * (y - 1))
                    dve.wait_ge(S("y_fwd"), y + 1)
                    dve.tensor_tensor(t1, re, KR[:, h, :, :], ALU.mult).then_inc(S("y_mul"), 1)
                    dve.tensor_tensor(t2, im, KIZ[:, h, :, :], ALU.mult).then_inc(S("y_mul"), 1)
                    dve.wait_ge(S("y_mul"), 7 * y + 2)
                    dve.tensor_tensor(YS[:, h, 0:2, :], t1, t2, ALU.subtract).then_inc(S("y_mul"), 1)
                    dve.wait_ge(S("y_mul"), 7 * y + 3)
                    dve.tensor_tensor(t1, re, KIZ[:, h, :, :], ALU.mult).then_inc(S("y_mul"), 1)
                    dve.tensor_tensor(t2[:, 0, :], im[:, 0, :], KRX[:, h, :], ALU.mult).then_inc(S("y_mul"), 1)
                    dve.tensor_tensor(t2[:, 1, :], im[:, 1, :], KR[:, h, 1, :], ALU.mult).then_inc(S("y_mul"), 1)
                    dve.wait_ge(S("y_mul"), 7 * y + 6)
                    dve.tensor_tensor(YS[:, h, 2:4, :], t1, t2, ALU.add).then_inc(S("y_mul"), 1)

                def convolved(y):
                    h, g = y % 2, slice(TX * (y // 2), TX * (y // 2) + TX)
                    y += 4 * layer
                    dve.wait_ge(S("y_mul"), 7 * y + 7)
                    dve.wait_ge(S("y_inv"), y + 1)
                    for m in range(2):
                        tile = 2 * h + m
                        tmp = YT1[:, h, m, :]
                        dve.scalar_tensor_tensor(out=tmp, in0=HY[:, 8 + tile, g], scalar=par("hyena_bias_2", 4 * layer + tile),
                                                 in1=PS[:, 6 + h, m * TX:m * TX + TX], op0=ALU.mult, op1=ALU.add).then_inc(S("y_h"), 1)
                    for m in range(2):
                        tile = 2 * h + m
                        dve.wait_ge(S("y_h"), 4 * y + m + 1)
                        dve.tensor_tensor(HY[:, 8 + tile, g], YT1[:, h, m, :], HY[:, tile, g], ALU.mult).then_inc(S("y_h"), 1)

                spectra(0)
                spectra(1)
                if nt == TB:
                    convolved(0)
                    spectra(2)
                    convolved(1)
                    spectra(3)
                last_y = nt // P - 1
                dve.wait_ge(S("h_rc"), layer + 1)
                maxima(0)
                convolved(last_y - 1)
                convolved(last_y)
                for m in range(HT):
                    dve.wait_ge(S("hh_hi"), HT * layer + m + 1)
                    dve.tensor_tensor(HLO[:, m, 0:nt], HY[:, 8 + m, 0:nt], HHI[:, m, 0:nt].bitcast(F32), ALU.subtract)\
                       .then_inc(S("hh_lo"), 1)
                for u in range(len(units)):
                    normalise2(u)
                    if u + 1 < len(units):
                        maxima(u + 1)
                    if u:
                        attended(u - 1)
                attended(len(units) - 1)

                dve.wait_ge(S("hh_lo"), HT * (layer + 1))
                for k in range(KT):
                    dve.wait_ge(S("a2_hi"), KT * layer + k + 1)
                    dve.tensor_tensor(A2LO[:, k, 0:nt], QKV[:, k, 0:nt], A2HI[:, k, 0:nt].bitcast(F32), ALU.subtract)\
                       .then_inc(S("a2_lo"), 1)
                for j in range(2):
                    split_w(None, FIRST[f"oh{layer}"] + j + AHEAD)

                def mix(i, m):
                    c = FIRST[f"mix{layer}"] + 3 * m
                    b = 12 * layer + 3 * m
                    mg = MG[:, bass.ds(lin(i, 2, 2 * m), 2), 0:nt]
                    split_w(i, c + AHEAD)
                    dve.wait_ge(S("gate"), lin(i, 2, 8 * layer + 2 * m + 1))
                    dve.tensor_tensor(mg, mg, SG[:, 0, :, 0:nt], ALU.mult).then_inc(S("merge"), 1)
                    split_w(i, c + 1 + AHEAD)
                    split_w(i, c + 2 + AHEAD)
                    dve.wait_ge(S("gate"), lin(i, 2, 8 * layer + 2 * m + 2))
                    dve.wait_ge(S("pe_done"), lin(i, 3, c + 3))
                    dve.tensor_tensor(SG[:, 1, :, 0:nt], SG[:, 1, :, 0:nt], ring2(2, nt), ALU.mult).then_inc(S("merge"), 1)
                    dve.wait_ge(S("merge"), lin(i, 3, b + 2))
                    dve.tensor_tensor(mg, mg, SG[:, 1, :, 0:nt], ALU.add).then_inc(S("merge"), 1)
                mix(None, 0)
                with dve.Fori(0, 3) as i:
                    mix(i, 1)
                for k in range(KT):
                    dve.wait_ge(S("mg_hi"), KT * layer + k + 1)
                    dve.tensor_tensor(ALO2[:, k, 0:nt], MG[:, k, 0:nt], AHI2[:, k, 0:nt].bitcast(F32), ALU.subtract)\
                       .then_inc(S("mg_lo"), 1)

                def gated_update(src, m, gate, sem):
                    for v in range(nt // TX):
                        g = slice(TX * v, TX * v + TX)
                        dve.scalar_tensor_tensor(out=X[:, m, g], in0=src[:, g], scalar=MOD[:, layer, gate + m, v:v + 1],
                                                 in1=X[:, m, g], op0=ALU.mult, op1=ALU.add).then_inc(S(sem), 1)
                for j in range(4):
                    c = FIRST[f"out{layer}"] + j
                    split_w(None, c + AHEAD)
                    dve.wait_ge(S("pe_done"), c + 1)
                    for t in range(2):
                        gated_update(ring2(j, nt)[:, t, :], 2 * j + t, 16, "xo")
                xo_now = 2 * KT if layer == 0 else 3 * KT
                dve.wait_ge(S("xo"), xo_now)
                modulated(9 + 2 * layer, 1 + 2 * layer, 6 + 2 * layer, 1, 24, nt // P)
                inst = 2 + layer

                def hidden2(i, j, c):
                    if i is None and j == FT - 1:
                        first_hidden(inst, HB2, SHI2, SLO2, nt)
                    split_w(i, c + AHEAD)
                    dve.wait_ge(S("sil"), lin(i, 3, FT * inst + j + 1))
                    dve.tensor_tensor(HB2[:, bass.ds(lin(i, 3, j), 1), 0:nt], SIL[:, j % RING:j % RING + 1, 0:nt],
                                      ring2(j, nt)[:, 1:2, :], ALU.mult).then_inc(S("h"), 1)
                steps(dve, f"gu{layer}", hidden2, tail=1)
                down(f"dn{layer}", inst, HB2, SHI2, SLO2, nt)
                dve.wait_ge(S("pe_done"), FIRST[f"dn{layer}"] + FT // 2)
                for m in range(KT):
                    gated_update(acc(m, nt), m, 40, "xd")

            dve.wait_ge(S("xd"), 3 * KT)
            norm_row(12, 2)
            for k in range(KT):
                dve.scalar_tensor_tensor(out=YF[:, k, :], in0=X[:, k, 0:TX], scalar=par("norm_final_2", k), in1=RT[:, 0:TX],
                                         op0=ALU.mult, op1=ALU.mult).then_inc(S("yf"), 1)
            for t in range(2):
                dve.wait_ge(S("out_tr"), 2 * t + 1)
                dve.tensor_copy(OUTS[:, t, 0:512], PS[:, 2 * t, :]).then_inc(S("out_ev0"), 1)

        @block.tensor
        def _(pe):
            def product(out, whi, wlo, xhi, xlo, first, last, shared=False):
                pe.matmul(out, whi, xhi, start=first, stop=False, skip_group_check=shared)
                pe.matmul(out, whi, xlo, start=False, stop=False, skip_group_check=shared)
                return pe.matmul(out, wlo, xhi, start=False, stop=last, skip_group_check=shared)

            def weights(c, t, k, width):
                a = k * width + t * P
                return WHI[:, c % RING, a:a + P], WLO[:, c % RING, a:a + P]

            def chunk_ready(i, c):
                pe.wait_ge(S("lo_done"), lin(i, 3, c + 1))

            def by_columns(i, c, outs, hi, lo, n, k_tiles=KT, width=2 * P, ready=None, turn=None):
                chunk_ready(i, c)
                for t, out in enumerate(outs):
                    if turn and t:
                        mod_row_ready(*turn)
                    for k in range(k_tiles):
                        if turn and t and k == 1:
                            mod_turn()
                        if ready and t == 0:
                            ready(k)
                        last = product(out, *weights(c, t, k, width), hi[:, k, 0:n], lo[:, k, 0:n], k == 0, k == k_tiles - 1)
                last.then_inc(S("pe_done"), 1)

            def by_halves(c, outs, hi, lo, x_lo, ctx_lo):
                chunk_ready(None, c)
                for half, (sem, before) in enumerate((x_lo, ctx_lo)):
                    g = slice(TX * half, TX * half + TX)
                    for t, out in enumerate(outs):
                        for k in range(KT):
                            if t == 0:
                                pe.wait_ge(S(sem), before + k + 1)
                            last = product(out[:, g], *weights(c, t, k, 2 * P), hi[:, k, g], lo[:, k, g],
                                           half == 0 and k == 0, k == KT - 1, shared=True)
                last.then_inc(S("pe_done"), 1)

            def down(stage, inst, shi, slo, n):
                def body(i, j, c):
                    chunk_ready(i, c)
                    pe.wait_ge(S("hs_lo"), lin(i, 3, FT // 2 * inst + j + 1))
                    end = i is None and j == FT // 2 - 1
                    for m in range(KT):
                        if m == KT // 2 and inst < 2 and i is None and j <= MODC - FT:
                            mod_row_ready(inst, None, FT + j - 1)
                            mod_turn()
                        for kk in range(2):
                            start = i is None and j == 0 and kk == 0 and (n == TB or m % 2 == 0)
                            last = product(acc(m, n), *weights(c, m, kk, D), shi[:, j % RING, kk, 0:n],
                                           slo[:, j % RING, kk, 0:n], start, end and kk == 1, shared=True)
                    last.then_inc(S("pe_done"), 1)
                    if stage in ("ffn1_dn", "ffn2_dn") and i is None and j < MODC - FT:
                        modulation(inst, None, FT + j)
                steps(pe, stage, body, tail=2)

            def mod_row_ready(layer, i, g):
                pe.wait_ge(S("mod_row"), lin(i, 3, MODC * layer + g + 1))

            def mod_turn():
                for t in range(2):
                    last = pe.transpose(PS[:, 7, 4 * t:4 * t + 4], MROW[:, t * P:t * P + P], IDENT[0:4, 0:4])
                last.then_inc(S("mod_tr"), 1)

            def modulation(layer, i, g):
                if g:
                    pe.wait_ge(S("mod_col"), lin(i, 3, MODC * layer + g))
                for hh in range(2):
                    t = 2 * (MODC * layer + g) + hh
                    pe.wait_ge(S("mod_lo"), lin(i, 6, t + 1))
                    for kk in range(4):
                        k = 4 * hh + kk
                        for w in (MHI, MLO):
                            last = pe.matmul(PS[0:4, 7, TX:TB], SCR[:, k, :], w[:, t % RING, kk * 2 * P:kk * 2 * P + 2 * P],
                                             start=k == 0 and w is MHI, stop=k == KT - 1 and w is MLO)
                    last.then_inc(S("mod_used"), 1)

            def norm_sums(n_norm, t, src):
                for k in range(KT):
                    pe.wait_ge(S("n_sq"), KT * n_norm + k + 1)
                    last = pe.matmul(stat_row(n_norm, t), ONES[:, :], src[:, k, 0:P * t], start=k == 0, stop=k == KT - 1)
                last.then_inc(S("n_ss"), 1)

            def norm_sum_added(count, n_norm):
                pe.wait_ge(S("n_pre"), 3 * count + 3)
                pe.matmul(stat_row(n_norm, 2), ONES[:, :], SQ1[:, 0, :], start=True, stop=True).then_inc(S("n_ss"), 1)

            def wait_k(sem, before):
                return lambda k: pe.wait_ge(S(sem), before + k + 1)

            pe.wait_ge(S("in_ident"), 16)
            pe.wait_ge(S("in_x"), 16)
            for b in range(4):
                for k in (2 * b, 2 * b + 1):
                    for t in range(2):
                        last = pe.transpose(PS[:, b, k % 2 * TX + t * P:k % 2 * TX + t * P + P], XS[:, t, k * P:k * P + P], IDENT[:, :])
                last.then_inc(S("tr_x"), 1)
            for n, g in enumerate((0, 2)):
                rows = PAR_USED[g]
                pe.wait_ge(S(f"in_par{g}"), 16 * sum(at[0] == g for at in PAR_AT.values()))
                pe.transpose(PS[:, 4 + n, 0:rows], GS[0:rows, g, :], IDENT[0:rows, 0:rows]).then_inc(S("tr_par"), 1)
            pe.wait_ge(S("const"), 3)

            def later_parameters():
                for n, g in enumerate((1, 3)):
                    rows = PAR_USED[g]
                    pe.wait_ge(S(f"in_par{g}"), 16 * sum(at[0] == g for at in PAR_AT.values()))
                    last = pe.transpose(PS[:, 1, n * P:n * P + rows], GS[0:rows, g, :], IDENT[0:rows, 0:rows])
                last.then_inc(S("tr_par"), 1)
                pe.wait_ge(S("in_p"), 16)
                for k in range(2):
                    for t in range(2):
                        last = pe.transpose(PS[:, 2, k * TX + t * P:k * TX + t * P + P], PST[:, t, k * P:k * P + P], IDENT[:, :])
                last.then_inc(S("tr_p"), 1)
                pe.wait_ge(S("in_bias"), 48)
                pe.matmul(PS[0:16, 3, 0:384], REL[:, :], ONEHOT[:, :], start=True, stop=True).then_inc(S("mm_ext"), 1)

            def context():
                pe.wait_ge(S("in_ctx"), 16)
                pe.wait_ge(S("n_std"), 1)
                pe.wait_ge(S("par_ev"), 4)
                pe.wait_ge(S("p_ev"), 1)
                pe.wait_ge(S("ext_ev"), 1)
                for b in range(4):
                    for k in (2 * b, 2 * b + 1):
                        for t in range(2):
                            last = pe.transpose(PS[:, b, k % 2 * TX + t * P:k % 2 * TX + t * P + P], CS[:, t, k * P:k * P + P],
                                                IDENT[:, :])
                    last.then_inc(S("tr_c"), 1)

            for inst, (pre, post) in enumerate(((0, 1), (4, 5))):
                f = f"ffn{inst + 1}"

                def gate_up(i, j, c):
                    first = i is None and j == 0
                    if first and inst == 0:
                        pe.wait_ge(S("par_ev"), 2)
                        pe.wait_ge(S("x_ev"), 4)
                    if j >= RING:
                        pe.wait_ge(S("gu"), lin(i, 3, FT * inst + j - RING + 1))
                    out = ring1(j)
                    by_columns(i, c, [out[:, 0, :], out[:, 1, :]], AHI1, ALO1, TX,
                               ready=wait_k("act_lo", 3 * KT * inst) if first else None,
                               turn=(inst, i, j - 1) if j else None)
                    if i is None and j == 0 and inst == 0:
                        pe.wait_ge(S("sc_lo"), 1)
                    modulation(inst, i, j)
                    if i is None and j == 0:
                        norm_sum_added(2 * inst, pre)
                    if inst == 0 and i is None:
                        if j == 0:
                            later_parameters()
                        elif j == 1:
                            context()
                steps(pe, f + "_gu", gate_up)
                if inst == 0:
                    pe.wait_ge(S("c_ev"), 4)
                down(f + "_dn", inst, SHI1, SLO1, TX)
                norm_sums(post, 2, SQ1)
                if inst == 1:
                    break

                def project(i, j, c):
                    if j >= RING:
                        pe.wait_ge(S("zt"), lin(i, 6, 2 * (j - RING) + 1))
                    out = ring1(j)
                    by_columns(i, c, [out[:, 0, :], out[:, 1, :]], AHI1, ALO1, TX,
                               ready=wait_k("act_lo", KT) if i is None and j == 0 else None)
                    if i is None and j == 0:
                        norm_sum_added(1, 2)
                steps(pe, "b1_in", project)

                def scores(g):
                    if g:
                        pe.wait_ge(S("a_sb"), 3 * g)
                    else:
                        pe.wait_ge(S("zt"), 18)
                    for hl in (0, 2, 1, 3):
                        h = 4 * g + hl
                        p0 = 64 * (h % 2)
                        if hl == 1:
                            pe.wait_ge(S("a_even"), g + 1)
                        if h < 8:
                            q = Z[p0:p0 + 64, h // 2, :]
                            k = Z[p0:p0 + 64, 4, :] if h // 4 == h % 2 else KS[p0:p0 + 64, :]
                        else:
                            q, k = Z[p0:p0 + 64, 6 + (h - 8) // 2, :], Z[p0:p0 + 64, 10 + (h - 8) // 2, :]
                        pe.matmul(PS[:, hl % 2, hl // 2 * TX:hl // 2 * TX + TX], q[:, P:TX], k[:, :], start=True, stop=True)
                        last = pe.matmul(PS[:, 2, hl * P:hl * P + P], q[:, 0:P], k[:, 0:P], start=True, stop=True)
                        if hl == 2:
                            last.then_inc(S("a_even"), 1)
                    last.then_inc(S("a_s"), 1)

                def keys_first(g):
                    s = g % 2
                    pe.wait_ge(S("a_p"), g + 1)
                    pe.wait_ge(S("a_p0"), g + 1)
                    if g:
                        pe.wait_ge(S("a_pt"), g)
                    else:
                        pe.wait_ge(S("vt_ev"), 3)
                    for hl in range(4):
                        for src, col in ((SB0[s][:, hl, :], 0), (SB1[s][:, hl, 0:P], P), (SB1[s][:, hl, P:TX], 2 * P)):
                            last = pe.transpose(PS[:, 3 + hl, col:col + P], src, IDENT[:, :])
                    last.then_inc(S("a_tr"), 1)

                def mixed(g):
                    s = g % 2
                    pe.wait_ge(S("a_pt"), g + 1)
                    if g:
                        pe.wait_ge(S("act_lo"), 2 * KT + 2 * g)
                    for hl in range(4):
                        h = 4 * g + hl
                        p0 = 64 * (h % 2)
                        v, c0 = (0, 64 * g) if h < 8 else (2 + 2 * ((h - 8) // 2), p0)
                        out = PS[p0:p0 + 64, 7, hl // 2 * TX:hl // 2 * TX + TX]
                        pe.matmul(out, VT1[:, v, c0:c0 + 64], PT1[s][:, hl, 0:TX], start=True, stop=False)
                        last = pe.matmul(out[:, P:TX], VT1[:, v + 1, c0:c0 + 64], PT1[s][:, hl, TX:3 * P], start=False, stop=True)
                    last.then_inc(S("a_pv"), 1)

                pe.wait_ge(S("ks"), 32)
                scores(0)
                for b in range(3):
                    for a in range(4 * b, min(4 * b + 4, 10)):
                        tile = 5 if a < 2 else 13 + a // 2
                        last = pe.transpose(PS[:, 3 + b, a % 4 * P:a % 4 * P + P], Z[:, tile, a % 2 * P:a % 2 * P + P], IDENT[:, :])
                    last.then_inc(S("vt_tr"), 1)
                for g in range(4):
                    if g < 3:
                        scores(g + 1)
                    if g:
                        mixed(g - 1)
                    keys_first(g)
                mixed(3)

                for j in range(4):
                    if j >= RING:
                        pe.wait_ge(S("f_ev"), j - RING + 1)
                    out = ring1(j)
                    by_columns(None, FIRST["b1_out"] + j, [out[:, 0, :], out[:, 1, :]], AHI1, ALO1, TX,
                               ready=wait_k("act_lo", 2 * KT) if j == 0 else None)
                norm_sums(3, 2, SQ1)

            pe.wait_ge(S("p_lo"), 1)
            pe.wait_ge(S("gu"), 2 * FT)
            pe.wait_ge(S("mod_col"), 2 * MODC)
            c = FIRST["ple_proj"]
            chunk_ready(None, c)
            for m in range(KT):
                if m == 6:
                    pe.wait_ge(S("n_std"), 6)
                for k in range(2):
                    last = product(projected(m // 2)[:, m % 2, :], *weights(c, m, k, D), PHI[:, k, :], PLO[:, k, :], k == 0, k == 1)
            last.then_inc(S("pe_done"), 1)
            for j in range(4):
                if j < RING:
                    pe.wait_ge(S("xt"), 2 * KT + 2 * j + 2)
                else:
                    pe.wait_ge(S("pg"), j - RING + 1)
                out = ringp(j)
                by_columns(None, FIRST["ple_gate"] + j, [out[:, 0, :], out[:, 1, :]], AHI1, ALO1, TX,
                           ready=wait_k("act_lo", 4 * KT) if j == 0 else None)
                if j == 0:
                    norm_sum_added(3, 6)
            norm_sums(7, 2, SQ1)

            for layer in range(2):
                nt = TB if layer == 0 else TX
                def network(l):
                    if l == 0:
                        pe.wait_ge(S(f"tables{layer}"), 160)
                    else:
                        pe.wait_ge(S("f_h"), 3 * layer + l)
                    pe.matmul(PS[0:FH, 7, 0:TX], FW[l][:, :], ZF[:, :] if l == 0 else HA[:, l - 1, :], start=True, stop=True)\
                      .then_inc(S("f_mm"), 1)

                def taps(t):
                    if t == 0:
                        pe.wait_ge(S("f_h"), 3 * layer + 3)
                        pe.wait_ge(S("n_std"), 9 + 2 * layer)
                    else:
                        pe.wait_ge(S("f_dec"), 4 * layer + 2)
                    for r in range(2):
                        last = pe.matmul(PS[:, 6 + r, :], HA[:, 2, t * P:t * P + P], FW4[:, r * HW:r * HW + HW],
                                         start=True, stop=True)
                    last.then_inc(S("f_taps"), 1)

                def spectrum(half):
                    if half == 0:
                        pe.wait_ge(S("f_dec"), 4 * layer + 4)
                    else:
                        pe.wait_ge(S("f_kc"), 5 * layer + 3)
                    for ct in (2 * half, 2 * half + 1):
                        for r in range(2):
                            for t in range(2):
                                last = pe.matmul(PS[:, 6 + ct % 2, :], DFT[:, r, t, ct * P:ct * P + P], HF[:, t, r, :],
                                                 start=r + t == 0, stop=r + t == 2)
                    last.then_inc(S("f_k"), 1)

                norm_sums(8 + 2 * layer, 4, SQ2)
                beside = [lambda: network(0), lambda: network(1), lambda: network(2), lambda: taps(0), lambda: taps(1),
                          lambda: spectrum(0)]
                for q in range(6):
                    n = TB if layer == 0 or q >= 4 else TX
                    if q >= RING:
                        pe.wait_ge(S("qkv_ev"), 6 * layer + q - RING + 1)
                    out = ring2(q, n)
                    outs = [out[:, 0, :], out[:, 1, :]]
                    if q == 0 and layer == 0:
                        by_halves(FIRST[f"qkv{layer}"], outs, AHI2, ALO2, ("act_lo", 5 * KT), ("ctx_lo", 0))
                    else:
                        if q == 4 and layer == 1:
                            pe.wait_ge(S("ctx_lo"), 3 * KT)
                        by_columns(None, FIRST[f"qkv{layer}"] + q, outs, AHI2, ALO2, n,
                                   ready=wait_k("act_lo", KT * (5 + 2 * layer)) if q == 0 else None)
                    beside[q]()

                tq = nt // P

                def key_sums():
                    pe.wait_ge(S("h_sq"), 5 * layer + 1)
                    pe.wait_ge(S("f_fix"), 2 * layer + 2)
                    for kv in range(2):
                        last = pe.matmul(PS[:, 6 + kv, :], ONES[:, :], HSQ[:, kv, :], start=True, stop=True)
                    last.then_inc(S("h_ss"), 1)

                def query_sums(pair):
                    pe.wait_ge(S("h_sq"), 5 * layer + pair + 2)
                    for h in (2 * pair, 2 * pair + 1):
                        for t in range(tq):
                            last = pe.matmul(PS[:, 6, h * tq + t:h * tq + t + 1], HSQ[:, h % 2, t * P:t * P + P], ONES[:, 0:1],
                                             start=True, stop=True)
                    last.then_inc(S("h_ss"), 1)

                def rotate(r, tile):
                    if r == 0:
                        pe.wait_ge(S("h_kn"), 2 * layer + 2)
                    else:
                        pe.wait_ge(S("h_gain"), 4 * layer + r)
                        pe.wait_ge(S("h_sin"), 5 * layer + r)
                    for j in range(2):
                        last = pe.matmul(PS[:, 7, j * TX:j * TX + TX], ROT[:, :], QKV[:, tile + j, 0:TX], start=True, stop=True)
                    last.then_inc(S("h_rot"), 1)

                for q in range(6):
                    if q < RING:
                        pe.wait_ge(S("qkv_ev"), 6 * layer + q + RING + 1)
                    else:
                        pe.wait_ge(S("hy_taps"), 24 * layer + 4 * (q - RING + 1))
                    out = ring2(q, nt)
                    by_columns(None, FIRST[f"hy{layer}"] + q, [out[:, 0, :], out[:, 1, :]], AHI2, ALO2, nt)
                    if q == 0:
                        spectrum(1)
                    elif q == 1:
                        key_sums()
                    elif q >= 3:
                        rotate(q - 3, (8, 0, 2)[q - 3])
                        query_sums(q - 3)
                rotate(3, 4)
                query_sums(3)
                rotate(4, 6)

                groups = nt // TX

                def turned(grp):
                    pe.wait_ge(S("hy_v"), HT * (layer + 1))
                    pe.wait_ge(S("hy_taps"), 24 * (layer + 1))
                    if grp:
                        pe.wait_ge(S("y_vt"), 2 * layer + grp)
                    for t in range(2):
                        for m in range(HT):
                            last = pe.transpose(PS[:, t, m * P:m * P + P], HY[:, 8 + m, TX * grp + t * P:TX * grp + t * P + P],
                                                IDENT[:, :])
                    last.then_inc(S("y_tr"), 1)

                def forward(y):
                    h = y % 2
                    y += 4 * layer
                    pe.wait_ge(S("y_vt"), y // 2 + 1)
                    if y >= 2:
                        pe.wait_ge(S("y_mul"), 7 * (y - 1))
                    for ct in range(CTILES):
                        for t in range(2):
                            last = pe.matmul(PS[:, 2 + 2 * h + ct // 2, ct % 2 * TX:ct % 2 * TX + TX], DFT[:, 0, t, ct * P:ct * P + P],
                                             VTT[:, t, TX * h:TX * h + TX], start=t == 0, stop=t == 1)
                    last.then_inc(S("y_fwd"), 1)

                def inverse(y):
                    h = y % 2
                    y += 4 * layer
                    pe.wait_ge(S("y_mul"), 7 * y + 7)
                    if y >= 2:
                        pe.wait_ge(S("y_h"), 4 * (y - 1))
                    for m in range(2):
                        for ct in range(CTILES):
                            last = pe.matmul(PS[:, 6 + h, m * TX:m * TX + TX], YS[:, h, ct, m * P:m * P + P], IDFT[:, ct, :],
                                             start=ct == 0, stop=ct == CTILES - 1)
                    last.then_inc(S("y_inv"), 1)

                turned(0)
                forward(0)
                forward(1)
                if groups == 2:
                    turned(1)
                    inverse(0)
                    forward(2)
                    inverse(1)
                    forward(3)
                last_y = 2 * groups - 1

                units = [(0, h) for h in range(NH2)] + ([(1, h) for h in range(NH2)] if layer == 0 else [])
                u0 = 2 * NH2 * layer

                def scores2(u):
                    grp, h = units[u]
                    if u >= 2:
                        pe.wait_ge(S("b_ex"), 2 * (u0 + u - 1))
                    for t in range(2):
                        q = QKV[:, h, TX * grp + t * P:TX * grp + t * P + P]
                        if grp == 0:
                            last = pe.matmul(PS[:, 2 * (u % 2) + t, :], q, QKV[:, 8 + h // 4, :], start=True, stop=True)
                        else:
                            last = pe.matmul(PS[:, 2 * (u % 2), TX * t:TX * t + TX], q, QKV[:, 8 + h // 4, TX:TB], start=True, stop=True)
                    last.then_inc(S("b_s"), 1)

                def values(u):
                    grp, h = units[u]
                    pe.wait_ge(S("b_pt"), u0 + u + 1)
                    if u >= 2:
                        pe.wait_ge(S("b_o"), u0 + u - 1)
                    kts = range(4) if grp == 0 else range(2, 4)
                    for a, kt in enumerate(kts):
                        last = pe.matmul(PS[:, 6 + u % 2, 0:TX], VT2[:, 2 * kt + h // 4, :], PT2[:, u % 2, a, :],
                                         start=a == 0, stop=a == len(kts) - 1)
                    last.then_inc(S("b_pv"), 1)

                pe.wait_ge(S("h_sum"), 5 * (layer + 1))
                scores2(0)
                inverse(last_y - 1)
                inverse(last_y)
                for a in range(8):
                    last = pe.transpose(PS[:, 4 + a // 4, a % 4 * P:a % 4 * P + P], QKV[:, 10 + a % 2, a // 2 * P:a // 2 * P + P],
                                        IDENT[:, :])
                last.then_inc(S("v_tr"), 1)
                for u, (grp, h) in enumerate(units):
                    if u + 1 < len(units):
                        scores2(u + 1)
                    if u:
                        values(u - 1)
                    if u == 0:
                        pe.wait_ge(S("v_ev"), layer + 1)
                    pe.wait_ge(S("b_p"), 2 * (u0 + u) + 2)
                    for a in range(4 if grp == 0 else 2):
                        for t in range(2):
                            last = pe.transpose(PS[:, 4 + a // 2, a % 2 * TX + t * P:a % 2 * TX + t * P + P],
                                                PB[:, u % 2, t, a * P:a * P + P], IDENT[:, :])
                    last.then_inc(S("b_tr"), 1)
                values(len(units) - 1)

                for j in range(2):
                    if j == 0:
                        pe.wait_ge(S("b_o"), u0 + len(units))
                    outs = [PS[:, 4 * j + t, 0:nt] for t in range(4)]
                    by_columns(None, FIRST[f"oh{layer}"] + j, outs, HHI, HLO, nt, k_tiles=HT, width=4 * P,
                               ready=wait_k("hh_lo", HT * layer) if j == 0 else None)

                def mix(i, m):
                    c = FIRST[f"mix{layer}"] + 3 * m
                    for g, (hi, lo) in enumerate(((AHI2, ALO2), (AHI2, ALO2), (A2HI, A2LO))):
                        if m == 0:
                            if g == 0:
                                pe.wait_ge(S("oh_ev"), 2 * (layer + 1))
                            if g == 2:
                                pe.wait_ge(S("a2_lo"), KT * (layer + 1))
                        elif g < 2:
                            pe.wait_ge(S("gate"), lin(i, 2, 8 * layer + 2 * (m - 1) + g + 1))
                        else:
                            pe.wait_ge(S("merge"), lin(i, 3, 12 * layer + 3 * (m - 1) + 2))
                        out = ring2(g, nt)
                        by_columns(i, c + g, [out[:, 0, :], out[:, 1, :]], hi, lo, nt)
                mix(None, 0)
                with pe.Fori(0, 3) as i:
                    mix(i, 1)
                pe.wait_ge(S("merge"), 12 * (layer + 1))
                for j in range(4):
                    if j >= RING:
                        pe.wait_ge(S("xo"), 2 * KT * layer + 2 * (nt // TX))
                    out = ring2(j, nt)
                    by_columns(None, FIRST[f"out{layer}"] + j, [out[:, 0, :], out[:, 1, :]], AHI2, ALO2, nt,
                               ready=wait_k("mg_lo", KT * layer) if j == 0 else None)
                norm_sums(9 + 2 * layer, nt // P, SQ2)
                inst = 2 + layer

                def gate_up2(i, j, c):
                    if j >= RING:
                        pe.wait_ge(S("h"), lin(i, 3, FT * inst + j - RING + 1))
                    out = ring2(j, nt)
                    outs = [out[:, 0, :], out[:, 1, :]]
                    if i is None and j == 0 and layer == 0:
                        by_halves(c, outs, AHI2, ALO2, ("act_lo", 6 * KT), ("ctx_lo", KT))
                    else:
                        by_columns(i, c, outs, AHI2, ALO2, nt,
                                   ready=wait_k("act_lo", KT * (6 + 2 * layer)) if i is None and j == 0 else None)
                steps(pe, f"gu{layer}", gate_up2)
                pe.wait_ge(S("h"), FT * (inst + 1))
                down(f"dn{layer}", inst, SHI2, SLO2, nt)

            pe.wait_ge(S("xd"), 3 * KT)
            norm_sums(12, 2, SQ1)
            for t in range(2):
                for a in range(2):
                    for k in range(4 * a, 4 * a + 4):
                        pe.wait_ge(S("yf"), k + 1)
                        last = pe.transpose(PS[:, 2 * t + a, k % 4 * P:k % 4 * P + P], YF[:, k, t * P:t * P + P], IDENT[:, :])
                    last.then_inc(S("out_tr"), 1)


_NAMES = ["x", "p", "rel_bias", "ffn1_pre_g", "ffn1_w_gu", "ffn1_w_down", "ffn1_post_g", "attn_pre_g", "w_in", "b_in",
          "sinks", "w_out", "b_out", "attn_post_g", "ffn2_pre_g", "ffn2_w_gu", "ffn2_w_down", "ffn2_post_g",
          "ple_pre_g", "w_ple_gate", "w_ple_proj", "ple_post_g", "c_2", "ctx_2", "c_ctx_2", "w_mod_2", "b_mod_2",
          "norm_mix_2", "w_in_2", "q_norm_2", "k_norm_2", "conv_w_2", "conv_b_2", "filt_w1_2", "filt_b1_2",
          "filt_w2_2", "filt_b2_2", "filt_w3_2", "filt_b3_2", "filt_w4_2", "filt_freq_2", "hyena_bias_2",
          "w_o_attn_2", "w_o_hyena_2", "w_out_2", "norm_ffn_2", "w_gate_up_2", "w_down_2", "norm_final_2"]


def kernel(**inputs):
    import concourse.bacc as bacc
    from concourse.bass_utils import run_bass_kernel_spmd

    nc = bacc.Bacc("TRN2", target_bir_lowering=False, num_devices=1)
    tensors = {n: np.ascontiguousarray(inputs[n]) for n in _NAMES}
    tensors.update(shape_tables())
    arrays, aps = {}, {}
    for name, a in tensors.items():
        arrays[f"in_{name}_dram"] = a
        aps[name] = nc.dram_tensor(f"in_{name}_dram", a.shape, mybir.dt.from_np(a.dtype), kind="ExternalInput").ap()
    aps["out"] = nc.dram_tensor("out_0_dram", (1, TX, D), F32, kind="ExternalOutput").ap()
    two_blocks_kernel(nc, aps)
    r = run_bass_kernel_spmd(nc, [arrays], core_ids=[0])
    return r.results[0]["out_0_dram"]
```
